# Optimizing a Trainium2 kernel written in Bass

```python
import math
import jax, jax.numpy as jnp
from jax import lax
import numpy as np

D_MODEL = 1024
BATCH = 1
SEQ = 512
DEPTH = 1

HEAD_DIM = 64
DIFF_HEADS = 4
DIFF_V_DIM = 2 * HEAD_DIM
DSA_HEADS = 4
DSA_LATENT = 128
DSA_V_DIM = 64
IDX_HEADS = 8
IDX_DIM = 32
DSA_TOPK_MAX = 256
MOBA_HEADS = 4
MOBA_BLOCK = 256
MOBA_TOPK_MAX = 3
N_BUCKETS = 32
MAX_DISTANCE = 128
N_BIAS_HEADS = DIFF_HEADS + DSA_HEADS + MOBA_HEADS
D_FF = 4 * D_MODEL
Q_BLOCK = 128
MOBA_Q_CHUNK = 32
EPS = 1e-6

A_Q = DIFF_HEADS * 2 * HEAD_DIM
A_K = DIFF_HEADS * 2 * HEAD_DIM
A_V = DIFF_HEADS * DIFF_V_DIM
B_Q = DSA_HEADS * DSA_LATENT
B_KV = DSA_LATENT
B_IQ = IDX_HEADS * IDX_DIM
B_IK = IDX_DIM
B_IW = IDX_HEADS
C_QKV = MOBA_HEADS * HEAD_DIM
G_COLS = 3 * D_MODEL
SPLIT_SIZES = (A_Q, A_K, A_V, B_Q, B_KV, B_IQ, B_IK, B_IW, C_QKV, C_QKV, C_QKV, G_COLS)
IN_COLS = A_Q + A_K + A_V + B_Q + B_KV + B_IQ + B_IK + B_IW + 3 * C_QKV + G_COLS


def rmsnorm(x, g):
    xf = x.astype(jnp.float32)
    y = xf * lax.rsqrt(jnp.mean(xf * xf, axis=-1, keepdims=True) + EPS)
    return y.astype(x.dtype) * g

def split_cols(p):
    out = []
    off = 0
    for n in SPLIT_SIZES:
        out.append(p[..., off:off + n])
        off += n
    return out

def t5_bucket(dist):
    max_exact = N_BUCKETS // 2
    n = jnp.maximum(dist, 0)
    nf = jnp.maximum(n, 1).astype(jnp.float32)
    large = max_exact + (jnp.log(nf / max_exact) / math.log(MAX_DISTANCE / max_exact)
                         * (N_BUCKETS - max_exact)).astype(jnp.int32)
    large = jnp.minimum(large, N_BUCKETS - 1)
    return jnp.where(n < max_exact, n, large)

def diff_attention(q, k, v, lam, lam_init, subln_g, bias_a):
    B, S, H = q.shape[0], q.shape[1], q.shape[2]
    E = v.shape[-1]
    kpos = jnp.arange(S)
    scale = HEAD_DIM ** -0.5
    bias_t = bias_a.T

    def block(i):
        q0 = i * Q_BLOCK
        qb = lax.dynamic_slice_in_dim(q, q0, Q_BLOCK, axis=1)
        qpos = q0 + jnp.arange(Q_BLOCK)
        dist = qpos[:, None] - kpos[None, :]
        bias = bias_t[:, t5_bucket(dist)]
        logits = jnp.einsum('bqhmd,bkhmd->bhmqk', qb, k).astype(jnp.float32) * scale + bias[None, :, None]
        logits = jnp.where(dist >= 0, logits, -jnp.inf)
        p = jax.nn.softmax(logits, axis=-1)
        attn = p[:, :, 0] - lam * p[:, :, 1]
        return jnp.einsum('bhqk,bkhe->bqhe', attn.astype(v.dtype), v)

    o = lax.map(block, jnp.arange(S // Q_BLOCK))
    o = jnp.moveaxis(o, 0, 1).reshape(B, S, H, E)
    o = rmsnorm(o, subln_g) * (1.0 - lam_init)
    return o.reshape(B, S, H * E)

def dsa_attention(q_lat, kv_lat, iq, ik, iw, w_uv, bias_b):
    B, S, H, R = q_lat.shape
    topk = min(DSA_TOPK_MAX, S // 4)
    kpos = jnp.arange(S)
    bidx = jnp.arange(B)[:, None, None]
    hidx = jnp.arange(H)[None, None, :, None]
    bias_t = bias_b.T
    idx_scale = (IDX_HEADS ** -0.5) * (IDX_DIM ** -0.5)

    def block(i):
        q0 = i * Q_BLOCK
        qpos = q0 + jnp.arange(Q_BLOCK)
        qb = lax.dynamic_slice_in_dim(q_lat, q0, Q_BLOCK, axis=1)
        iqb = lax.dynamic_slice_in_dim(iq, q0, Q_BLOCK, axis=1)
        iwb = lax.dynamic_slice_in_dim(iw, q0, Q_BLOCK, axis=1)
        causal = qpos[:, None] >= kpos[None, :]
        s_idx = jax.nn.relu(jnp.einsum('bqhd,bkd->bqhk', iqb, ik))
        score = jnp.einsum('bqhk,bqh->bqk', s_idx, iwb).astype(jnp.float32) * idx_scale
        score = jnp.where(causal[None], score, -jnp.inf)
        _, sel = lax.top_k(score, topk)
        dist = qpos[None, :, None] - sel
        valid = dist >= 0
        kv_sel = kv_lat[bidx, sel]
        logits = jnp.einsum('bqhr,bqkr->bqhk', qb, kv_sel).astype(jnp.float32) * (R ** -0.5)
        bias = bias_t[hidx, t5_bucket(dist)[:, :, None, :]]
        logits = jnp.where(valid[:, :, None, :], logits + bias, -jnp.inf)
        p = jax.nn.softmax(logits, axis=-1)
        return jnp.einsum('bqhk,bqkr->bqhr', p.astype(kv_sel.dtype), kv_sel)

    o = lax.map(block, jnp.arange(S // Q_BLOCK))
    o = jnp.moveaxis(o, 0, 1).reshape(B, S, H, R)
    o = jnp.einsum('bshr,hre->bshe', o, w_uv)
    return o.reshape(B, S, H * DSA_V_DIM)

def moba_attention(q, k, v, bias_c):
    B, S, H, Dh = q.shape
    nb = -(-S // MOBA_BLOCK)
    sp = nb * MOBA_BLOCK
    pad = ((0, 0), (0, sp - S), (0, 0), (0, 0))
    k_bh = jnp.pad(k, pad).reshape(B, nb, MOBA_BLOCK, H, Dh).transpose(0, 3, 1, 2, 4)
    v_bh = jnp.pad(v, pad).reshape(B, nb, MOBA_BLOCK, H, Dh).transpose(0, 3, 1, 2, 4)
    k_mean = jnp.mean(k_bh, axis=3)
    topb = min(MOBA_TOPK_MAX, nb)
    bias_t = bias_c.T
    bi = jnp.arange(B)[:, None, None, None]
    hi = jnp.arange(H)[None, :, None, None]
    hi5 = jnp.arange(H)[None, :, None, None, None]
    blk_ids = jnp.arange(nb)
    in_blk = jnp.arange(MOBA_BLOCK)
    scale = Dh ** -0.5

    def chunk(i):
        q0 = i * MOBA_Q_CHUNK
        qpos = q0 + jnp.arange(MOBA_Q_CHUNK)
        j = q0 // MOBA_BLOCK
        qc = lax.dynamic_slice_in_dim(q, q0, MOBA_Q_CHUNK, axis=1).transpose(0, 2, 1, 3)
        gate = jnp.einsum('bhqd,bhnd->bhqn', qc, k_mean).astype(jnp.float32)
        gate = jnp.where(blk_ids < j, gate, -jnp.inf)
        _, sel = lax.top_k(gate, topb)
        sel_valid = sel < j
        k_sel = k_bh[bi, hi, sel]
        v_sel = v_bh[bi, hi, sel]
        lp = jnp.einsum('bhqd,bhqnkd->bhqnk', qc, k_sel).astype(jnp.float32) * scale
        dist_p = qpos[None, None, :, None, None] - (sel[..., None] * MOBA_BLOCK + in_blk)
        lp = lp + bias_t[hi5, t5_bucket(dist_p)]
        lp = jnp.where(sel_valid[..., None], lp, -jnp.inf).reshape(B, H, MOBA_Q_CHUNK, topb * MOBA_BLOCK)
        k_own = lax.dynamic_slice_in_dim(k_bh, j, 1, axis=2)[:, :, 0]
        v_own = lax.dynamic_slice_in_dim(v_bh, j, 1, axis=2)[:, :, 0]
        lo = jnp.einsum('bhqd,bhkd->bhqk', qc, k_own).astype(jnp.float32) * scale
        dist_o = qpos[:, None] - (j * MOBA_BLOCK + in_blk)[None, :]
        lo = jnp.where(dist_o >= 0, lo + bias_t[:, t5_bucket(dist_o)][None], -jnp.inf)
        p = jax.nn.softmax(jnp.concatenate([lp, lo], axis=-1), axis=-1)
        pp = p[..., :topb * MOBA_BLOCK].reshape(B, H, MOBA_Q_CHUNK, topb, MOBA_BLOCK)
        po = p[..., topb * MOBA_BLOCK:]
        o = (jnp.einsum('bhqnk,bhqnkd->bhqd', pp.astype(v.dtype), v_sel)
             + jnp.einsum('bhqk,bhkd->bhqd', po.astype(v.dtype), v_own))
        return o.transpose(0, 2, 1, 3)

    o = lax.map(chunk, jnp.arange(S // MOBA_Q_CHUNK))
    return jnp.moveaxis(o, 0, 1).reshape(B, S, H * Dh)

def first_inputs(seed: int = 0) -> dict:
    key = jax.random.key(seed)
    ks = jax.random.split(key, 20)

    def nrm(k, shape, s):
        return jax.random.normal(k, shape, jnp.float32) * s

    return {
        'x': nrm(ks[0], (BATCH, SEQ, D_MODEL), 1.0),
        'c': nrm(ks[1], (BATCH, D_MODEL), 1.0),
        'rel_bias': nrm(ks[2], (N_BUCKETS, N_BIAS_HEADS), 0.5),
        'ada_w': nrm(ks[3], (DEPTH, D_MODEL, 6 * D_MODEL), D_MODEL ** -0.5),
        'ada_b': nrm(ks[4], (DEPTH, 6 * D_MODEL), 0.02),
        'norm_mix': 1.0 + nrm(ks[5], (DEPTH, D_MODEL), 0.02),
        'w_in': nrm(ks[6], (DEPTH, D_MODEL, IN_COLS), D_MODEL ** -0.5),
        'gate_b': nrm(ks[7], (DEPTH, G_COLS), 0.02),
        'diff_lambda': nrm(ks[8], (DEPTH, 4, HEAD_DIM), 0.1),
        'diff_subln': 1.0 + nrm(ks[9], (DEPTH, DIFF_V_DIM), 0.02),
        'dsa_kv_norm': 1.0 + nrm(ks[10], (DEPTH, DSA_LATENT), 0.02),
        'dsa_w_uv': nrm(ks[11], (DEPTH, DSA_HEADS, DSA_LATENT, DSA_V_DIM), DSA_LATENT ** -0.5),
        'w_br_a': nrm(ks[12], (DEPTH, A_V, D_MODEL), A_V ** -0.5),
        'w_br_b': nrm(ks[13], (DEPTH, DSA_HEADS * DSA_V_DIM, D_MODEL), (DSA_HEADS * DSA_V_DIM) ** -0.5),
        'w_br_c': nrm(ks[14], (DEPTH, C_QKV, D_MODEL), C_QKV ** -0.5),
        'w_o': nrm(ks[15], (DEPTH, D_MODEL, D_MODEL), D_MODEL ** -0.5),
        'norm_mlp': 1.0 + nrm(ks[16], (DEPTH, D_MODEL), 0.02),
        'w_ff1': nrm(ks[17], (DEPTH, D_MODEL, D_FF), D_MODEL ** -0.5),
        'w_ff2': nrm(ks[18], (DEPTH, D_FF, D_MODEL), D_FF ** -0.5),
        'norm_final': 1.0 + nrm(ks[19], (D_MODEL,), 0.02),
    }

def first_block(x, c, rel_bias, ada_w, ada_b, norm_mix, w_in, gate_b, diff_lambda, diff_subln,
              dsa_kv_norm, dsa_w_uv, w_br_a, w_br_b, w_br_c, w_o, norm_mlp, w_ff1, w_ff2,
              norm_final):
    B, S, _ = x.shape
    bias_tab = rel_bias.astype(jnp.float32)
    bias_a = bias_tab[:, :DIFF_HEADS]
    bias_b = bias_tab[:, DIFF_HEADS:DIFF_HEADS + DSA_HEADS]
    bias_c = bias_tab[:, DIFF_HEADS + DSA_HEADS:]
    cond = jax.nn.silu(c)
    for l in range(DEPTH):
        mod = (cond @ ada_w[l] + ada_b[l]).reshape(B, 6, D_MODEL)[:, :, None, :]
        shift1, scale1, gate1 = mod[:, 0], mod[:, 1], mod[:, 2]
        shift2, scale2, gate2 = mod[:, 3], mod[:, 4], mod[:, 5]

        u = rmsnorm(x, norm_mix[l]) * (1.0 + scale1) + shift1
        aq, ak, av, bq, bkv, biq, bik, biw, cq, ck, cv, g = split_cols(u @ w_in[l])

        lam_init = 0.8 - 0.6 * math.exp(-0.3 * l)
        dl = diff_lambda[l].astype(jnp.float32)
        lam = jnp.exp(jnp.sum(dl[0] * dl[1])) - jnp.exp(jnp.sum(dl[2] * dl[3])) + lam_init
        y_a = diff_attention(aq.reshape(B, S, DIFF_HEADS, 2, HEAD_DIM),
                             ak.reshape(B, S, DIFF_HEADS, 2, HEAD_DIM),
                             av.reshape(B, S, DIFF_HEADS, DIFF_V_DIM),
                             lam, lam_init, diff_subln[l], bias_a) @ w_br_a[l]
        y_b = dsa_attention(bq.reshape(B, S, DSA_HEADS, DSA_LATENT),
                            rmsnorm(bkv, dsa_kv_norm[l]),
                            biq.reshape(B, S, IDX_HEADS, IDX_DIM), bik, biw,
                            dsa_w_uv[l], bias_b) @ w_br_b[l]
        y_c = moba_attention(cq.reshape(B, S, MOBA_HEADS, HEAD_DIM),
                             ck.reshape(B, S, MOBA_HEADS, HEAD_DIM),
                             cv.reshape(B, S, MOBA_HEADS, HEAD_DIM), bias_c) @ w_br_c[l]
        gates = jax.nn.sigmoid(g + gate_b[l]).reshape(B, S, 3, D_MODEL)
        merged = gates[:, :, 0] * y_a + gates[:, :, 1] * y_b + gates[:, :, 2] * y_c
        x = x + gate1 * (merged @ w_o[l])

        u2 = rmsnorm(x, norm_mlp[l]) * (1.0 + scale2) + shift2
        h = jnp.square(jax.nn.relu(u2 @ w_ff1[l]))
        x = x + gate2 * (h @ w_ff2[l])
    return rmsnorm(x, norm_final)


DEPTH_2 = 2

DEEPNORM_ALPHA = (2 * DEPTH_2) ** 0.25
DEEPNORM_BETA = (8 * DEPTH_2) ** -0.25
LN_EPS = 1e-5

CONV_CH = D_MODEL
CONV_WIDTH = 31
SSM_INNER = D_MODEL
SSM_HEAD_DIM = 64
SSM_HEADS = SSM_INNER // SSM_HEAD_DIM
SSM_GROUPS = 2
SSM_HPG = SSM_HEADS // SSM_GROUPS
SSM_STATE = 128
SSM_CONV = 4
SSM_CHUNK = 128
SSM_XBC = SSM_INNER + 2 * SSM_GROUPS * SSM_STATE
EVEN_IN = 2 * CONV_CH + SSM_INNER + SSM_XBC + SSM_HEADS
EVEN_MIX = CONV_CH + SSM_INNER

GLA_HEADS = 4
GLA_DK_TOTAL = D_MODEL // 2
GLA_DV_TOTAL = D_MODEL
GLA_DK = GLA_DK_TOTAL // GLA_HEADS
GLA_DV = GLA_DV_TOTAL // GLA_HEADS
GLA_RANK = 16
GLA_TAU = 16.0
GLA_CHUNK = 64
ODD_IN = 2 * GLA_DK_TOTAL + 2 * GLA_DV_TOTAL + GLA_RANK

MEM_LEN = 256
XA_HEADS = 4
XA_HEAD_DIM = D_MODEL // XA_HEADS
D_FF_2 = 4 * D_MODEL

N_EVEN = (DEPTH_2 + 1) // 2
N_ODD = DEPTH_2 // 2


def layer_norm(x, g, b):
    xf = x.astype(jnp.float32)
    mu = jnp.mean(xf, -1, keepdims=True)
    var = jnp.mean(jnp.square(xf - mu), -1, keepdims=True)
    return ((xf - mu) * lax.rsqrt(var + LN_EPS) * g + b).astype(x.dtype)

def rms_norm(x, g):
    xf = x.astype(jnp.float32)
    return (xf * lax.rsqrt(jnp.mean(xf * xf, -1, keepdims=True) + LN_EPS) * g).astype(x.dtype)

def causal_depthwise_conv(x, w, b):
    width = w.shape[0]
    y = lax.conv_general_dilated(x, w[:, None, :].astype(x.dtype), window_strides=(1,),
                                 padding=[(width - 1, 0)],
                                 dimension_numbers=('NWC', 'WIO', 'NWC'),
                                 feature_group_count=x.shape[-1])
    return y + b

def ssd_chunked(x, a, b_mat, c_mat):
    bsz, seqlen = x.shape[:2]
    nc, q = seqlen // SSM_CHUNK, SSM_CHUNK
    xc = x.reshape(bsz, nc, q, SSM_GROUPS, SSM_HPG, SSM_HEAD_DIM)
    ac = jnp.moveaxis(a.astype(jnp.float32).reshape(bsz, nc, q, SSM_GROUPS, SSM_HPG), 2, -1)
    bm = b_mat.reshape(bsz, nc, q, SSM_GROUPS, SSM_STATE)
    cm = c_mat.reshape(bsz, nc, q, SSM_GROUPS, SSM_STATE)
    a_cs = jnp.cumsum(ac, axis=-1)
    causal = jnp.tril(jnp.ones((q, q), dtype=bool))
    seg = a_cs[..., :, None] - a_cs[..., None, :]
    decay = jnp.exp(jnp.where(causal, seg, -jnp.inf)).astype(x.dtype)
    cb = jnp.einsum('bclgn,bcsgn->bcgls', cm, bm)
    y_diag = jnp.einsum('bcgkls,bcsgkp->bclgkp', cb[:, :, :, None] * decay, xc)
    decay_to_end = jnp.exp(a_cs[..., -1:] - a_cs).astype(x.dtype)
    states = jnp.einsum('bcsgn,bcgks,bcsgkp->bcgkpn', bm, decay_to_end, xc)
    chunk_decay = jnp.exp(a_cs[..., -1])

    def step(h, inp):
        st, dec = inp
        return h * dec[..., None, None] + st, h

    h0 = jnp.zeros((bsz, SSM_GROUPS, SSM_HPG, SSM_HEAD_DIM, SSM_STATE), jnp.float32)
    _, prev = lax.scan(step, h0, (jnp.moveaxis(states, 1, 0), jnp.moveaxis(chunk_decay, 1, 0)))
    prev = jnp.moveaxis(prev, 0, 1)
    y_off = jnp.einsum('bclgn,bcgkpn,bcgkl->bclgkp', cm, prev, jnp.exp(a_cs))
    return (y_diag + y_off).astype(x.dtype).reshape(bsz, seqlen, SSM_HEADS, SSM_HEAD_DIM)

def even_mixer(x, w_in, conv_w, conv_b, conv_ln_g, conv_ln_b, ssm_conv_w, ssm_conv_b,
               dt_bias, a_log, d_skip, ssm_norm_g, w_out):
    bsz, seqlen, _ = x.shape
    proj = x @ w_in
    c0 = CONV_CH
    c1 = 2 * CONV_CH
    c2 = c1 + SSM_INNER
    c3 = c2 + SSM_XBC
    conv_val, conv_gate, z, xbc, dt = jnp.split(proj, [c0, c1, c2, c3], axis=-1)
    u = conv_val * jax.nn.sigmoid(conv_gate)
    u = causal_depthwise_conv(u, conv_w, conv_b)
    u = jax.nn.silu(layer_norm(u, conv_ln_g, conv_ln_b))
    xbc = jax.nn.silu(causal_depthwise_conv(xbc, ssm_conv_w, ssm_conv_b))
    xs, bm, cm = jnp.split(xbc, [SSM_INNER, SSM_INNER + SSM_GROUPS * SSM_STATE], axis=-1)
    dt = jax.nn.softplus((dt + dt_bias).astype(jnp.float32))
    a = -jnp.exp(a_log.astype(jnp.float32))
    xs_h = xs.reshape(bsz, seqlen, SSM_HEADS, SSM_HEAD_DIM)
    y = ssd_chunked((xs_h * dt[..., None]).astype(x.dtype), dt * a,
                    bm.reshape(bsz, seqlen, SSM_GROUPS, SSM_STATE),
                    cm.reshape(bsz, seqlen, SSM_GROUPS, SSM_STATE))
    y = (y + xs_h * d_skip[:, None]).reshape(bsz, seqlen, SSM_INNER) * jax.nn.silu(z)
    y = rms_norm(y.reshape(bsz, seqlen, SSM_GROUPS, SSM_INNER // SSM_GROUPS),
                 ssm_norm_g.reshape(SSM_GROUPS, SSM_INNER // SSM_GROUPS)).reshape(bsz, seqlen, SSM_INNER)
    return jnp.concatenate([u, y.astype(u.dtype)], axis=-1) @ w_out

def gla_chunked(q, k, v, log_g):
    bsz, seqlen = q.shape[:2]
    n, c = seqlen // GLA_CHUNK, GLA_CHUNK
    q = q.reshape(bsz, n, c, GLA_HEADS, GLA_DK)
    k = k.reshape(bsz, n, c, GLA_HEADS, GLA_DK)
    v = v.reshape(bsz, n, c, GLA_HEADS, GLA_DV)
    b_cs = jnp.cumsum(log_g.astype(jnp.float32).reshape(bsz, n, c, GLA_HEADS, GLA_DK), axis=2)
    q_t = q * jnp.exp(b_cs) * (GLA_DK ** -0.5)
    k_t = k * jnp.exp(-b_cs)
    k_end = k * jnp.exp(b_cs[:, :, -1:] - b_cs)
    causal = jnp.tril(jnp.ones((c, c), dtype=bool))
    att = jnp.where(causal, jnp.einsum('bnlhd,bnshd->bnhls', q_t, k_t), 0.0)
    o = jnp.einsum('bnhls,bnshv->bnlhv', att, v)
    kv = jnp.einsum('bnshd,bnshv->bnhdv', k_end, v)
    chunk_decay = jnp.exp(b_cs[:, :, -1])

    def step(s, inp):
        kv_c, dec = inp
        return s * dec[..., None] + kv_c, s

    s0 = jnp.zeros((bsz, GLA_HEADS, GLA_DK, GLA_DV), jnp.float32)
    _, prev = lax.scan(step, s0, (jnp.moveaxis(kv, 1, 0), jnp.moveaxis(chunk_decay, 1, 0)))
    prev = jnp.moveaxis(prev, 0, 1)
    o = o + jnp.einsum('bnlhd,bnhdv->bnlhv', q_t, prev)
    return o.astype(v.dtype).reshape(bsz, seqlen, GLA_HEADS, GLA_DV)

def odd_mixer(x, w_in, w_gate2, b_gate, head_norm_g, w_out):
    bsz, seqlen, _ = x.shape
    proj = x @ w_in
    s0 = GLA_DK_TOTAL
    s1 = 2 * GLA_DK_TOTAL
    s2 = s1 + GLA_DV_TOTAL
    s3 = s2 + GLA_DV_TOTAL
    q, k, v, g_out, g_low = jnp.split(proj, [s0, s1, s2, s3], axis=-1)
    log_g = jax.nn.log_sigmoid((g_low @ w_gate2 + b_gate).astype(jnp.float32)) / GLA_TAU
    o = gla_chunked(q.reshape(bsz, seqlen, GLA_HEADS, GLA_DK),
                    k.reshape(bsz, seqlen, GLA_HEADS, GLA_DK),
                    v.reshape(bsz, seqlen, GLA_HEADS, GLA_DV),
                    log_g.reshape(bsz, seqlen, GLA_HEADS, GLA_DK))
    o = rms_norm(o, head_norm_g).reshape(bsz, seqlen, GLA_DV_TOTAL) * jax.nn.silu(g_out)
    return o @ w_out

def memory_cross_attention(x, mem, w_q, w_k, w_v, w_o):
    bsz, seqlen, _ = x.shape
    q = (x @ w_q).reshape(bsz, seqlen, XA_HEADS, XA_HEAD_DIM)
    k = (mem @ w_k).reshape(bsz, mem.shape[1], XA_HEADS, XA_HEAD_DIM)
    v = (mem @ w_v).reshape(bsz, mem.shape[1], XA_HEADS, XA_HEAD_DIM)
    s = jnp.einsum('blhd,bmhd->bhlm', q, k).astype(jnp.float32) * (XA_HEAD_DIM ** -0.5)
    p = jax.nn.softmax(s, axis=-1).astype(v.dtype)
    o = jnp.einsum('bhlm,bmhd->blhd', p, v).reshape(bsz, seqlen, D_MODEL)
    return o @ w_o

def sq_relu_mlp(x, w1, w2):
    return jnp.square(jax.nn.relu(x @ w1)) @ w2

def second_inputs(seed: int = 0) -> dict:
    key = jax.random.key(seed)
    ks = iter(jax.random.split(key, 40))
    f32 = jnp.float32

    def nrm(shape, scale):
        return jax.random.normal(next(ks), shape, f32) * scale

    dt0 = jnp.exp(jax.random.uniform(next(ks), (N_EVEN, SSM_HEADS), f32,
                                     np.log(1e-3).astype(np.float32), np.log(1e-1).astype(np.float32)))
    return {
        "x": nrm((BATCH, SEQ, D_MODEL), 1.0),
        "mem": nrm((BATCH, MEM_LEN, D_MODEL), 1.0),
        "even_w_in": nrm((N_EVEN, D_MODEL, EVEN_IN), D_MODEL ** -0.5),
        "even_conv_w": nrm((N_EVEN, CONV_WIDTH, CONV_CH), CONV_WIDTH ** -0.5),
        "even_conv_b": nrm((N_EVEN, CONV_CH), 0.01),
        "even_conv_ln_g": 1.0 + nrm((N_EVEN, CONV_CH), 0.02),
        "even_conv_ln_b": nrm((N_EVEN, CONV_CH), 0.02),
        "even_ssm_conv_w": nrm((N_EVEN, SSM_CONV, SSM_XBC), SSM_CONV ** -0.5),
        "even_ssm_conv_b": nrm((N_EVEN, SSM_XBC), 0.01),
        "even_dt_bias": dt0 + jnp.log(-jnp.expm1(-dt0)),
        "even_a_log": jnp.log(jax.random.uniform(next(ks), (N_EVEN, SSM_HEADS), f32, 1.0, 16.0)),
        "even_d_skip": 1.0 + nrm((N_EVEN, SSM_HEADS), 0.02),
        "even_ssm_norm_g": 1.0 + nrm((N_EVEN, SSM_INNER), 0.02),
        "even_w_out": nrm((N_EVEN, EVEN_MIX, D_MODEL), EVEN_MIX ** -0.5 * DEEPNORM_BETA),
        "odd_w_in": nrm((N_ODD, D_MODEL, ODD_IN), D_MODEL ** -0.5),
        "odd_w_gate2": nrm((N_ODD, GLA_RANK, GLA_DK_TOTAL), GLA_RANK ** -0.5),
        "odd_b_gate": nrm((N_ODD, GLA_DK_TOTAL), 0.1),
        "odd_head_norm_g": 1.0 + nrm((N_ODD, GLA_DV), 0.02),
        "odd_w_out": nrm((N_ODD, GLA_DV_TOTAL, D_MODEL), GLA_DV_TOTAL ** -0.5 * DEEPNORM_BETA),
        "xa_w_q": nrm((DEPTH_2, D_MODEL, D_MODEL), D_MODEL ** -0.5),
        "xa_w_k": nrm((DEPTH_2, D_MODEL, D_MODEL), D_MODEL ** -0.5),
        "xa_w_v": nrm((DEPTH_2, D_MODEL, D_MODEL), D_MODEL ** -0.5),
        "xa_w_o": nrm((DEPTH_2, D_MODEL, D_MODEL), D_MODEL ** -0.5 * DEEPNORM_BETA),
        "mlp_w1": nrm((DEPTH_2, D_MODEL, D_FF_2), D_MODEL ** -0.5),
        "mlp_w2": nrm((DEPTH_2, D_FF_2, D_MODEL), D_FF_2 ** -0.5 * DEEPNORM_BETA),
        "ln_g": 1.0 + nrm((DEPTH_2, 3, D_MODEL), 0.02),
        "ln_b": nrm((DEPTH_2, 3, D_MODEL), 0.02),
    }

def second_block(x, mem, even_w_in, even_conv_w, even_conv_b, even_conv_ln_g, even_conv_ln_b,
              even_ssm_conv_w, even_ssm_conv_b, even_dt_bias, even_a_log, even_d_skip,
              even_ssm_norm_g, even_w_out, odd_w_in, odd_w_gate2, odd_b_gate, odd_head_norm_g,
              odd_w_out, xa_w_q, xa_w_k, xa_w_v, xa_w_o, mlp_w1, mlp_w2, ln_g, ln_b):
    h = x
    for i in range(DEPTH_2):
        j = i // 2
        if i % 2 == 0:
            m = even_mixer(h, even_w_in[j], even_conv_w[j], even_conv_b[j], even_conv_ln_g[j],
                           even_conv_ln_b[j], even_ssm_conv_w[j], even_ssm_conv_b[j],
                           even_dt_bias[j], even_a_log[j], even_d_skip[j], even_ssm_norm_g[j],
                           even_w_out[j])
        else:
            m = odd_mixer(h, odd_w_in[j], odd_w_gate2[j], odd_b_gate[j], odd_head_norm_g[j],
                          odd_w_out[j])
        h = layer_norm(DEEPNORM_ALPHA * h + m, ln_g[i, 0], ln_b[i, 0])
        h = layer_norm(DEEPNORM_ALPHA * h + memory_cross_attention(h, mem, xa_w_q[i], xa_w_k[i],
                                                                   xa_w_v[i], xa_w_o[i]),
                       ln_g[i, 1], ln_b[i, 1])
        h = layer_norm(DEEPNORM_ALPHA * h + sq_relu_mlp(h, mlp_w1[i], mlp_w2[i]),
                       ln_g[i, 2], ln_b[i, 2])
    return h


def setup_inputs(seed=0):
    out = dict(first_inputs(seed))
    for name, value in second_inputs(seed + 1).items():
        if name != "x":
            out[name + "_2"] = value
    return out


def reference(
    x, c, rel_bias, ada_w, ada_b, norm_mix, w_in, gate_b, diff_lambda, diff_subln, dsa_kv_norm,
    dsa_w_uv, w_br_a, w_br_b, w_br_c, w_o, norm_mlp, w_ff1, w_ff2, norm_final, mem_2,
    even_w_in_2, even_conv_w_2, even_conv_b_2, even_conv_ln_g_2, even_conv_ln_b_2,
    even_ssm_conv_w_2, even_ssm_conv_b_2, even_dt_bias_2, even_a_log_2, even_d_skip_2,
    even_ssm_norm_g_2, even_w_out_2, odd_w_in_2, odd_w_gate2_2, odd_b_gate_2, odd_head_norm_g_2,
    odd_w_out_2, xa_w_q_2, xa_w_k_2, xa_w_v_2, xa_w_o_2, mlp_w1_2, mlp_w2_2, ln_g_2, ln_b_2,
):
    x = first_block(
        x, c, rel_bias, ada_w, ada_b, norm_mix, w_in, gate_b, diff_lambda, diff_subln,
        dsa_kv_norm, dsa_w_uv, w_br_a, w_br_b, w_br_c, w_o, norm_mlp, w_ff1, w_ff2, norm_final,
    )
    return second_block(
        x, mem_2, even_w_in_2, even_conv_w_2, even_conv_b_2, even_conv_ln_g_2, even_conv_ln_b_2,
        even_ssm_conv_w_2, even_ssm_conv_b_2, even_dt_bias_2, even_a_log_2, even_d_skip_2,
        even_ssm_norm_g_2, even_w_out_2, odd_w_in_2, odd_w_gate2_2, odd_b_gate_2,
        odd_head_norm_g_2, odd_w_out_2, xa_w_q_2, xa_w_k_2, xa_w_v_2, xa_w_o_2, mlp_w1_2,
        mlp_w2_2, ln_g_2, ln_b_2,
    )


_drawn_inputs = setup_inputs


def setup_inputs(seed=0):
    import zlib

    import numpy as np

    out = dict(_drawn_inputs(seed))
    spreads = {}
    factors = {'norm_mix': 4.771,
     'gate_b': 8.0,
     'diff_subln': 7.499,
     'dsa_kv_norm': 8.0,
     'norm_mlp': 3.163,
     'even_conv_b_2': 8.0,
     'even_conv_ln_g_2': 8.0,
     'even_conv_ln_b_2': 8.0,
     'even_ssm_conv_b_2': 8.0,
     'even_d_skip_2': 8.0,
     'even_ssm_norm_g_2': 8.0,
     'odd_head_norm_g_2': 8.0}
    for name, (base, spread) in spreads.items():
        noise = np.random.default_rng([zlib.crc32(name.encode()), seed]).standard_normal(out[name].shape)
        drawn = base * np.exp(spread * noise) if base else spread * noise
        out[name] = __import__('jax').numpy.asarray(drawn.astype(out[name].dtype))
    for name, factor in factors.items():
        out[name] = (out[name] * factor).astype(out[name].dtype)
    return out
```

```python
import math
from contextlib import ExitStack

import numpy as np

import concourse.bass as bass
from concourse import mybir

F32 = mybir.dt.float32
ALU = mybir.AluOpType
ACT = mybir.ActivationFunctionType
AX = mybir.AxisListType

P = 128
D = 1024
S = 512
KC = D // P
NT = S // P
NEG = -1.0e30
TAKEN = -3.0e38

HEADS_A = HEADS_B = HEADS_C = 4
DH = 64
IDX_HEADS = 8
IDX_DIM = 32
BUCKETS = 32
TOPK = min(256, S // 4)
FF = 4 * D
LAM_INIT = 0.8 - 0.6 * math.exp(0.0)

COL_AQ, COL_AK, COL_AV, COL_BQ = 0, 512, 1024, 1536
COL_BKV = 2048
COL_IQ = COL_BKV + 128
COL_IK = COL_IQ + 256
COL_IW = COL_IK + 32
COL_CQ = COL_IW + 8
COL_CK = COL_CQ + 256
COL_CV = COL_CK + 256
COL_G = COL_CV + 256

ALPHA = 4 ** 0.25
CONV_W = 31
SSM_CONV = 4
SSM_HEADS = 16
XBC = D + 2 * 2 * 128
XBC_C = XBC // P
EV_VAL, EV_GATE, EV_Z, EV_XBC, EV_DT = 0, D, 2 * D, 3 * D, 3 * D + XBC
GLA_HEADS = 4
GLA_C = 64
OD_Q, OD_K, OD_V, OD_G, OD_LOW = 0, 512, 1024, 2048, 3072
GLA_RANK = 16
MEM = 256
XA_HEADS = 4
SLOTS = 3
ARENA = 25728


def t5_bucket(n):
    n = np.maximum(n, 0)
    nf = np.maximum(n, 1).astype(np.float32)
    half = BUCKETS // 2
    large = half + (np.log(nf / np.float32(half)) / np.float32(math.log(128 / half)) * np.float32(half)).astype(np.int32)
    return np.where(n < half, n, np.minimum(large, BUCKETS - 1))


def shape_constants():
    i = np.arange(P)
    ident = np.eye(P, dtype=np.float32)
    upper = (i[:, None] <= i[None, :]).astype(np.float32)
    seg_mask = np.where(i[:, None] <= i[None, :], 0.0, NEG).astype(np.float32)
    again = np.tile((np.arange(S) % GLA_C != 0).astype(np.float32), (P, 1))
    causal = np.zeros((P, S), np.float32)
    causal[:, S - P:] = np.where(i[:, None] >= i[None, :], 0.0, NEG)
    square = np.concatenate([ident, upper, seg_mask, again, causal, ident[::-1]], axis=1)
    width = 640
    dist = (S - 1) - np.arange(width)
    onehot = np.zeros((BUCKETS + 1, width), np.float32)
    bucket = t5_bucket(dist)
    for m in range(width):
        onehot[bucket[m], m] = 1.0
    onehot[BUCKETS] = np.where(dist < 0, NEG, 0.0)
    return np.ascontiguousarray(square), onehot


class Queue:

    def __init__(self, sem):
        self.sem, self.count, self.jobs, self.waited = sem, 0, [], {}

    def wait(self, *tokens):
        for t in tokens:
            if t is None:
                continue
            if isinstance(t, list):
                self.wait(*t)
                continue
            sem, value = t
            if self.waited.get(id(sem), 0) < value:
                self.waited[id(sem)] = value
                self.jobs.append((sem, value, None))

    def do(self, make, *tokens, signal=True):
        self.wait(*tokens)
        if signal:
            self.count += 1
        self.jobs.append((self.sem if signal else None, 1, make))
        return (self.sem, self.count)

    def dma(self, sem, make, *tokens):
        self.wait(*tokens)
        sem.count += 16
        self.jobs.append((sem.sem, 16, make))
        return (sem.sem, sem.count)

    @property
    def now(self):
        return (self.sem, self.count) if self.count else None

    def run(self, eng):
        for sem, value, make in self.jobs:
            if make is None:
                eng.wait_ge(sem, value)
            elif sem is None:
                make(eng)
            else:
                make(eng).then_inc(sem, value)


class DmaCount:
    def __init__(self, sem):
        self.sem, self.count = sem, 0


class Ring:

    def __init__(self, bufs):
        self.bufs, self.free, self.n = bufs, [None] * len(bufs), 0

    def take(self):
        i = self.n % len(self.bufs)
        self.n += 1
        return i, self.bufs[i], self.free[i]


def program(nc, A, out):
    ctx = ExitStack()
    with ctx:
        def sb(name, shape):
            return ctx.enter_context(nc.sbuf_tensor(name, shape, F32))

        def semaphore(name):
            return ctx.enter_context(nc.semaphore(name))

        pe, act, dve, pool, sp = (Queue(semaphore("s_" + n)) for n in ("pe", "act", "dve", "pool", "sp"))

        def so_far():
            return [q.now for q in (pe, act, dve, pool)]

        def stage():
            t = so_far()
            for q in (act, dve, pool):
                q.wait(*t)

        hT = sb("hT", [P, KC, S])
        uT = sb("uT", [P, KC, S])
        arena = sb("arena", [P, ARENA])
        slots = [sb(f"w{i}", [P, KC, 512]) for i in range(SLOTS)]
        const = sb("const", [P, 4 * P + 2 * S])
        ones = sb("ones", [P, P])
        vec = sb("vec", [P, 6, P])
        wsmall = sb("wsmall", [P, KC, 16])
        stat = sb("stat", [P, 3, S])
        sq = sb("sq", [P, 2, S])
        eps_t = sb("eps", [P, 4])
        lamb = sb("lamb", [P, 3 * P])
        modc = sb("modc", [P, 7 * KC])
        soft = sb("soft", [P, 64])
        gates = sb("gates", [P, 2, S])[:, :, :]

        ident = const[:, 0:P]
        upper = const[:, P:2 * P]
        seg_mask = const[:, 2 * P:3 * P]
        again = const[:, 3 * P:3 * P + S]
        causal = const[:, 3 * P + S:3 * P + 2 * S]
        flip = const[:, 3 * P + 2 * S:4 * P + 2 * S]

        def area(off, *shape):
            n = int(np.prod(shape))
            assert off + n <= ARENA, (off, shape)
            v = arena[:, off:off + n]
            if len(shape) == 2:
                v = v.rearrange("p (a b) -> p a b", a=shape[0])
            if len(shape) == 3:
                v = v.rearrange("p (a b c) -> p a b c", a=shape[0], b=shape[1])
            return v, off + n

        banks = [ctx.enter_context(nc.psum_tensor(f"ps{i}", [P, 512], F32)) for i in range(8)]
        lin = Ring(banks[0:4])
        att = Ring(banks[4:8])

        slot_sem = [DmaCount(semaphore(f"s_w{i}")) for i in range(SLOTS)]
        slot_ring = Ring(slots)

        def load_weights(dram, rows, cols, transposed_rows=None):
            i, slot, free = slot_ring.take()
            kc = rows // P
            dst = slot[:, 0:kc, 0:cols]
            t = sp.dma(slot_sem[i], lambda e: e.dma_start(dst, dram.rearrange("(k p) n -> p k n", p=P)), free)
            return i, slot, t

        def free_slot(i, token):
            slot_ring.free[i] = token

        n_small = [0]

        def small_dma(q, dst, src, *tokens):
            n_small[0] += 1
            c = DmaCount(semaphore(f"s_d{n_small[0]}"))
            return q.dma(c, lambda e: e.dma_start(dst, src), *tokens)

        def mm(o, l, r, start, stop, *tokens, signal=False):
            return pe.do(lambda e: e.matmul(o, l, r, start=start, stop=stop), *tokens, signal=signal)

        def mm_group(o, pairs, *tokens):
            t = None
            for n, (l, r) in enumerate(pairs):
                last = n == len(pairs) - 1
                t = mm(o, l, r, n == 0, last, *(tokens if n == 0 else ()), signal=last)
            return t

        def turn(o, i, *tokens, signal=True):
            return pe.do(lambda e: e.transpose(o, i, ident[0:i.shape[0], 0:i.shape[0]]), *tokens, signal=signal)

        def copy(q, o, i, *t):
            if q is act:
                return q.do(lambda e: e.activation(o, i, ACT.Copy), *t)
            return q.do(lambda e: e.tensor_copy(o, i), *t)

        def fn(o, i, f, *t, bias=0.0, scale=1.0, accum=None):
            if accum is None:
                return act.do(lambda e: e.activation(o, i, f, bias=bias, scale=scale), *t)
            return act.do(lambda e: e.activation(o, i, f, bias=bias, scale=scale, accum_out=accum), *t)

        def tt(q, o, a, b, op, *t):
            return q.do(lambda e: e.tensor_tensor(o, a, b, op), *t)

        def ts(q, o, a, s1, op0, *t, s2=None, op1=None):
            if op1 is None:
                return q.do(lambda e: e.tensor_scalar(o, a, s1, None, op0), *t)
            return q.do(lambda e: e.tensor_scalar(o, a, s1, s2, op0, op1), *t)

        def stt(o, a, s, b, op0, op1, *t):
            return dve.do(lambda e: e.scalar_tensor_tensor(out=o, in0=a, scalar=s, in1=b, op0=op0, op1=op1), *t)

        def recip(o, i, *t):
            return dve.do(lambda e: e.reciprocal(o, i), *t)

        def memset(q, o, v, *t):
            return q.do(lambda e: e.memset(o, v), *t)

        t_const = small_dma(act, const[:, :], A["c_square"])
        t_ones = memset(dve, ones[:, :], 1.0)
        t_e1 = memset(dve, eps_t[:, 0:1], 1e-6)
        t_e2 = memset(dve, eps_t[:, 1:2], 1e-5)
        for q in (act, dve, pe):
            q.wait(t_const, t_ones, t_e1, t_e2)

        xin, o1 = area(0, NT, D)
        packs, o2 = area(o1, 6, P)
        t_x = small_dma(sp, xin, A["x"][0].rearrange("(t p) n -> p t n", p=P))
        pack_lists = [
            [("norm_mix", 8), ("gate_b", 24), ("norm_mlp", 8), ("norm_final", 8), ("diff_subln", 1),
             ("dsa_kv_norm", 1), ("ada_b", 48), ("c", 8)],
            [("even_conv_b_2", 8), ("even_conv_ln_g_2", 8), ("even_conv_ln_b_2", 8),
             ("even_ssm_conv_b_2", 12), ("even_ssm_norm_g_2", 8), ("even_ssm_conv_w_2", 48),
             ("odd_b_gate_2", 4), ("odd_head_norm_g_2", 2)],
            [("ln_g_2", 48), ("ln_b_2", 48)],
        ]
        col = {}
        t_zero = memset(pool, packs, 0.0)
        t_packs = [[] for _ in range(5)]
        for n, names in enumerate(pack_lists):
            at = 0
            for name, rows in names:
                a = A[name]
                while len(a.shape) > 1:
                    a = a.rearrange("a b ... -> (a b) ...") if len(a.shape) > 2 else a.rearrange("a b -> (a b)")
                t_packs[n].append(small_dma(act if n else sp, packs[at:at + rows, n, :],
                                            a.rearrange("(r p) -> r p", p=P), t_zero))
                col[name] = (n, at)
                at += rows
        conv_rows = A["even_conv_w_2"][0].rearrange("t (m p) -> (t m) p", p=P)
        t_packs[3].append(small_dma(act, packs[:, 3, :], conv_rows[0:P, :], t_zero))
        t_packs[4].append(small_dma(act, packs[0:CONV_W * KC - P, 4, :], conv_rows[P:CONV_W * KC, :], t_zero))
        for n in range(5):
            i, b, free = att.take()
            t = turn(b[:, 0:P], packs[:, n, :], *t_packs[n], free)
            t_vec = att.free[i] = copy(dve, vec[:, n, :], b[:, 0:P], t)
        for q in (act, dve, pe, pool):
            q.wait(t_vec)

        def column(name, m=0):
            n, at = col[name]
            return vec[:, n, at + m:at + m + 1]

        def columns(name, m, k):
            n, at = col[name]
            return vec[:, n, at + m:at + m + k]

        def conv_tap(t, m):
            r = t * KC + m
            return vec[:, 3 + r // P, r % P:r % P + 1]

        for k in range(KC):
            i, b, free = att.take()
            for t in range(NT):
                tok = turn(b[:, t * P:(t + 1) * P], xin[:, t, k * P:(k + 1) * P], t_x, free, signal=t == NT - 1)
            t_h = att.free[i] = copy(dve if k % 2 else act, hT[:, k, :], b[:, :], tok)
            if k >= KC - 2:
                pe.wait(t_h)
        stage()

        def linear(x, parts, n_cols, evac, *x_tokens):
            for c0 in range(0, n_cols, 512):
                w = min(512, n_cols - c0)
                chunks = range(0, w, P)
                took = []
                for pi, (dram, xc) in enumerate(parts):
                    rows = dram.shape[0]
                    si, slot, t_w = load_weights(dram[:, c0:c0 + w], rows, w)
                    for j, c in enumerate(chunks):
                        if pi == 0:
                            took.append(lin.take())
                        bi, b, free = took[j]
                        kc = rows // P
                        for k in range(kc):
                            first = pi == 0 and k == 0
                            last = k == kc - 1
                            t = mm(b[:, :], slot[:, k, c:c + P], xc(k), first,
                                   pi == len(parts) - 1 and last,
                                   t_w, free if first else None, *x_tokens, signal=last)
                        if pi == len(parts) - 1:
                            lin.free[bi] = evac(c0 // P + j, b[:, :], t)
                        if j == len(chunks) - 1:
                            free_slot(si, t)
                        yield

        def linear_tokens(x, dram, evac, *x_tokens):
            cols = dram.shape[1]
            si, slot, t_w = load_weights(dram, dram.shape[0], cols)
            for t in range(x(0).shape[1] // P):
                bi, b, free = lin.take()
                tok = mm_group(b[:, 0:cols], [(x(k)[:, t * P:(t + 1) * P], slot[:, k, 0:cols])
                                              for k in range(dram.shape[0] // P)], t_w, free, *x_tokens)
                lin.free[bi] = evac(t, b, tok)
                free_slot(si, tok)
                yield

        def run_all(gen):
            for _ in gen:
                pass

        def step(gen, n=1):
            for _ in range(n):
                if next(gen, "end") == "end":
                    return

        def chain(*gens):
            for g in gens:
                yield from g

        sq_ring = Ring([sq[:, 0, :], sq[:, 1, :]])

        def add_square(b, src, first, last, free, *tokens):
            i, s, f = sq_ring.take()
            t = fn(s, src, ACT.Square, f, *tokens)
            sq_ring.free[i] = t2 = mm(b, ones[:, :], s, first, last, t, free if first else None, signal=True)
            return t2

        def rstd_of(ss_bank, t_ss, n, eps_col, o, mean_sq=None, *tokens):
            if mean_sq is None:
                t = fn(o, ss_bank, ACT.Ln, t_ss, *tokens, bias=eps_t[0:o.shape[0], eps_col:eps_col + 1], scale=1.0 / n)
            else:
                t = stt(o, ss_bank, 1.0 / n, mean_sq, ALU.mult, ALU.subtract, t_ss, *tokens)
                t = fn(o, o, ACT.Ln, t, bias=eps_t[:, eps_col:eps_col + 1])
            return fn(o, o, ACT.Exp, t, scale=-0.5), t

        def rms_stats(src, chunks, n, eps_col, o, tokens, *w):
            i, b, free = att.take()
            for j, k in enumerate(chunks):
                t = add_square(b[:, :], src(k), j == 0, j == len(chunks) - 1, free, tokens[k], *w)
            r, freed = rstd_of(b[:, :], t, n, eps_col, o, None, *w)
            att.free[i] = freed
            return r

        def layer_norm(src, src_tokens, g, bcol, dst, func=None):
            i1, b1, f1 = att.take()
            i2, b2, f2 = att.take()
            for k in range(KC):
                add = mm(b1[:, :], ones[:, :], src(k), k == 0, k == KC - 1, src_tokens[k], f1, signal=True)
                t = add_square(b2[:, :], src(k), k == 0, k == KC - 1, f2, src_tokens[k])
            mean, msq, rstd = (stat[:, j, :] for j in range(3))
            tm = ts(dve, mean, b1[:, :], 1.0 / D, ALU.mult, add, *stat_free)
            att.free[i1] = tm
            t3 = tt(dve, msq, mean, mean, ALU.mult, tm)
            r, fr = rstd_of(b2[:, :], t, D, 1, rstd, msq, t3)
            att.free[i2] = fr
            toks = []
            for k in range(KC):
                s = src(k)
                t1 = tt(pool if k % 2 else dve, s, s, mean, ALU.subtract, tm, add, t)
                t2 = stt(s, s, g(k), rstd, ALU.mult, ALU.mult, t1, r)
                if func is None:
                    toks.append(fn(dst(k), s, ACT.Identity, t2, bias=bcol(k)))
                else:
                    toks.append(func(k, s, t2))
            stat_free[:] = [t2, t1]
            return toks

        stat_free = []

        cond = modc[:, 6 * KC:7 * KC].unsqueeze(2)
        cc = columns("c", 0, KC)
        ct = cond[:, :, 0]
        t = fn(ct, cc, ACT.Tanh, scale=0.5)
        t = stt(ct, ct, 1.0, cc, ALU.add, ALU.mult, t)
        t_cond = ts(dve, ct, ct, 0.5, ALU.mult, t)
        rows_ring = Ring([gates[0:1, j, :] for j in range(2)])

        def ada(n0, n1):
            for n in range(n0, n1):
                si, slot, t_w = load_weights(A["ada_w"][0][:, n * 512:(n + 1) * 512], D, 512)
                bi, b, free = lin.take()
                t = mm_group(b[0:1, :], [(cond[:, k, :], slot[:, k, :]) for k in range(KC)], t_w, free, t_cond)
                free_slot(si, t)
                ri, r, rf = rows_ring.take()
                t = lin.free[bi] = copy(dve, r, b[0:1, :], t, rf)
                ai, ab, af = att.take()
                for j in range(4):
                    tok = mm(ab[:, j:j + 1], r[:, j * P:(j + 1) * P], ones[0:1, 0:1], True, True, t, af, signal=j == 3)
                rows_ring.free[ri] = tok
                m = n * 4
                t_mod[0] = att.free[ai] = tt(dve, modc[:, m:m + 4], ab[:, 0:4], columns("ada_b", m, 4), ALU.add, tok)
                yield

        t_mod = [None]
        run_all(ada(0, 4))
        shift = lambda i, m: modc[:, 24 * i + m:24 * i + m + 1]

        def modulated_gain(i, name):
            s = modc[:, 24 * i + 8:24 * i + 16]
            return stt(s, s, 1.0, columns(name, 0, 8), ALU.add, ALU.mult, t_mod[0])

        def modulated_norm(i, name, h_tokens):
            t_g = modulated_gain(i, name)
            r = rms_stats(lambda k: hT[:, k, :], range(KC), D, 0, stat[:, 0, :], h_tokens, *stat_free)
            toks = []
            for k in range(KC):
                t = stt(uT[:, k, :], hT[:, k, :], modc[:, 24 * i + 8 + k:24 * i + 9 + k], stat[:, 0, :],
                        ALU.mult, ALU.mult, r, t_g)
                stat_free[:] = [t]
                toks.append(fn(uT[:, k, :], uT[:, k, :], ACT.Identity, t, bias=shift(i, k)))
            return toks

        t_u = modulated_norm(0, "norm_mix", [t_h] * KC)
        u = lambda k: uT[:, k, :]
        t_u = [t_u[-1]]
        stage()

        o = 0
        aq, o = area(o, 4, S)
        ak, o = area(o, 4, S)
        av, o = area(o, NT, 512)
        bq, o = area(o, 4, S)
        kvT, o = area(o, S)
        kv, o = area(o, NT, P)
        iq, o = area(o, 2, S)
        ik, o = area(o, S)
        cq, o = area(o, 2, S)
        ck, o = area(o, 2, S)
        cv, o = area(o, NT, 4, P)
        bias, o = area(o, 12, S)
        ws, o = area(o, 4, S)
        PT, o = area(o, NT, S)
        iw, o = area(o, NT, 8)
        top8, o = area(o, 8)
        w_in = A["w_in"][0]
        pick = stat

        table = lamb[0:BUCKETS + 1, 0:12]
        t0 = memset(dve, lamb[BUCKETS:BUCKETS + 1, 0:12], 1.0)
        t_tab = small_dma(sp, lamb[0:BUCKETS, 0:12], A["rel_bias"])
        oneh = ws[0:BUCKETS + 1, 0:2, :].rearrange("p a b -> p (a b)")[:, 0:640]
        t_one = small_dma(sp, oneh, A["c_onehot"], *so_far())
        strip = PT[0:12, 0:2, :].rearrange("p a b -> p (a b)")[:, 0:640]
        for c0, c1 in ((0, 512), (512, 640)):
            i, b, free = att.take()
            t = mm_group(b[0:12, 0:c1 - c0], [(table, oneh[:, c0:c1])], t_tab, t_one, t0, free)
            t_s = att.free[i] = copy(act, strip[:, c0:c1], b[0:12, 0:c1 - c0], t)
        t_sd = small_dma(sp, A["strip"], strip, t_s)
        flip_ring = Ring([cv[:, j, :, :].rearrange("p a b -> p (a b)") for j in range(NT)])
        for h in range(12):
            src = bass.AP(A["strip"].tensor, h * 640, [[1, P], [1, S]])
            fi, fb, ff = flip_ring.take()
            t = small_dma(sp, fb, src, t_sd, ff)
            i, b, free = att.take()
            t = flip_ring.free[fi] = mm_group(b[:, :], [(flip, fb)], t, free)
            t_bias = att.free[i] = copy(act, bias[:, h, :], b[:, :], t)
        dve.wait(t_bias)
        act.wait(t_sd)

        dl = lamb[:, P:P + 256]
        t = small_dma(sp, dl, A["diff_lambda"].rearrange("a b c -> a (b c)").to_broadcast([P, 256]))
        pr = lamb[:, 32:96]
        lam = lamb[:, 96:100]
        for j in range(2):
            t = tt(dve, pr, dl[:, j * 128:j * 128 + 64], dl[:, j * 128 + 64:j * 128 + 128], ALU.mult, t)
            t = dve.do(lambda e, j=j: e.tensor_reduce(lam[:, j:j + 1], pr, AX.X, ALU.add), t)
        t = fn(lam[:, 0:2], lam[:, 0:2], ACT.Exp, t)
        t = tt(dve, lam[:, 2:3], lam[:, 1:2], lam[:, 0:1], ALU.subtract, t)
        t_lam = ts(dve, lam[:, 2:3], lam[:, 2:3], -LAM_INIT, ALU.add, t)
        sub_g = lam[:, 3:4]
        t_subg = ts(dve, sub_g, column("diff_subln"), 1.0 - LAM_INIT, ALU.mult)

        def to(dst, q=None):
            def evac(m, b, t):
                return copy(q or act, dst[:, m, :], b, t)
            return evac

        def to_tokens(dst):
            def evac(t, b, tok):
                return copy(act, dst[:, t, :], b[:, 0:512], tok)
            return evac

        run_all(linear(u, [(w_in[:, COL_AQ:COL_AQ + 512], u)], 512, to(aq), *t_u))
        run_all(linear(u, [(w_in[:, COL_AK:COL_AK + 512], u)], 512, to(ak), *t_u))
        run_all(linear_tokens(u, w_in[:, COL_AV:COL_AV + 512], to_tokens(av), *t_u))
        t_a = act.now

        t_cvz = memset(pool, cv, 0.0, pe.now)
        t_iw = [None]

        def evac_kv(m, b, t):
            return copy(act, kvT[:, :], b, t)

        def evac_cv(t, b, tok):
            src = b[:, 0:256].rearrange("p (h d) -> p h d", h=4)
            dst = cv[:, t, :, :].rearrange("p (g two) d -> p g two d", two=2)
            for par in range(2):
                last = copy(dve, dst[:, :, par, par * DH:(par + 1) * DH],
                            b[:, 0:256].rearrange("p (g two d) -> p g two d", two=2, d=DH)[:, :, par, :], tok, t_cvz)
            return last

        wik = gates.rearrange("p a b -> p (a b)").rearrange("p (a b) -> p a b", a=KC)
        t_wik = []
        for r in range(4):
            t_wik.append(small_dma(sp, wik[:, :, r * IDX_DIM:(r + 1) * IDX_DIM],
                                   w_in[:, COL_IK:COL_IK + IDX_DIM].rearrange("(k p) n -> p k n", p=P)))
        t_wiw = small_dma(sp, wsmall[:, :, 0:8], w_in[:, COL_IW:COL_IW + 8].rearrange("(k p) n -> p k n", p=P))

        def index_small():
            bi, b, free = lin.take()
            t = mm_group(b[:, :], [(wik[:, k, :], u(k)) for k in range(KC)], *t_wik, free)
            lin.free[bi] = copy(act, ik[:, :], b[:, :], t)
            yield
            bi, b, free = lin.take()
            for tt_ in range(NT):
                t = mm_group(b[:, tt_ * 8:tt_ * 8 + 8],
                             [(u(k)[:, tt_ * P:(tt_ + 1) * P], wsmall[:, k, 0:8]) for k in range(KC)], t_wiw, free)
            t_iw[0] = lin.free[bi] = ts(dve, iw, b[:, 0:32].rearrange("p (a b) -> p a b", a=NT),
                                        IDX_HEADS ** -0.5 * IDX_DIM ** -0.5, ALU.mult, t)
            yield

        fill = chain(
            linear(u, [(w_in[:, COL_BQ:COL_BQ + 512], u)], 512, to(bq)),
            linear(u, [(w_in[:, COL_BKV:COL_BKV + P], u)], P, evac_kv),
            linear(u, [(w_in[:, COL_IQ:COL_IQ + 256], u)], 256, to(iq)),
            index_small(),
            linear(u, [(w_in[:, COL_CQ:COL_CQ + 256], u)], 256, to(cq)),
            linear(u, [(w_in[:, COL_CK:COL_CK + 256], u)], 256, to(ck)),
            linear_tokens(u, w_in[:, COL_CV:COL_CV + 256], evac_cv),
        )

        ws_ring = Ring([ws[:, j, :] for j in range(4)])
        st_ring = Ring([soft[:, 4 * j:4 * j + 4] for j in range(8)])
        pt_free = [None]
        pt_written = {}

        def causal_softmax(q, k, qt, scale, hb, *tokens, extra=None):
            L = (qt + 1) * P
            i, b, free = att.take()
            t = mm(b[:, 0:L], q, k, True, True, free, *tokens, signal=True)
            wi, w, wf = ws_ring.take()
            si, st, sf = st_ring.take()
            w = w[:, 0:L]
            t = att.free[i] = stt(w, b[:, 0:L], scale, bias[:, hb, S - L:S], ALU.mult, ALU.add, t, wf, sf)
            if extra is not None:
                t = tt(dve, w, w, extra, ALU.add, t)
            t = dve.do(lambda e: e.tensor_reduce(st[:, 0:1], w, AX.X, ALU.max, negate=True), t)
            t = fn(w, w, ACT.Exp, t, bias=st[:, 0:1], accum=st[:, 1:2])
            t_r = recip(st[:, 2:3], st[:, 1:2], t)
            return w, wi, st, si, t_r

        def turn_rows(w, wi, qt, t_w, first):
            i, b, free = att.take()
            for kt in range(qt + 1):
                t = turn(b[:, kt * P:(kt + 1) * P], w[:, kt * P:(kt + 1) * P], t_w, free, signal=kt == qt)
            ws_ring.free[wi] = t
            t = att.free[i] = copy(act, PT[:, 0:qt + 1, qt * P:(qt + 1) * P],
                                   b[:, 0:(qt + 1) * P].rearrange("p (a b) -> p a b", b=P), t, pt_free[0])
            return t

        def weigh(b, v, free, first, last, t_pt):
            for kt in range(NT):
                t = mm(b[:, kt * P:S], v(kt), PT[:, kt, kt * P:S], first and kt == 0, last and kt == NT - 1,
                       t_pt, free if kt == 0 else None, signal=kt == NT - 1)
            pt_free[0] = t
            return t

        def diff_tiles():
            t_heads = []
            for h in range(HEADS_A):
                for qt in range(NT):
                    two = [causal_softmax(aq[DH * m:DH * (m + 1), h, qt * P:(qt + 1) * P],
                                          ak[DH * m:DH * (m + 1), h, 0:(qt + 1) * P], qt, DH ** -0.5, h, t_a)
                           for m in range(2)]
                    (w0, i0, s0, j0, r0), (w1, i1, s1, j1, r1) = two
                    t = tt(dve, s1[:, 3:4], s1[:, 2:3], lam[:, 2:3], ALU.mult, r1, t_lam)
                    t0 = ts(dve, w0, w0, s0[:, 2:3], ALU.mult, r0)
                    t = stt(w0, w1, s1[:, 3:4], w0, ALU.mult, ALU.add, t, t0)
                    ws_ring.free[i1] = t
                    st_ring.free[j0] = st_ring.free[j1] = t
                    yield
                    t_pt = turn_rows(w0, i0, qt, t, qt == 0)
                i, b, free = att.take()
                t = weigh(b, lambda kt: av[:, kt, h * P:(h + 1) * P], free, True, True, t_pt)
                t_o = copy(dve, aq[:, h, :], b[:, :], t)
                att.free[i] = t_o
                yield
                r = rms_stats(lambda k: aq[:, h, :], [0], P, 0, stat[:, 0, :], [t_o], *stat_free)
                t = stt(aq[:, h, :], aq[:, h, :], sub_g, stat[:, 0, :], ALU.mult, ALU.mult, r, t_subg)
                stat_free[:] = [t]
                t_heads.append(t)
            t_ya[0] = t_heads[-1]

        t_ya = [None]
        for _ in diff_tiles():
            step(fill)
        run_all(fill)
        t_proj = so_far()

        r = rms_stats(lambda k: kvT[:, :], [0], P, 0, stat[:, 0, :], t_proj[1:2], *stat_free)
        t_kv = stt(kvT[:, :], kvT[:, :], column("dsa_kv_norm"), stat[:, 0, :], ALU.mult, ALU.mult, r)
        stat_free[:] = [t_kv]
        i, b, free = att.take()
        for t_ in range(NT):
            t = turn(b[:, t_ * P:(t_ + 1) * P], kvT[:, t_ * P:(t_ + 1) * P], t_kv, free, signal=t_ == NT - 1)
        t_kv = att.free[i] = copy(act, kv, b[:, :].rearrange("p (a b) -> p a b", b=P), t)

        def index_scores():
            for qt in range(1, NT):
                L = (qt + 1) * P
                acc = pick[:, qt - 1, 0:L]
                t_acc = None
                for h in range(IDX_HEADS):
                    i, b, free = att.take()
                    r0 = IDX_DIM * (h % 4)
                    t = mm(b[:, 0:L], iq[r0:r0 + IDX_DIM, h // 4, qt * P:(qt + 1) * P],
                           ik[r0:r0 + IDX_DIM, 0:L], True, True, free, *t_proj, signal=True)
                    wi, w, wf = ws_ring.take()
                    t = att.free[i] = fn(w[:, 0:L], b[:, 0:L], ACT.Relu, t, wf)
                    if h == 0:
                        prev = causal[:, S - L:S]
                        t_acc = ts(dve, acc, w[:, 0:L], iw[:, qt, h:h + 1], ALU.mult, t, t_iw[0])
                    else:
                        t_acc = stt(acc, w[:, 0:L], iw[:, qt, h:h + 1], acc, ALU.mult, ALU.add, t, t_acc)
                    ws_ring.free[wi] = t_acc
                    if h % 4 == 3:
                        yield
                t_acc = tt(dve, acc, acc, causal[:, S - L:S], ALU.add, t_acc)
                t_pick[qt] = t_acc

        t_pick = [None] * NT

        def topk_rounds():
            for qt in range(1, NT):
                L = (qt + 1) * P
                acc = pick[:, qt - 1, 0:L]
                t = t_pick[qt]
                for r in range(TOPK // 8):
                    t = dve.do(lambda e, acc=acc: e.max(top8[:, :], acc), t)
                    t = dve.do(lambda e, acc=acc: e.match_replace(acc, top8[:, :], acc, TAKEN), t)
                    yield
                t_pick[qt] = ts(dve, acc, acc, 2.0 * NEG * 1e8, ALU.is_gt, t, s2=NEG, op1=ALU.mult)

        merged = arena[:, 2048:2048 + 8 * S].rearrange("p (a b) -> p a b", a=KC)
        gate_ring = Ring([gates[:, j, :] for j in range(2)])
        t_merged = [None] * KC

        def branch(n, weights, x_chunks, *tokens):
            for c0 in range(0, D, 512):
                si, slot, t_w = load_weights(w_in[:, COL_G + n * D + c0:COL_G + n * D + c0 + 512], D, 512)
                parts_rows = weights.shape[0]
                sj, slot2, t_w2 = load_weights(weights[:, c0:c0 + 512], parts_rows, 512)
                for j in range(4):
                    m = c0 // P + j
                    bi, b, free = lin.take()
                    t = mm_group(b[:, :], [(slot[:, k, j * P:(j + 1) * P], u(k)) for k in range(KC)], t_w, free)
                    if j == 3:
                        free_slot(si, t)
                    gi, g, gf = gate_ring.take()
                    tg = lin.free[bi] = fn(g, b[:, :], ACT.Tanh, t, gf, t_half, bias=gbh[:, n * 8 + m:n * 8 + m + 1], scale=0.5)
                    tg = ts(pool, g, g, 0.5, ALU.mult, tg, s2=0.5, op1=ALU.add)
                    bi, b, free = lin.take()
                    t = mm_group(b[:, :], [(slot2[:, k, j * P:(j + 1) * P], x_chunks(k)) for k in range(parts_rows // P)],
                                 t_w2, free, *tokens)
                    if j == 3:
                        free_slot(sj, t)
                    if n == 0:
                        t = tt(dve, merged[:, m, :], b[:, :], g, ALU.mult, t, tg)
                        t_merged[m] = gate_ring.free[gi] = lin.free[bi] = t
                    else:
                        t = lin.free[bi] = tt(dve, g, b[:, :], g, ALU.mult, t, tg)
                        t_merged[m] = gate_ring.free[gi] = tt(pool, merged[:, m, :], merged[:, m, :], g, ALU.add,
                                                              t, t_merged[m])
                    yield

        gbh = sb("gbh", [P, 24])
        t_half = ts(dve, gbh[:, :], columns("gate_b", 0, 24), 0.5, ALU.mult)

        def block_tiles():
            for g in range(2):
                oi, ob, of = att_out.take()
                for par in range(2):
                    h = 2 * g + par
                    for qt in range(NT):
                        w, wi, st, si, t = causal_softmax(
                            cq[DH * par:DH * (par + 1), g, qt * P:(qt + 1) * P],
                            ck[DH * par:DH * (par + 1), g, 0:(qt + 1) * P], qt, DH ** -0.5, 8 + h, *t_proj)
                        t = fn(w, w, ACT.Copy, t, scale=st[:, 2:3])
                        st_ring.free[si] = t
                        yield
                        t_pt = turn_rows(w, wi, qt, t, qt == 0)
                    t = weigh(ob, lambda kt: cv[:, kt, h, :], of if par == 0 else None, par == 0, par == 1, t_pt)
                t_c[g] = att_out.free[oi] = copy(dve, cq[:, g, :], ob[:, :], t)

        att.bufs, att.free = banks[4:7], att.free[:3]
        att.n = 0
        att.free = [so_far()] * 3
        att_out = Ring([banks[7]])
        att_out.free = [so_far()]
        t_c = [None, None]
        t_b = [None] * 4

        def latent_tiles():
            for h in range(HEADS_B):
                for qt in range(NT):
                    extra = pick[:, qt - 1, 0:(qt + 1) * P] if qt else None
                    w, wi, st, si, t = causal_softmax(
                        bq[:, h, qt * P:(qt + 1) * P], kvT[:, 0:(qt + 1) * P], qt, P ** -0.5, 4 + h,
                        *t_proj, t_kv, t_pick[qt] if qt else None, extra=extra)
                    t = fn(w, w, ACT.Copy, t, scale=st[:, 2:3])
                    st_ring.free[si] = t
                    yield
                    t_pt = turn_rows(w, wi, qt, t, qt == 0)
                oi, ob, of = att_out.take()
                t = weigh(ob, lambda kt: kv[:, kt, :], of, True, True, t_pt)
                t_b[h] = att_out.free[oi] = copy(dve, bq[:, h, :], ob[:, :], t)

        filler = branch(0, A["w_br_a"][0], lambda k: aq[:, k, :], t_ya[0])
        tops = topk_rounds()
        for _ in index_scores():
            step(filler)
        for _ in block_tiles():
            step(tops, 3)
            step(filler)
        run_all(tops)
        filler = chain(filler, branch(2, A["w_br_c"][0], lambda k: cq[:, k, :], t_c[1]))
        for n, _ in enumerate(latent_tiles()):
            if n % 2:
                step(filler)
        run_all(filler)
        wuv = sq[:, 0, :].rearrange("p (a b) -> p a b", a=4)
        t_z = memset(pool, wuv, 0.0, *so_far())
        t_wuv = [small_dma(pool, wuv[:, h, (h % 2) * DH:(h % 2) * DH + DH], A["dsa_w_uv"][0, h], t_z) for h in range(4)]
        ob_ = iq
        for g in range(2):
            bi, b, free = lin.take()
            t = mm_group(b[:, :], [(wuv[:, 2 * g + j, :], bq[:, 2 * g + j, :]) for j in range(2)], *t_wuv, t_b[3], free)
            t_ob = lin.free[bi] = copy(act, ob_[:, g, :], b[:, :], t)
        run_all(branch(1, A["w_br_b"][0], lambda k: ob_[:, k, :], t_ob))

        rows_ring.free = [so_far()] * 2
        run_all(ada(4, 12))
        gate = lambda i, m: modc[:, 24 * i + 16 + m:24 * i + 17 + m]
        t_hs = [None] * KC

        def to_residual(i):
            def evac(m, b, t):
                t_hs[m] = stt(hT[:, m, :], b, gate(i, m), hT[:, m, :], ALU.mult, ALU.add, t, t_mod[0])
                return t_hs[m]
            return evac

        run_all(linear(None, [(A["w_o"][0], lambda k: merged[:, k, :])], D, to_residual(0), *t_merged))
        att.bufs, att.free, att.n = banks[4:8], [so_far()] * 4, 0

        ffn_h, _ = area(0, FF // P, S)

        def mlp(w1, w2, x_tokens, evac2):
            stage()
            t_f = [None] * (FF // P)

            def evac1(m, b, t):
                t = fn(ffn_h[:, m, :], b, ACT.Relu, t)
                t_f[m] = tt(pool if m % 2 else dve, ffn_h[:, m, :], ffn_h[:, m, :], ffn_h[:, m, :], ALU.mult, t)
                return t

            run_all(linear(None, [(w1, u)], FF, evac1, *x_tokens))
            pe.wait(t_f[-1], t_f[-2])
            run_all(linear(None, [(w2[i * D:(i + 1) * D, :], lambda k, i=i: ffn_h[:, i * KC + k, :])
                                  for i in range(4)], D, evac2))

        t_u = modulated_norm(1, "norm_mlp", t_hs)
        mlp(A["w_ff1"][0], A["w_ff2"][0], t_u, to_residual(1))

        r = rms_stats(lambda k: hT[:, k, :], range(KC), D, 0, stat[:, 0, :], t_hs, *stat_free)
        for k in range(KC):
            t_hs[k] = stt(hT[:, k, :], hT[:, k, :], column("norm_final", k), stat[:, 0, :], ALU.mult, ALU.mult, r)
            stat_free[:] = [t_hs[k]]

        h = lambda k: hT[:, k, :]

        def to_deepnorm(m, b, t):
            t_hs[m] = stt(hT[:, m, :], hT[:, m, :], ALPHA, b, ALU.mult, ALU.add, t)
            return t_hs[m]

        def block_norm(i, j):
            c = (i * 3 + j) * 8
            t_hs[:] = layer_norm(h, list(t_hs), lambda k: column("ln_g_2", c + k), lambda k: column("ln_b_2", c + k), h)

        def silu_of(o, b, scratch, t, *tokens, half_bias=None):
            hb = 0.0 if half_bias is None else half_bias
            t1 = fn(scratch, b, ACT.Tanh, t, *tokens, bias=hb, scale=0.5)
            t2 = ts(dve, o, b, 0.5, ALU.mult, t1, s2=hb, op1=ALU.add)
            return stt(o, scratch, 1.0, o, ALU.add, ALU.mult, t1, t2), t2

        stage()
        w_even = A["even_w_in_2"][0]
        o = 0
        VALW = S + CONV_W - 1
        XW_ = S + SSM_CONV - 1
        val, o = area(o, KC, VALW)
        zT, o = area(o, KC, S)
        xbc, o = area(o, XBC_C, S)
        raw, o = area(o, 3, XW_)
        XP, o = area(o, SSM_HEADS, P)
        XW, o = area(o, SSM_HEADS, DH)
        ST, o = area(o, SSM_HEADS, P)
        BM, o = area(o, 2, P)
        CB, o = area(o, 2, P)
        E1, o = area(o, 4, P)
        DEC, o = area(o, 4, P)
        CE, o = area(o, 4, P)
        tmp4, o = area(o, 2, S)
        dts, o = area(o, 8, 64)
        DE, o = area(o, SSM_HEADS)
        dsk, o = area(o, KC)
        hb12, o = area(o, XBC_C)
        prm, o = area(o, 3, 16)
        dt_, adt, nacs, dte, sc1, sc2, sc3, sc4 = (dts[:, j, :] for j in range(8))
        conv = uT

        ev = so_far()
        t_p = [small_dma(act, prm[:, 0, :], A["even_dt_bias_2"].to_broadcast([P, 16])),
               small_dma(act, prm[:, 1, :], A["even_a_log_2"].to_broadcast([P, 16])),
               small_dma(act, prm[:, 2, :], A["even_d_skip_2"].to_broadcast([P, 16]))]
        t_wdt = small_dma(act, wsmall[:, :, :], w_even[:, EV_DT:EV_DT + 16].rearrange("(k p) n -> p k n", p=P), *ev)
        t_a = fn(prm[:, 1, :], prm[:, 1, :], ACT.Exp, *t_p)
        pd = prm[:, 2, :].rearrange("p (m two) -> p m two", two=2)
        t1 = copy(dve, dsk[0:DH, :], pd[0:DH, :, 0], *t_p)
        t_dsk = copy(dve, dsk[DH:P, :], pd[DH:P, :, 1], t1)
        t_hb = ts(dve, hb12, columns("even_ssm_conv_b_2", 0, XBC_C), 0.5, ALU.mult)
        t_pad = [memset(pool, val[:, :, 0:CONV_W - 1], 0.0), memset(pool, raw[:, :, 0:SSM_CONV - 1], 0.0),
                 memset(pool, XP, 0.0), memset(pool, ST, 0.0)]

        bi, b, free = lin.take()
        for c in range(NT):
            t = mm_group(b[:, c * 16:(c + 1) * 16],
                         [(h(k)[:, c * P:(c + 1) * P], wsmall[:, k, :]) for k in range(KC)], t_wdt, free, *t_hs)
        b4 = b[:, 0:64].rearrange("p (c h) -> p c h", c=NT)
        v4 = lambda a: a.rearrange("p (c h) -> p c h", c=NT)
        t = lin.free[bi] = tt(dve, v4(dt_), b4, prm[:, 0, :].unsqueeze(1).to_broadcast([P, NT, 16]), ALU.add, t, *t_p)

        def log1p_exp_minus(x, e, uu, ln, o, t):
            t1 = ts(dve, e, x, -1.0, ALU.mult, t)
            t1 = tt(dve, e, e, x, ALU.min, t1)
            t1 = fn(e, e, ACT.Exp, t1)
            t2 = ts(dve, uu, e, 1.0, ALU.add, t1)
            t3 = fn(ln, uu, ACT.Ln, t2)
            t1 = stt(e, uu, -1.0, e, ALU.add, ALU.subtract, t1, t2)
            t2 = recip(uu, uu, t2, t3, t1)
            t1 = tt(dve, e, e, uu, ALU.mult, t1, t2)
            return tt(dve, o, ln, e, ALU.subtract, t3, t1)

        t = log1p_exp_minus(dt_, sc1, sc2, sc3, sc4, t)
        t_dt = stt(dt_, dt_, 0.0, sc4, ALU.max, ALU.add, t)
        a_b = prm[:, 1, :].unsqueeze(1).to_broadcast([P, NT, 16])
        t = tt(dve, v4(adt), v4(dt_), a_b, ALU.mult, t_dt, t_a)
        t_adt = ts(dve, adt, adt, -1.0, ALU.mult, t)
        i, b, free = att.take()
        t = mm_group(b[:, 0:64], [(upper, adt)], t_adt, free)
        t = mm_group(b[:, 64:128], [(ones[:, :], adt)])
        t_n = ts(dve, nacs, b[:, 0:64], -1.0, ALU.mult, t)
        t = att.free[i] = tt(dve, dte, b[:, 64:128], nacs, ALU.add, t_n)
        t_dte = fn(dte, dte, ACT.Exp, t)

        raw_ring = Ring([raw[:, j, :] for j in range(3)])
        sil = Ring([tmp4[:, j, :] for j in range(2)])
        t_xbc = [None] * XBC_C

        def evac_xbc(m, b, t):
            i, r, f = raw_ring.take()
            te = copy(act, r[:, SSM_CONV - 1:], b, t, f, t_pad[1])
            wcol = lambda j: column("even_ssm_conv_w_2", j * XBC_C + m)
            o = xbc[:, m, :]
            tc = ts(dve, o, r[:, 0:S], wcol(0), ALU.mult, te)
            for j in range(1, SSM_CONV):
                tc = stt(o, r[:, j:j + S], wcol(j), o, ALU.mult, ALU.add, tc)
            raw_ring.free[i] = tc
            si, s, sf = sil.take()
            t1 = fn(s, o, ACT.Tanh, tc, sf, t_hb, bias=hb12[:, m:m + 1], scale=0.5)
            t2 = ts(dve, o, o, 0.5, ALU.mult, t1, t_hb, s2=hb12[:, m:m + 1], op1=ALU.add)
            t_xbc[m] = sil.free[si] = stt(o, s, 1.0, o, ALU.add, ALU.mult, t1, t2)
            return te

        def evac_z(m, b, t):
            si, s, sf = sil.take()
            sil.free[si], t2 = silu_of(zT[:, m, :], b, s, t, sf)
            return t2

        run_all(linear(None, [(w_even[:, EV_XBC:EV_XBC + XBC], h)], XBC, evac_xbc, *t_hs))

        t_conv = [None] * KC

        def conv_units():
            for c0 in range(0, D, 512):
                si, slot, t_w = load_weights(w_even[:, EV_VAL + c0:EV_VAL + c0 + 512], D, 512)
                sj, slot2, t_w2 = load_weights(w_even[:, EV_GATE + c0:EV_GATE + c0 + 512], D, 512)
                for j in range(4):
                    m = c0 // P + j
                    b1i, b1, f1 = lin.take()
                    t1 = mm_group(b1[:, :], [(slot2[:, k, j * P:(j + 1) * P], h(k)) for k in range(KC)], t_w2, f1)
                    gi, g, gf = gate_ring.take()
                    tg = lin.free[b1i] = fn(g, b1[:, :], ACT.Tanh, t1, gf, scale=0.5)
                    tg = ts(pool, g, g, 0.5, ALU.mult, tg, s2=0.5, op1=ALU.add)
                    yield
                    b2i, b2, f2 = lin.take()
                    t2 = mm_group(b2[:, :], [(slot[:, k, j * P:(j + 1) * P], h(k)) for k in range(KC)], t_w, f2)
                    if j == 3:
                        free_slot(si, t2)
                        free_slot(sj, t2)
                    t = tt(dve, val[:, m, CONV_W - 1:], b2[:, :], g, ALU.mult, t2, tg, t_pad[0])
                    lin.free[b2i] = gate_ring.free[gi] = t
                    o = conv[:, m, :]
                    t = ts(dve, o, val[:, m, 0:S], conv_tap(0, m), ALU.mult, t, s2=column("even_conv_b_2", m), op1=ALU.add)
                    for tap in range(1, CONV_W):
                        t = stt(o, val[:, m, tap:tap + S], conv_tap(tap, m), o, ALU.mult, ALU.add, t)
                        if tap == 15:
                            yield
                    t_conv[m] = t
                    yield

        def ssm_steps():
            pair = lambda a: a.rearrange("p (g two) d -> p g two d", two=2)
            t_y = None
            t_st = None
            for c in range(NT):
                cs = slice(c * P, (c + 1) * P)
                dtc = dt_[:, c * 16:(c + 1) * 16].rearrange("p (g two) -> p g two", two=2)
                t_xp = []
                for half in range(2):
                    i, b, free = att.take()
                    for j in range(4):
                        t = turn(b[:, j * P:(j + 1) * P], xbc[:, half * 4 + j, cs], free, *t_xbc, t_y, signal=j == 3)
                    bb = b[:, :].rearrange("p (g two d) -> p g two d", two=2, d=DH)
                    for par in range(2):
                        t2 = tt(dve, pair(XP)[:, half * 4:half * 4 + 4, par, par * DH:(par + 1) * DH], bb[:, :, par, :],
                                dtc[:, half * 4:half * 4 + 4, par].unsqueeze(2).to_broadcast([P, 4, DH]), ALU.mult,
                                t, t_dt, t_pad[2], t_y)
                        t_xp.append(t2)
                    att.free[i] = t2
                t_xw = None
                dtec = dte[:, c * 16:(c + 1) * 16].rearrange("p (g two) -> p g two", two=2)
                for par in range(2):
                    t_xw = tt(pool, pair(XW)[:, :, par, :], pair(XP)[:, :, par, par * DH:(par + 1) * DH],
                              dtec[:, :, par].unsqueeze(2).to_broadcast([P, 8, DH]), ALU.mult, *t_xp, t_dte, t_st)
                i, b, free = att.take()
                for g in range(2):
                    t = turn(b[:, g * P:(g + 1) * P], xbc[:, 8 + g, cs], free, signal=False)
                for g in range(2):
                    t = mm(b[:, 256 + g * P:256 + (g + 1) * P], xbc[:, 8 + g, cs], xbc[:, 10 + g, cs], True, True,
                           signal=g == 1)
                t_bm = copy(act, BM, b[:, 0:256].rearrange("p (a b) -> p a b", a=2), t, t_st)
                t_cb = att.free[i] = copy(act, CB, b[:, 256:512].rearrange("p (a b) -> p a b", a=2), t, dve.now)
                yield
                for q4 in range(4):
                    g = q4 // 2
                    i, b, free = att.take()
                    for j in range(4):
                        hd = c * 16 + q4 * 4 + j
                        t = mm(b[:, j * P:(j + 1) * P], adt[:, hd:hd + 1].to_broadcast([P, P]), upper, True, True,
                               free, t_adt, signal=j == 3)
                    bb = b[:, :].rearrange("p (a b) -> p a b", a=4)
                    t_e = fn(E1, bb, ACT.Exp, t, pool.now, t_y, t_st)
                    t_seg = att.free[i] = tt(dve, DEC, bb, seg_mask.unsqueeze(1).to_broadcast([P, 4, P]), ALU.add, t, t_y, t_e)
                    t_de = copy(dve, DE[:, q4 * 4:q4 * 4 + 4], E1[:, :, P - 1], t_e, t_st)
                    for j in range(4):
                        hd = c * 16 + q4 * 4 + j
                        t = fn(DEC[:, j, :], DEC[:, j, :], ACT.Exp, t_seg, t_n, bias=nacs[:, hd:hd + 1])
                    t_g = tt(dve, DEC, DEC, CB[:, g, :].unsqueeze(1).to_broadcast([P, 4, P]), ALU.mult, t, t_cb)
                    t_ce = tt(pool, CE, E1, xbc[:, 10 + g, cs].unsqueeze(1).to_broadcast([P, 4, P]), ALU.mult, t_e, t_y)
                    yield
                    i, b, free = att.take()
                    for pr_ in range(2):
                        ops = []
                        for par in range(2):
                            hh = q4 * 4 + pr_ * 2 + par
                            ops.append((XP[:, hh, :], DEC[:, pr_ * 2 + par, :]))
                        for par in range(2):
                            hh = q4 * 4 + pr_ * 2 + par
                            ops.append((ST[:, hh, :], CE[:, pr_ * 2 + par, :]))
                        t = mm_group(b[:, pr_ * P:(pr_ + 1) * P], ops, free, t_g, t_ce, t_st, *t_xp, t_pad[3])
                    for pr_ in range(2):
                        m = q4 * 2 + pr_
                        t_y = stt(xbc[:, m, cs], xbc[:, m, cs], dsk[:, m:m + 1], b[:, pr_ * P:(pr_ + 1) * P],
                                  ALU.mult, ALU.add, t, t_dsk)
                    att.free[i] = t_y
                for g in range(2):
                    i, b, free = att.take()
                    t = mm_group(b[:, :], [(BM[:, g, :], XW[:, g * 8:(g + 1) * 8, :].rearrange("p a b -> p (a b)"))],
                                 t_bm, t_xw, free)
                    bb = b[:, :].rearrange("p (g two d) -> p g two d", two=2, d=DH)
                    de = DE.rearrange("p (g two) -> p g two", two=2)
                    for par in range(2):
                        s_ = pair(ST)[:, g * 4:(g + 1) * 4, par, par * DH:(par + 1) * DH]
                        t2 = tt(dve, s_, s_, de[:, g * 4:(g + 1) * 4, par].unsqueeze(2).to_broadcast([P, 4, DH]),
                                ALU.mult, t_de, t, t_y)
                        t_st = tt(dve, s_, s_, bb[:, :, par, :], ALU.add, t2)
                    att.free[i] = t_st
            t_yend[0] = t_y

        t_yend = [None]
        cu = conv_units()
        for _ in ssm_steps():
            step(cu, 2)
        run_all(cu)
        run_all(linear(None, [(w_even[:, EV_Z:EV_Z + D], h)], D, evac_z))

        ty = []
        for m in range(KC):
            ty.append(tt(dve, xbc[:, m, :], xbc[:, m, :], zT[:, m, :], ALU.mult, t_yend[0], dve.now))
        t_y2 = [None] * KC
        for g in range(2):
            r = rms_stats(lambda k: xbc[:, k, :], range(g * 4, g * 4 + 4), 4 * P, 1, stat[:, 1 + g, :], ty, *stat_free)
            for m in range(g * 4, g * 4 + 4):
                t_y2[m] = stt(xbc[:, m, :], xbc[:, m, :], column("even_ssm_norm_g_2", m), stat[:, 1 + g, :],
                              ALU.mult, ALU.mult, r)
        stat_free[:] = [t_y2[-1]]

        sil2 = Ring([tmp4[:, j, :] for j in range(2)])
        sil2.free = [dve.now] * 2

        def ln_silu(k, s, t):
            bcol = column("even_conv_ln_b_2", k)
            i, w, f = sil2.take()
            t = fn(s, s, ACT.Identity, t, bias=bcol)
            t1 = fn(w, s, ACT.Tanh, t, f, scale=0.5)
            t2 = stt(s, w, 1.0, s, ALU.add, ALU.mult, t1)
            sil2.free[i] = t2
            return ts(dve, s, s, 0.5, ALU.mult, t2)

        tu = layer_norm(lambda k: conv[:, k, :], t_conv, lambda k: column("even_conv_ln_g_2", k), None, None, func=ln_silu)
        w_out = A["even_w_out_2"][0]
        run_all(linear(None, [(w_out[0:D, :], lambda k: conv[:, k, :]), (w_out[D:2 * D, :], lambda k: xbc[:, k, :])],
                       D, to_deepnorm, *tu, *t_y2))
        block_norm(0, 0)

        def cross_attention(li):
            stage()
            o = 0
            qT, o = area(o, KC, S)
            kT, o = area(o, KC, MEM)
            vv, o = area(o, 2, D)
            memT, o = area(o, KC, MEM)
            mem, o = area(o, 2, D)
            ws2, o = area(o, 4, MEM)
            PT2, o = area(o, 2, 2, S)
            t_m = small_dma(act, mem, A["mem_2"][0].rearrange("(t p) n -> p t n", p=P), *so_far())
            for k in range(0, KC, 2):
                i, b, free = att.take()
                for kk in range(2):
                    for t_ in range(2):
                        t = turn(b[:, kk * MEM + t_ * P:kk * MEM + (t_ + 1) * P], mem[:, t_, (k + kk) * P:(k + kk + 1) * P],
                                 t_m, free, signal=kk + t_ == 2)
                t_mt = att.free[i] = copy(act, memT[:, k:k + 2, :], b[:, :].rearrange("p (a b) -> p a b", a=2), t)
            for c0 in range(0, D, 512):
                si, slot, t_w = load_weights(A["xa_w_k_2"][li][:, c0:c0 + 512], D, 512)
                for j in range(4):
                    bi, b, free = lin.take()
                    t = mm_group(b[:, 0:MEM], [(slot[:, k, j * P:(j + 1) * P], memT[:, k, :]) for k in range(KC)],
                                 t_w, free, t_mt)
                    lin.free[bi] = copy(act, kT[:, c0 // P + j, :], b[:, 0:MEM], t)
                free_slot(si, t)
            for c0 in range(0, D, 512):
                def evac_v(t, b, tok, c0=c0):
                    return copy(act, vv[:, t, c0:c0 + 512], b[:, :], tok)
                run_all(linear_tokens(lambda k: memT[:, k, :], A["xa_w_v_2"][li][:, c0:c0 + 512], evac_v, t_mt))
            run_all(linear(None, [(A["xa_w_q_2"][li], h)], D, to(qT), *t_hs))
            t_q = act.now
            ring = Ring([ws2[:, j, :] for j in range(4)])
            ptr = Ring([PT2[:, j, :, :] for j in range(2)])
            oT = uT
            t_o = [None] * KC
            tiles = [(hd, qt) for hd in range(XA_HEADS) for qt in range(NT)]
            state = {}

            def first_half(hd, qt):
                i, b, free = att.take()
                t = mm_group(b[:, 0:MEM], [(qT[:, 2 * hd + j, qt * P:(qt + 1) * P], kT[:, 2 * hd + j, :]) for j in range(2)],
                             t_q, free)
                wi, w, wf = ring.take()
                si, st, sf = st_ring.take()
                t = dve.do(lambda e: e.tensor_reduce(st[:, 0:1], b[:, 0:MEM], AX.X, ALU.max, negate=True), t, sf)
                t = ts(dve, st[:, 1:2], st[:, 0:1], 256 ** -0.5, ALU.mult, t)
                t = att.free[i] = fn(w, b[:, 0:MEM], ACT.Exp, t, wf, bias=st[:, 1:2], scale=256 ** -0.5, accum=st[:, 2:3])
                t = recip(st[:, 3:4], st[:, 2:3], t)
                t = st_ring.free[si] = ts(dve, w, w, st[:, 3:4], ALU.mult, t)
                state[hd, qt] = (wi, w, t)

            def second_half(hd, qt):
                wi, w, tw = state.pop((hd, qt))
                if qt == 0:
                    state["pt"] = ptr.take()
                pi, pt, pf = state["pt"]
                i, b, free = att.take()
                for kt in range(2):
                    t = turn(b[:, kt * P:(kt + 1) * P], w[:, kt * P:(kt + 1) * P], tw, free, signal=kt == 1)
                ring.free[wi] = t
                t = att.free[i] = copy(act, pt[:, :, qt * P:(qt + 1) * P],
                                       b[:, 0:MEM].rearrange("p (a b) -> p a b", a=2), t, pf)
                if qt == NT - 1:
                    for e_ in range(2):
                        bi, b, free = lin.take()
                        m = 2 * hd + e_
                        t2 = mm_group(b[:, :], [(vv[:, kt, m * P:(m + 1) * P], pt[:, kt, :]) for kt in range(2)], t, free)
                        t_o[m] = lin.free[bi] = copy(dve, oT[:, m, :], b[:, :], t2)
                    ptr.free[pi] = t2

            first_half(*tiles[0])
            for n in range(1, len(tiles)):
                first_half(*tiles[n])
                second_half(*tiles[n - 1])
            second_half(*tiles[-1])
            run_all(linear(None, [(A["xa_w_o_2"][li], lambda k: oT[:, k, :])], D, to_deepnorm, *t_o))

        def block_mlp(li):
            run_tokens = list(t_hs)
            stage()
            t_f = [None] * (FF // P)

            def evac1(m, b, t):
                t = fn(ffn_h[:, m, :], b, ACT.Relu, t)
                t_f[m] = tt(pool if m % 2 else dve, ffn_h[:, m, :], ffn_h[:, m, :], ffn_h[:, m, :], ALU.mult, t)
                return t

            run_all(linear(None, [(A["mlp_w1_2"][li], h)], FF, evac1, *run_tokens))
            pe.wait(t_f[-1], t_f[-2])
            w2 = A["mlp_w2_2"][li]
            run_all(linear(None, [(w2[i * D:(i + 1) * D, :], lambda k, i=i: ffn_h[:, i * KC + k, :])
                                  for i in range(4)], D, to_deepnorm))

        cross_attention(0)
        block_norm(0, 1)
        block_mlp(0)
        block_norm(0, 2)

        stage()
        w_odd = A["odd_w_in_2"][0]
        o = 0
        q_, o = area(o, 4, S)
        k_, o = area(o, 4, S)
        gv, o = area(o, NT, D)
        go, o = area(o, KC, S)
        kend, o = area(o, 4, S)
        kt_, o = area(o, 4, S)
        lg, o = area(o, S)
        bcs, o = area(o, 4, S)
        sca, o = area(o, 3, S)
        SG, o = area(o, 2, GLA_HEADS, 256)
        low, o = area(o, S)
        wg2, o = area(o, 512)
        KE, o = area(o, NT, 512)
        dec, o = area(o, 4, 8)
        ATT = kend
        gT = uT
        ev = so_far()
        t_wl = small_dma(act, wsmall[:, :, :], w_odd[:, OD_LOW:OD_LOW + GLA_RANK].rearrange("(k p) n -> p k n", p=P), *ev)
        t_wg = small_dma(act, wg2[0:GLA_RANK, :], A["odd_w_gate2_2"][0], *ev)
        bi, b, free = lin.take()
        t = mm_group(b[0:GLA_RANK, :], [(wsmall[:, k, :], h(k)) for k in range(KC)], t_wl, free, *t_hs)
        t_low = lin.free[bi] = copy(act, low[0:GLA_RANK, :], b[0:GLA_RANK, :], t)

        t_qk = {}

        def evac_q(m, b, t):
            t_qk["q", m] = copy(act, q_[:, m, :], b, t)
            return t_qk["q", m]

        def evac_k(m, b, t):
            t_qk["k", m] = copy(act, k_[:, m, :], b, t)
            return t_qk["k", m]

        odd_fill = chain(linear(None, [(w_odd[:, OD_Q:OD_Q + 512], h)], 512, evac_q, *t_hs),
                         linear(None, [(w_odd[:, OD_K:OD_K + 512], h)], 512, evac_k, *t_hs))
        t_b4 = [None] * 4
        for hd in range(4):
            i, b, free = att.take()
            t = mm_group(b[:, :], [(wg2[0:GLA_RANK, hd * P:(hd + 1) * P], low[0:GLA_RANK, :])], t_wg, t_low, free)
            x_ = lg[:, :]
            t = att.free[i] = ts(dve, x_, b[:, :], column("odd_b_gate_2", hd), ALU.add, t, t_b4[hd - 1] if hd else None)
            t = log1p_exp_minus(x_, sca[:, 0, :], sca[:, 1, :], sca[:, 2, :], sca[:, 2, :], t)
            t = stt(x_, x_, 0.0, sca[:, 2, :], ALU.min, ALU.subtract, t)
            t = ts(dve, x_, x_, 1.0 / 16.0, ALU.mult, t)
            t_b4[hd] = dve.do(lambda e, hd=hd: e.tensor_tensor_scan(bcs[:, hd, :], again, lg[:, :], 0.0, ALU.mult, ALU.add), t)
            step(odd_fill, 2)
        run_all(odd_fill)
        t_dec = copy(dve, dec, bcs.rearrange("p h (n c) -> p h n c", c=GLA_C)[:, :, :, GLA_C - 1], *t_b4)
        t_qt = [None] * 4
        t_kt = [None] * 4
        t_ke = [None] * 4
        vfill = chain(*[linear_tokens(h, w_odd[:, OD_V + c0:OD_V + c0 + 512],
                                      (lambda c0: lambda t, b, tok: copy(act, gv[:, t, c0:c0 + 512], b[:, :], tok))(c0))
                        for c0 in (0, 512)])
        for hd in range(4):
            s0, s1, s2 = (sca[:, j, :] for j in range(3))
            bh = bcs[:, hd, :]
            t0 = fn(s0, bh, ACT.Exp, *t_b4, dve.now)
            t_qt[hd] = stt(q_[:, hd, :], q_[:, hd, :], P ** -0.5, s0, ALU.mult, ALU.mult, t0, t_qk["q", hd])
            t0 = fn(s1, bh, ACT.Exp, scale=-1.0)
            t_kt[hd] = tt(dve, kt_[:, hd, :], k_[:, hd, :], s1, ALU.mult, t0, t_qk["k", hd])
            t0 = tt(dve, s2.rearrange("p (n c) -> p n c", c=GLA_C), dec[:, hd, :].unsqueeze(2).to_broadcast([P, 8, GLA_C]),
                    bh.rearrange("p (n c) -> p n c", c=GLA_C), ALU.subtract, t_dec, act.now)
            t0 = fn(s2, s2, ACT.Exp, t0)
            t_ke[hd] = tt(dve, kend[:, hd, :], k_[:, hd, :], s2, ALU.mult, t0)
            step(vfill, 2)
        t_dec = fn(dec, dec, ACT.Exp, t_dec, *t_ke)
        run_all(vfill)
        t_v = act.now
        t_g = {}

        def evac_go(m, b, t):
            t_g[m], t2 = silu_of(go[:, m, :], b, sca[:, m % 2, :], t, dve.now)
            return t2

        gfill = linear(None, [(w_odd[:, OD_G:OD_G + D], h)], D, evac_go)
        for tt_ in range(NT):
            i, b, free = att.take()
            for hd in range(4):
                t = turn(b[:, hd * P:(hd + 1) * P], kend[:, hd, tt_ * P:(tt_ + 1) * P], free, t_ke[hd], signal=hd == 3)
            t_KE = att.free[i] = copy(act, KE[:, tt_, :], b[:, :], t)
        t_at = [None] * NT
        for tt_ in range(NT):
            ts_ = slice(tt_ * P, (tt_ + 1) * P)
            i, b, free = att.take()
            for hd in range(4):
                t = mm(b[:, hd * P:(hd + 1) * P], kt_[:, hd, ts_], q_[:, hd, ts_], True, True,
                       t_kt[hd], t_qt[hd], free, signal=hd == 3)
            a4 = ATT[:, tt_, :].rearrange("p (a b) -> p a b", a=4)
            t = att.free[i] = copy(act, ATT[:, tt_, :], b[:, :], t, t_KE)
            t = pool.do(lambda e, a4=a4: e.affine_select(out=a4, in_=a4, compare_op=ALU.is_ge, fill=0.0, base=0,
                                                         pattern=[[0, 4], [1, P]], channel_multiplier=-1), t)
            a5 = a4[:, :, GLA_C:P]
            t_at[tt_] = pool.do(lambda e, a5=a5: e.affine_select(out=a5, in_=a5, compare_op=ALU.is_ge, fill=0.0, base=-GLA_C,
                                                                 pattern=[[0, 4], [0, GLA_C]], channel_multiplier=1), t)
            step(gfill)
        t_s = memset(dve, SG[:, 0, :, :], 0.0)
        t_og = [None] * NT
        rd = None
        t_cur = [t_s] * 4
        for tt_ in range(NT):
            ts_ = slice(tt_ * P, (tt_ + 1) * P)
            outs = [att.take(), att.take()]
            for half in range(2):
                n = 2 * tt_ + half
                hs = slice(half * GLA_C, (half + 1) * GLA_C)
                for e_ in range(8):
                    hd, vh = e_ // 2, e_ % 2
                    i, b, free = outs[e_ // 4]
                    dst = b[:, (e_ % 4) * P + half * GLA_C:(e_ % 4) * P + (half + 1) * GLA_C]
                    t = mm_group(dst, [
                        (gv[:, tt_, hd * 256 + vh * P:hd * 256 + (vh + 1) * P], ATT[:, tt_, hd * P + half * GLA_C:hd * P + (half + 1) * GLA_C]),
                        (SG[:, n % 2, hd, vh * P:(vh + 1) * P], q_[:, hd, tt_ * P + half * GLA_C:tt_ * P + (half + 1) * GLA_C]),
                    ], t_v, t_at[tt_], free, t_cur[hd])
                rd = t
                if n < 7:
                    for pr_ in range(2):
                        bi, b, free = lin.take()
                        for j in range(2):
                            hd = pr_ * 2 + j
                            t = mm(b[:, j * 256:(j + 1) * 256], KE[hs, tt_, hd * P:(hd + 1) * P],
                                   gv[hs, tt_, hd * 256:(hd + 1) * 256], True, True, free, t_KE, signal=j == 1)
                        for j in range(2):
                            hd = pr_ * 2 + j
                            t_cur[hd] = stt(SG[:, (n + 1) % 2, hd, :], SG[:, n % 2, hd, :], dec[:, hd, n:n + 1],
                                            b[:, j * 256:(j + 1) * 256], ALU.mult, ALU.add, t, t_dec, rd, t_cur[hd])
                        lin.free[bi] = t_cur[hd]
                step(gfill)
            for z in range(2):
                i, b, free = outs[z]
                t_og[tt_] = att.free[i] = copy(dve, gT[:, 4 * z:4 * z + 4, ts_], b[:, :].rearrange("p (a b) -> p a b", a=4), rd)
        run_all(gfill)
        t_fin = [None] * KC
        for hd in range(4):
            r = rms_stats(lambda k: gT[:, k, :], [2 * hd, 2 * hd + 1], 256, 1, stat[:, hd % 2, :], [t_og[-1]] * KC, *stat_free)
            for j in range(2):
                m = 2 * hd + j
                t = stt(gT[:, m, :], gT[:, m, :], column("odd_head_norm_g_2", j), stat[:, hd % 2, :], ALU.mult, ALU.mult, r)
                stat_free[:] = [t]
                t_fin[m] = tt(dve, gT[:, m, :], gT[:, m, :], go[:, m, :], ALU.mult, t, t_g[m])
        run_all(linear(None, [(A["odd_w_out_2"][0], lambda k: gT[:, k, :])], D, to_deepnorm, *t_fin))
        block_norm(1, 0)
        cross_attention(1)
        block_norm(1, 1)
        block_mlp(1)
        block_norm(1, 2)

        stage()
        ot, _ = area(0, NT, D)
        outs = []
        for t_ in range(NT):
            for half in range(2):
                i, b, free = att.take()
                for j in range(4):
                    t = turn(b[:, j * P:(j + 1) * P], hT[:, half * 4 + j, t_ * P:(t_ + 1) * P], *t_hs, free, signal=j == 3)
                t_o = att.free[i] = copy(act if half else dve, ot[:, t_, half * 512:(half + 1) * 512], b[:, :], t)
                outs.append(small_dma(sp, out[0, t_ * P:(t_ + 1) * P, half * 512:(half + 1) * 512],
                                      ot[:, t_, half * 512:(half + 1) * 512], t_o))
        sp.wait(*outs, t_sd)

        with nc.Block() as block:
            @block.sync
            def _(e):
                sp.run(e)

            @block.scalar
            def _(e):
                act.run(e)

            @block.vector
            def _(e):
                dve.run(e)

            @block.gpsimd
            def _(e):
                pool.run(e)

            @block.tensor
            def _(e):
                pe.run(e)


_INS = ['x', 'c', 'rel_bias', 'ada_w', 'ada_b', 'norm_mix', 'w_in', 'gate_b', 'diff_lambda', 'diff_subln',
        'dsa_kv_norm', 'dsa_w_uv', 'w_br_a', 'w_br_b', 'w_br_c', 'w_o', 'norm_mlp', 'w_ff1', 'w_ff2', 'norm_final',
        'mem_2', 'even_w_in_2', 'even_conv_w_2', 'even_conv_b_2', 'even_conv_ln_g_2', 'even_conv_ln_b_2',
        'even_ssm_conv_w_2', 'even_ssm_conv_b_2', 'even_dt_bias_2', 'even_a_log_2', 'even_d_skip_2',
        'even_ssm_norm_g_2', 'even_w_out_2', 'odd_w_in_2', 'odd_w_gate2_2', 'odd_b_gate_2', 'odd_head_norm_g_2',
        'odd_w_out_2', 'xa_w_q_2', 'xa_w_k_2', 'xa_w_v_2', 'xa_w_o_2', 'mlp_w1_2', 'mlp_w2_2', 'ln_g_2', 'ln_b_2']


def kernel(**inputs):
    import concourse.bacc as bacc
    from concourse.bass_utils import run_bass_kernel_spmd

    nc = bacc.Bacc("TRN2", target_bir_lowering=False, num_devices=1)
    square, onehot = shape_constants()
    arrays, A = {}, {}
    for name in _INS:
        arrays[f"in_{name}"] = np.ascontiguousarray(inputs[name])
    arrays["in_c_square"], arrays["in_c_onehot"] = square, onehot
    for key, a in arrays.items():
        A[key[3:]] = nc.dram_tensor(key, a.shape, mybir.dt.from_np(a.dtype), kind="ExternalInput").ap()
    A["strip"] = nc.dram_tensor("strip", (12, 640), F32, kind="Internal").ap()
    out = nc.dram_tensor("out", (1, S, D), F32, kind="ExternalOutput").ap()
    program(nc, A, out)
    r = run_bass_kernel_spmd(nc, [arrays], core_ids=[0])
    return r.results[0]["out"]
```

```python
import math
from contextlib import ExitStack

import numpy as np

import concourse.bass as bass
from concourse import mybir

F32 = mybir.dt.float32
F32R = mybir.dt.float32r
ALU = mybir.AluOpType
ACT = mybir.ActivationFunctionType
AX = mybir.AxisListType

P = 128
D = 1024
S = 512
KC = D // P
NT = S // P
NEG = -1.0e30
TAKEN = -3.0e38

HEADS_A = HEADS_B = HEADS_C = 4
DH = 64
IDX_HEADS = 8
IDX_DIM = 32
BUCKETS = 32
TOPK = min(256, S // 4)
FF = 4 * D
LAM_INIT = 0.8 - 0.6 * math.exp(0.0)

COL_AQ, COL_AK, COL_AV, COL_BQ = 0, 512, 1024, 1536
COL_BKV = 2048
COL_IQ = COL_BKV + 128
COL_IK = COL_IQ + 256
COL_IW = COL_IK + 32
COL_CQ = COL_IW + 8
COL_CK = COL_CQ + 256
COL_CV = COL_CK + 256
COL_G = COL_CV + 256

ALPHA = 4 ** 0.25
CONV_W = 31
SSM_CONV = 4
SSM_HEADS = 16
XBC = D + 2 * 2 * 128
XBC_C = XBC // P
EV_VAL, EV_GATE, EV_Z, EV_XBC, EV_DT = 0, D, 2 * D, 3 * D, 3 * D + XBC
GLA_HEADS = 4
GLA_C = 64
OD_Q, OD_K, OD_V, OD_G, OD_LOW = 0, 512, 1024, 2048, 3072
GLA_RANK = 16
MEM = 256
XA_HEADS = 4
WC = 128
RAW_SLOTS = 5
HIGH_SLOTS = 3
LOAD_AHEAD = RAW_SLOTS - 1
SPLIT_AHEAD = HIGH_SLOTS - 1
ARENA = 25728


def t5_bucket(n):
    n = np.maximum(n, 0)
    nf = np.maximum(n, 1).astype(np.float32)
    half = BUCKETS // 2
    large = half + (np.log(nf / np.float32(half)) / np.float32(math.log(128 / half)) * np.float32(half)).astype(np.int32)
    return np.where(n < half, n, np.minimum(large, BUCKETS - 1))


def shape_constants():
    i = np.arange(P)
    ident = np.eye(P, dtype=np.float32)
    upper = (i[:, None] <= i[None, :]).astype(np.float32)
    seg_mask = np.where(i[:, None] <= i[None, :], 0.0, NEG).astype(np.float32)
    again = np.tile((np.arange(S) % GLA_C != 0).astype(np.float32), (P, 1))
    causal = np.zeros((P, S), np.float32)
    causal[:, S - P:] = np.where(i[:, None] >= i[None, :], 0.0, NEG)
    square = np.concatenate([ident, upper, seg_mask, again, causal, ident[::-1]], axis=1)
    width = 640
    dist = (S - 1) - np.arange(width)
    onehot = np.zeros((BUCKETS + 1, width), np.float32)
    bucket = t5_bucket(dist)
    for m in range(width):
        onehot[bucket[m], m] = 1.0
    onehot[BUCKETS] = np.where(dist < 0, NEG, 0.0)
    return np.ascontiguousarray(square), onehot


class Queue:

    def __init__(self, sem):
        self.sem, self.count, self.jobs, self.waited = sem, 0, [], {}

    def wait(self, *tokens):
        for t in tokens:
            if t is None:
                continue
            if isinstance(t, list):
                self.wait(*t)
                continue
            sem, value = t
            if self.waited.get(id(sem), 0) < value:
                self.waited[id(sem)] = value
                self.jobs.append((sem, value, None))

    def do(self, make, *tokens, signal=True):
        self.wait(*tokens)
        if signal:
            self.count += 1
        self.jobs.append((self.sem if signal else None, 1, make))
        return (self.sem, self.count)

    def dma(self, sem, make, *tokens):
        self.wait(*tokens)
        sem.count += 16
        self.jobs.append((sem.sem, 16, make))
        return (sem.sem, sem.count)

    @property
    def now(self):
        return (self.sem, self.count) if self.count else None

    def run(self, eng):
        for sem, value, make in self.jobs:
            if make is None:
                eng.wait_ge(sem, value)
            elif sem is None:
                make(eng)
            else:
                make(eng).then_inc(sem, value)


class DmaCount:
    def __init__(self, sem):
        self.sem, self.count = sem, 0


class Ring:

    def __init__(self, bufs):
        self.bufs, self.free, self.n = bufs, [None] * len(bufs), 0

    def take(self):
        i = self.n % len(self.bufs)
        self.n += 1
        return i, self.bufs[i], self.free[i]


def program(nc, A, out, schedule):
    ctx = ExitStack()
    with ctx:
        def sb(name, shape):
            return ctx.enter_context(nc.sbuf_tensor(name, shape, F32))

        def semaphore(name):
            return ctx.enter_context(nc.semaphore(name))

        pe, act, dve, pool, sp = (Queue(semaphore("s_" + n)) for n in ("pe", "act", "dve", "pool", "sp"))

        def so_far():
            return [q.now for q in (pe, act, dve, pool)]

        def stage():
            t = so_far()
            for q in (act, dve, pool):
                q.wait(*t)

        hT = sb("hT", [P, KC, S])
        def sb_r(name, shape):
            return ctx.enter_context(nc.sbuf_tensor(name, shape, F32R))

        XH = sb_r("XH", [P, KC, S])
        XL = sb_r("XL", [P, KC, S])
        high_slots = [sb_r(f"wh{i}", [P, KC, WC]) for i in range(HIGH_SLOTS)]
        adat = sb("adat", [P, 2, P])

        def two_views(name, words):
            start = -(-nc.sbuf_base // 32) * 32
            sb(name, [P, words + 8])
            return (nc.alloc_sbuf_tensor_at(name + "_f", [P, words], F32, offset=start),
                    nc.alloc_sbuf_tensor_at(name + "_r", [P, words], F32R, offset=start))

        arena, arena_r = two_views("arena", ARENA)
        raw_slots = [two_views(f"w{i}", KC * WC) for i in range(RAW_SLOTS)]
        const = sb("const", [P, 4 * P + 2 * S])
        ones = sb("ones", [P, P])
        vec = sb("vec", [P, 6, P])
        wsmall = sb("wsmall", [P, KC, 16])
        stat = sb("stat", [P, 3, S])
        sq = sb("sq", [P, 2, S])
        eps_t = sb("eps", [P, 4])
        lamb = sb("lamb", [P, 3 * P])
        modc = sb("modc", [P, 7 * KC])
        soft = sb("soft", [P, 64])
        gates = sb("gates", [P, 2, S])[:, :, :]

        ident = const[:, 0:P]
        upper = const[:, P:2 * P]
        seg_mask = const[:, 2 * P:3 * P]
        again = const[:, 3 * P:3 * P + S]
        causal = const[:, 3 * P + S:3 * P + 2 * S]
        flip = const[:, 3 * P + 2 * S:4 * P + 2 * S]

        def area(off, *shape, r=False):
            n = int(np.prod(shape))
            assert off + n <= ARENA, (off, shape)
            v = (arena_r if r else arena)[:, off:off + n]
            if len(shape) == 2:
                v = v.rearrange("p (a b) -> p a b", a=shape[0])
            if len(shape) == 3:
                v = v.rearrange("p (a b c) -> p a b c", a=shape[0], b=shape[1])
            return v, off + n

        banks = [ctx.enter_context(nc.psum_tensor(f"ps{i}", [P, 512], F32)) for i in range(8)]
        lin = Ring(banks[0:4])
        att = Ring(banks[4:8])

        raw_sem = [DmaCount(semaphore(f"s_w{i}")) for i in range(RAW_SLOTS)]
        raw_free = [None] * RAW_SLOTS
        high_free = [None] * HIGH_SLOTS
        noted, loaded, split_done = [], [], []
        tensors = {a.tensor.name: a.tensor for a in A.values()}

        def view(a, kc, cols):
            return a[:, 0:kc * cols].rearrange("p (k c) -> p k c", k=kc)

        def load_unit(n):
            dram = [bass.AP(tensors[name], offset, ap) for name, offset, ap in schedule[n][0]]
            i = n % RAW_SLOTS
            kc, cols = dram[0].shape[0] // P, sum(d.shape[1] for d in dram)
            c = 0
            for d in dram:
                dst = view(raw_slots[i][0], kc, cols)[:, :, c:c + d.shape[1]]
                src = d.rearrange("(k p) n -> p k n", p=P)
                t = sp.dma(raw_sem[i], lambda e, dst=dst, src=src: e.dma_start(dst, src), raw_free[i])
                c += d.shape[1]
            loaded.append((i, kc, cols, t))

        def split_unit(n):
            i, kc, cols, t = loaded[n]
            if not schedule[n][1]:
                split_done.append(None)
                return
            j = sum(1 for x in split_done if x) % HIGH_SLOTS
            hi = high_slots[j][:, :, :].rearrange("p k c -> p (k c)")[:, 0:kc * cols]
            t_h = act.do(lambda e: e.activation(hi, raw_slots[i][0][:, 0:kc * cols], ACT.Copy), t, high_free[j])
            t_l = dve.do(lambda e: e.tensor_tensor(raw_slots[i][1][:, 0:kc * cols], raw_slots[i][0][:, 0:kc * cols],
                                                   hi.bitcast(F32), ALU.subtract), t, t_h)
            split_done.append((j, [t_h, t_l]))

        def unit(*dram, split=True):
            n = len(noted)
            noted.append(([(d.tensor.name, d.offset, [list(x) for x in d.ap]) for d in dram], split))
            if schedule is None:
                kc, cols = dram[0].shape[0] // P, sum(d.shape[1] for d in dram)
                if not split:
                    return (lambda t: None), view(raw_slots[0][0], kc, cols), None
                return (lambda t: None), view(high_slots[0][:, :, :].rearrange("p k c -> p (k c)"), kc, cols), \
                    view(raw_slots[0][1], kc, cols), None
            while len(loaded) < min(n + LOAD_AHEAD + 1, len(schedule)):
                load_unit(len(loaded))
            while len(split_done) < min(n + SPLIT_AHEAD + 1, len(schedule)):
                split_unit(len(split_done))
            i, kc, cols, t = loaded[n]
            if not split:
                def free_raw(t):
                    raw_free[i] = t
                return free_raw, view(raw_slots[i][0], kc, cols), t
            j, t = split_done[n]

            def free_both(t):
                raw_free[i] = high_free[j] = t
            return free_both, view(high_slots[j][:, :, :].rearrange("p k c -> p (k c)"), kc, cols), \
                view(raw_slots[i][1], kc, cols), t

        n_small = [0]

        def small_dma(q, dst, src, *tokens):
            n_small[0] += 1
            c = DmaCount(semaphore(f"s_d{n_small[0]}"))
            return q.dma(c, lambda e: e.dma_start(dst, src), *tokens)

        def mm(o, l, r, start, stop, *tokens, signal=False):
            return pe.do(lambda e: e.matmul(o, l, r, start=start, stop=stop), *tokens, signal=signal)

        def mm_group(o, pairs, *tokens):
            t = None
            for n, (l, r) in enumerate(pairs):
                last = n == len(pairs) - 1
                t = mm(o, l, r, n == 0, last, *(tokens if n == 0 else ()), signal=last)
            return t

        def turn(o, i, *tokens, signal=True):
            return pe.do(lambda e: e.transpose(o, i, ident[0:i.shape[0], 0:i.shape[0]]), *tokens, signal=signal)

        def copy(q, o, i, *t):
            if q is act:
                return q.do(lambda e: e.activation(o, i, ACT.Copy), *t)
            return q.do(lambda e: e.tensor_copy(o, i), *t)

        def fn(o, i, f, *t, bias=0.0, scale=1.0, accum=None):
            if accum is None:
                return act.do(lambda e: e.activation(o, i, f, bias=bias, scale=scale), *t)
            return act.do(lambda e: e.activation(o, i, f, bias=bias, scale=scale, accum_out=accum), *t)

        def tt(q, o, a, b, op, *t):
            return q.do(lambda e: e.tensor_tensor(o, a, b, op), *t)

        def ts(q, o, a, s1, op0, *t, s2=None, op1=None):
            if op1 is None:
                return q.do(lambda e: e.tensor_scalar(o, a, s1, None, op0), *t)
            return q.do(lambda e: e.tensor_scalar(o, a, s1, s2, op0, op1), *t)

        def stt(o, a, s, b, op0, op1, *t):
            return dve.do(lambda e: e.scalar_tensor_tensor(out=o, in0=a, scalar=s, in1=b, op0=op0, op1=op1), *t)

        def recip(o, i, *t):
            return dve.do(lambda e: e.reciprocal(o, i), *t)

        def memset(q, o, v, *t):
            return q.do(lambda e: e.memset(o, v), *t)

        t_const = small_dma(act, const[:, :], A["c_square"])
        t_ones = memset(dve, ones[:, :], 1.0)
        t_e1 = memset(dve, eps_t[:, 0:1], 1e-6)
        t_e2 = memset(dve, eps_t[:, 1:2], 1e-5)
        for q in (act, dve, pe):
            q.wait(t_const, t_ones, t_e1, t_e2)

        xin, o1 = area(0, NT, D)
        packs, o2 = area(o1, 6, P)
        t_x = small_dma(sp, xin, A["x"][0].rearrange("(t p) n -> p t n", p=P))
        pack_lists = [
            [("norm_mix", 8), ("gate_b", 24), ("norm_mlp", 8), ("norm_final", 8), ("diff_subln", 1),
             ("dsa_kv_norm", 1), ("ada_b", 48), ("c", 8)],
            [("even_conv_b_2", 8), ("even_conv_ln_g_2", 8), ("even_conv_ln_b_2", 8),
             ("even_ssm_conv_b_2", 12), ("even_ssm_norm_g_2", 8), ("even_ssm_conv_w_2", 48),
             ("odd_b_gate_2", 4), ("odd_head_norm_g_2", 2)],
            [("ln_g_2", 48), ("ln_b_2", 48)],
        ]
        col = {}
        t_zero = memset(pool, packs, 0.0)
        t_packs = [[] for _ in range(5)]
        for n, names in enumerate(pack_lists):
            at = 0
            for name, rows in names:
                a = A[name]
                while len(a.shape) > 1:
                    a = a.rearrange("a b ... -> (a b) ...") if len(a.shape) > 2 else a.rearrange("a b -> (a b)")
                t_packs[n].append(small_dma(act if n else sp, packs[at:at + rows, n, :],
                                            a.rearrange("(r p) -> r p", p=P), t_zero))
                col[name] = (n, at)
                at += rows
        conv_rows = A["even_conv_w_2"][0].rearrange("t (m p) -> (t m) p", p=P)
        t_packs[3].append(small_dma(act, packs[:, 3, :], conv_rows[0:P, :], t_zero))
        t_packs[4].append(small_dma(act, packs[0:CONV_W * KC - P, 4, :], conv_rows[P:CONV_W * KC, :], t_zero))
        for n in range(5):
            i, b, free = att.take()
            t = turn(b[:, 0:P], packs[:, n, :], *t_packs[n], free)
            t_vec = att.free[i] = copy(dve, vec[:, n, :], b[:, 0:P], t)
        for q in (act, dve, pe, pool):
            q.wait(t_vec)

        def column(name, m=0):
            n, at = col[name]
            return vec[:, n, at + m:at + m + 1]

        def columns(name, m, k):
            n, at = col[name]
            return vec[:, n, at + m:at + m + k]

        def conv_tap(t, m):
            r = t * KC + m
            return vec[:, 3 + r // P, r % P:r % P + 1]

        for k in range(KC):
            i, b, free = att.take()
            for t in range(NT):
                tok = turn(b[:, t * P:(t + 1) * P], xin[:, t, k * P:(k + 1) * P], t_x, free, signal=t == NT - 1)
            t_h = att.free[i] = copy(dve, hT[:, k, :], b[:, :], tok)
        stage()

        def products(bank, hi, lo, x, first, last, t_w, free, cols=None):
            kc = hi.shape[1]
            for k in range(kc):
                xh, xl, tx = x(k)
                start = first and k == 0
                end = last and k == kc - 1
                mm(bank, hi[:, k, :], xh, start, False, t_w, free if start else None, tx)
                mm(bank, hi[:, k, :], xl, False, False)
                t = mm(bank, lo[:, k, :], xh, False, end, signal=k == kc - 1)
            return t

        def linear(parts, n_cols, evac, n=S):
            group = 1 if len(parts) == 1 else 4
            for m0 in range(0, n_cols // P, group):
                took = []
                for pi, (dram, x) in enumerate(parts):
                    for j in range(group):
                        m = m0 + j
                        if pi == 0:
                            took.append(lin.take())
                        bi, b, free = took[j]
                        done, hi, lo, t_w = unit(dram[:, m * P:(m + 1) * P])
                        t = products(b[:, 0:n], hi, lo, x, pi == 0, pi == len(parts) - 1, t_w, free)
                        done(t)
                        if pi == len(parts) - 1:
                            lin.free[bi] = evac(m, b[:, 0:n], t)
                        yield

        def split_of(src, hi, lo, *tokens):
            t_h = act.do(lambda e: e.activation(hi, src, ACT.Copy), *tokens)
            t_l = dve.do(lambda e: e.tensor_tensor(lo, src, hi.bitcast(F32), ALU.subtract), t_h, *tokens)
            return [t_h, t_l]

        t_X = [None] * KC
        X = lambda k: (XH[:, k, :], XL[:, k, :], t_X[k])

        turn_ring = Ring([gates[:, j, :] for j in range(2)])
        waiting = []

        def flush():
            while waiting:
                waiting.pop(0)()

        def by_tokens(store, n=S):
            def evac(m, b, t):
                gi, g, gf = turn_ring.take()
                t_g = copy(act, g[:, 0:n], b, t, gf)

                def later():
                    i, b2, free = att.take()
                    for j in range(n // P):
                        t2 = turn(b2[:, j * P:(j + 1) * P], g[:, j * P:(j + 1) * P], t_g, free, signal=j == n // P - 1)
                    turn_ring.free[gi] = t2
                    att.free[i] = store(m, b2, t2)
                if waiting:
                    waiting.pop(0)()
                waiting.append(later)
                return t_g
            return evac

        def run_all(gen):
            for _ in gen:
                pass

        def step(gen, n=1):
            for _ in range(n):
                if next(gen, "end") == "end":
                    return

        def chain(*gens):
            for g in gens:
                yield from g

        sq_ring = Ring([sq[:, 0, :], sq[:, 1, :]])

        def rstd_of(ss_bank, t_ss, n, eps_col, o, mean_sq=None, *tokens):
            if mean_sq is None:
                t = fn(o, ss_bank, ACT.Ln, t_ss, *tokens, bias=eps_t[0:o.shape[0], eps_col:eps_col + 1], scale=1.0 / n)
            else:
                t = stt(o, ss_bank, 1.0 / n, mean_sq, ALU.mult, ALU.subtract, t_ss, *tokens)
                t = fn(o, o, ACT.Ln, t, bias=eps_t[:, eps_col:eps_col + 1])
            return fn(o, o, ACT.Exp, t, scale=-0.5), t

        acc_s, acc_q = stat[:, 0, :], stat[:, 1, :]

        class Sums:

            def __init__(self, want_sum):
                self.n, self.want_sum, self.t_s, self.t_q = 0, want_sum, None, None
                self.first, self.free = None, list(stat_free)

            def add(self, src, tok):
                self.n += 1
                if self.n == 1:
                    self.first = (src, tok)
                    self.t_q = fn(acc_q, src, ACT.Square, tok, *self.free)
                    self.t_s = tok
                    return
                i, s, f = sq_ring.take()
                t = fn(s, src, ACT.Square, tok, f)
                self.t_q = sq_ring.free[i] = tt(dve, acc_q, acc_q, s, ALU.add, t, self.t_q)
                if self.want_sum:
                    a = self.first[0] if self.n == 2 else acc_s
                    self.t_s = tt(pool, acc_s, a, src, ALU.add, tok, self.t_s, self.free)

            def over_partitions(self, acc, t):
                i, b, free = att.take()
                t = mm(b[:, :], ones[:, :], acc, True, True, t, free, signal=True)
                return i, b, t

        def rms_stats(src, chunks, n, eps_col, o, tokens):
            sums = Sums(False)
            for k in chunks:
                sums.add(src(k), tokens[k])
            return rms_of(sums, n, eps_col, o)

        def rms_of(sums, n, eps_col, o):
            i, b, t = sums.over_partitions(acc_q, sums.t_q)
            r, freed = rstd_of(b[:, :], t, n, eps_col, o)
            att.free[i] = freed
            return r

        def layer_norm(src, sums, g, finish):
            i1, b1, t_m = sums.over_partitions(acc_s, sums.t_s)
            i2, b2, t_v = sums.over_partitions(acc_q, sums.t_q)
            mean, msq, rstd = (stat[:, j, :] for j in range(3))
            tm = ts(dve, mean, b1[:, :], 1.0 / D, ALU.mult, t_m)
            att.free[i1] = tm
            t3 = tt(dve, msq, mean, mean, ALU.mult, tm, t_v)
            r, fr = rstd_of(b2[:, :], t_v, D, 1, rstd, msq, t3)
            att.free[i2] = fr
            out_t = []
            t1s = [tt(pool, src(k), src(k), mean, ALU.subtract, tm, t_m, t_v) for k in range(KC)]
            for k in range(KC):
                t2 = stt(src(k), src(k), g(k), rstd, ALU.mult, ALU.mult, t1s[k], r)
                out_t.append(finish(k, src(k), t2))
            stat_free[:] = [t2, t1s[-1]]
            return out_t

        stat_free = []

        cond = modc[:, 6 * KC:7 * KC].unsqueeze(2)
        cc = columns("c", 0, KC)
        ct = cond[:, :, 0]
        t = fn(ct, cc, ACT.Tanh, scale=0.5)
        t = stt(ct, ct, 1.0, cc, ALU.add, ALU.mult, t)
        t_cond = ts(dve, ct, ct, 0.5, ALU.mult, t)
        ada_ring = Ring([adat[:, j, :] for j in range(2)])

        def ada(m0, m1):
            for m in range(m0, m1):
                done, w, t = unit(A["ada_w"][0][:, m * P:(m + 1) * P], split=False)
                ri, a, rf = ada_ring.take()
                t = ts(dve, a, w[:, 0, :], cond[:, 0, :], ALU.mult, t, rf, t_cond)
                for k in range(1, KC):
                    t = stt(a, w[:, k, :], cond[:, k, :], a, ALU.mult, ALU.add, t)
                done(t)
                ai, ab, af = att.take()
                ada_ring.free[ri] = t = mm(ab[:, 0:1], a, ones[:, 0:1], True, True, t, af, signal=True)
                t_mod[0] = att.free[ai] = tt(dve, modc[:, m:m + 1], ab[:, 0:1], column("ada_b", m), ALU.add, t)
                yield

        t_mod = [None]
        run_all(ada(0, 16))
        shift = lambda i, m: modc[:, 24 * i + m:24 * i + m + 1]

        def modulated_gain(i, name):
            s = modc[:, 24 * i + 8:24 * i + 16]
            return stt(s, s, 1.0, columns(name, 0, 8), ALU.add, ALU.mult, t_mod[0])

        def modulated_norm(i, name, sums):
            t_g = modulated_gain(i, name)
            r = rms_of(sums, D, 0, stat[:, 0, :])
            for k in range(KC):
                si, s_, sf = sq_ring.take()
                t = stt(s_, hT[:, k, :], modc[:, 24 * i + 8 + k:24 * i + 9 + k], stat[:, 0, :],
                        ALU.mult, ALU.mult, r, t_g, sf)
                stat_free[:] = [t]
                t = ts(dve, s_, s_, shift(i, k), ALU.add, t)
                t_X[k] = split_of(s_, XH[:, k, :], XL[:, k, :], t)
                sq_ring.free[si] = t_X[k]

        sums = Sums(False)
        for k in range(KC):
            sums.add(hT[:, k, :], t_h)
        modulated_norm(0, "norm_mix", sums)
        stage()

        o = 0
        aq, o = area(o, 4, S)
        ak, o = area(o, 4, S)
        av, o = area(o, NT, 512)
        bq, o = area(o, 4, S)
        kvT, o = area(o, S)
        kv, o = area(o, NT, P)
        O_IQ = o
        iq, o = area(o, 2, S)
        ik, o = area(o, S)
        O_CQ = o
        cq, o = area(o, 2, S)
        ck, o = area(o, 2, S)
        cv, o = area(o, NT, 4, P)
        O_BIAS = o
        bias, o = area(o, 12, S)
        ws, o = area(o, 4, S)
        PT, o = area(o, NT, S)
        iw, o = area(o, NT, 8)
        top8, o = area(o, 8)
        w_in = A["w_in"][0]
        pick = stat

        table = lamb[0:BUCKETS + 1, 0:12]
        t0 = memset(dve, lamb[BUCKETS:BUCKETS + 1, 0:12], 1.0)
        t_tab = small_dma(sp, lamb[0:BUCKETS, 0:12], A["rel_bias"])
        oneh = ws[0:BUCKETS + 1, 0:2, :].rearrange("p a b -> p (a b)")[:, 0:640]
        t_one = small_dma(sp, oneh, A["c_onehot"], *so_far())
        strip = PT[0:12, 0:2, :].rearrange("p a b -> p (a b)")[:, 0:640]
        for c0, c1 in ((0, 512), (512, 640)):
            i, b, free = att.take()
            t = mm_group(b[0:12, 0:c1 - c0], [(table, oneh[:, c0:c1])], t_tab, t_one, t0, free)
            t_s = att.free[i] = copy(act, strip[:, c0:c1], b[0:12, 0:c1 - c0], t)
        t_sd = small_dma(sp, A["strip"], strip, t_s)
        flip_ring = Ring([cv[:, j, :, :].rearrange("p a b -> p (a b)") for j in range(NT)])
        for h in range(12):
            src = bass.AP(A["strip"].tensor, h * 640, [[1, P], [1, S]])
            fi, fb, ff = flip_ring.take()
            t = small_dma(sp, fb, src, t_sd, ff)
            i, b, free = att.take()
            t = flip_ring.free[fi] = mm_group(b[:, :], [(flip, fb)], t, free)
            t_bias = att.free[i] = copy(act, bias[:, h, :], b[:, :], t)
        dve.wait(t_bias)
        act.wait(t_sd)

        dl = lamb[:, P:P + 256]
        t = small_dma(sp, dl, A["diff_lambda"].rearrange("a b c -> a (b c)").to_broadcast([P, 256]))
        pr = lamb[:, 32:96]
        lam = lamb[:, 96:100]
        for j in range(2):
            t = tt(dve, pr, dl[:, j * 128:j * 128 + 64], dl[:, j * 128 + 64:j * 128 + 128], ALU.mult, t)
            t = dve.do(lambda e, j=j: e.tensor_reduce(lam[:, j:j + 1], pr, AX.X, ALU.add), t)
        t = fn(lam[:, 0:2], lam[:, 0:2], ACT.Exp, t)
        t = tt(dve, lam[:, 2:3], lam[:, 1:2], lam[:, 0:1], ALU.subtract, t)
        t_lam = ts(dve, lam[:, 2:3], lam[:, 2:3], -LAM_INIT, ALU.add, t)
        sub_g = lam[:, 3:4]
        t_subg = ts(dve, sub_g, column("diff_subln"), 1.0 - LAM_INIT, ALU.mult)

        def to(dst, q=None):
            def evac(m, b, t):
                return copy(q or act, dst[:, m, :], b, t)
            return evac

        def to_av(m, b, t):
            return copy(act, av[:, :, m * P:(m + 1) * P], b[:, :].rearrange("p (t c) -> p t c", t=NT), t)

        mod_fill = ada(16, 48)
        for _ in chain(linear([(w_in[:, COL_AV:COL_AV + 512], X)], 512, by_tokens(to_av)),
                       linear([(w_in[:, COL_AQ:COL_AQ + 512], X)], 512, to(aq)),
                       linear([(w_in[:, COL_AK:COL_AK + 512], X)], 512, to(ak))):
            step(mod_fill)
        flush()
        t_a = act.now

        t_cvz = memset(pool, cv, 0.0, pe.now)
        t_iw = [None]

        def evac_kv(m, b, t):
            return copy(act, kvT[:, :], b, t)

        def to_cv(m, b, t):
            src = b[:, :].rearrange("p (t c) -> p t c", t=NT)
            for par in range(2):
                last = copy(act, cv[:, :, 2 * m + par, par * DH:(par + 1) * DH], src[:, :, par * DH:(par + 1) * DH], t, t_cvz)
            return last

        def index_small():
            bi, b, free = lin.take()
            done, hi, lo, t_w = unit(*[w_in[:, COL_IK:COL_IK + IDX_DIM]] * 4)
            t = products(b[:, :], hi, lo, X, True, True, t_w, free)
            done(t)
            lin.free[bi] = copy(act, ik[:, :], b[:, :], t)
            yield
            bi, b, free = lin.take()
            done, hi, lo, t_w = unit(w_in[:, COL_IW:COL_IW + 8])
            for tt_ in range(NT):
                o_ = b[:, tt_ * 8:tt_ * 8 + 8]
                for k in range(KC):
                    xh, xl = (a[:, k, tt_ * P:(tt_ + 1) * P] for a in (XH, XL))
                    mm(o_, xh, hi[:, k, :], k == 0, False, t_w, free)
                    mm(o_, xl, hi[:, k, :], False, False)
                    t = mm(o_, xh, lo[:, k, :], False, k == KC - 1, signal=k == KC - 1)
            done(t)
            t_iw[0] = lin.free[bi] = ts(dve, iw, b[:, 0:32].rearrange("p (a b) -> p a b", a=NT),
                                        IDX_HEADS ** -0.5 * IDX_DIM ** -0.5, ALU.mult, t)
            yield

        fill = chain(
            linear([(w_in[:, COL_CV:COL_CV + 256], X)], 256, by_tokens(to_cv)),
            linear([(w_in[:, COL_BQ:COL_BQ + 512], X)], 512, to(bq)),
            linear([(w_in[:, COL_BKV:COL_BKV + P], X)], P, evac_kv),
            linear([(w_in[:, COL_IQ:COL_IQ + 256], X)], 256, to(iq)),
            index_small(),
            linear([(w_in[:, COL_CQ:COL_CQ + 256], X)], 256, to(cq)),
            linear([(w_in[:, COL_CK:COL_CK + 256], X)], 256, to(ck)),
        )

        ws_ring = Ring([ws[:, j, :] for j in range(4)])
        st_ring = Ring([soft[:, 4 * j:4 * j + 4] for j in range(8)])
        pt_free = [None]
        pt_written = {}

        def causal_softmax(q, k, qt, scale, hb, *tokens, extra=None):
            L = (qt + 1) * P
            i, b, free = att.take()
            t = mm(b[:, 0:L], q, k, True, True, free, *tokens, signal=True)
            wi, w, wf = ws_ring.take()
            si, st, sf = st_ring.take()
            w = w[:, 0:L]
            t = att.free[i] = stt(w, b[:, 0:L], scale, bias[:, hb, S - L:S], ALU.mult, ALU.add, t, wf, sf)
            if extra is not None:
                t = tt(dve, w, w, extra, ALU.add, t)
            t = dve.do(lambda e: e.tensor_reduce(st[:, 0:1], w, AX.X, ALU.max, negate=True), t)
            t = fn(w, w, ACT.Exp, t, bias=st[:, 0:1], accum=st[:, 1:2])
            t_r = recip(st[:, 2:3], st[:, 1:2], t)
            return w, wi, st, si, t_r

        def turn_rows(w, wi, qt, t_w, first):
            i, b, free = att.take()
            for kt in range(qt + 1):
                t = turn(b[:, kt * P:(kt + 1) * P], w[:, kt * P:(kt + 1) * P], t_w, free, signal=kt == qt)
            ws_ring.free[wi] = t
            t = att.free[i] = copy(act, PT[:, 0:qt + 1, qt * P:(qt + 1) * P],
                                   b[:, 0:(qt + 1) * P].rearrange("p (a b) -> p a b", b=P), t, pt_free[0])
            return t

        def weigh(b, v, free, first, last, t_pt):
            for kt in range(NT):
                t = mm(b[:, kt * P:S], v(kt), PT[:, kt, kt * P:S], first and kt == 0, last and kt == NT - 1,
                       t_pt, free if kt == 0 else None, signal=kt == NT - 1)
            pt_free[0] = t
            return t

        def diff_tiles():
            for h in range(HEADS_A):
                for qt in range(NT):
                    two = [causal_softmax(aq[DH * m:DH * (m + 1), h, qt * P:(qt + 1) * P],
                                          ak[DH * m:DH * (m + 1), h, 0:(qt + 1) * P], qt, DH ** -0.5, h, t_a)
                           for m in range(2)]
                    (w0, i0, s0, j0, r0), (w1, i1, s1, j1, r1) = two
                    t = tt(dve, s1[:, 3:4], s1[:, 2:3], lam[:, 2:3], ALU.mult, r1, t_lam)
                    t0 = ts(dve, w0, w0, s0[:, 2:3], ALU.mult, r0)
                    t = stt(w0, w1, s1[:, 3:4], w0, ALU.mult, ALU.add, t, t0)
                    ws_ring.free[i1] = t
                    st_ring.free[j0] = st_ring.free[j1] = t
                    yield
                    t_pt = turn_rows(w0, i0, qt, t, qt == 0)
                i, b, free = att.take()
                t = weigh(b, lambda kt: av[:, kt, h * P:(h + 1) * P], free, True, True, t_pt)
                t_o = copy(dve, aq[:, h, :], b[:, :], t)
                att.free[i] = t_o
                yield
                r = rms_stats(lambda k: aq[:, h, :], [0], P, 0, stat[:, 0, :], [t_o])
                t = stt(aq[:, h, :], aq[:, h, :], sub_g, stat[:, 0, :], ALU.mult, ALU.mult, r, t_subg)
                stat_free[:] = [t]
                t_ya[h] = split_of(aq[:, h, :], bias_r[:, h, :], aq_r[:, h, :], t)

        bias_r = area(O_BIAS, 12, S, r=True)[0]
        aq_r = area(0, 4, S, r=True)[0]
        cq_r = area(O_CQ, 2, S, r=True)[0]
        ob_r = area(O_IQ, 2, S, r=True)[0]
        t_ya = [None] * 4
        for _ in diff_tiles():
            step(fill)
            step(mod_fill, 2)
        run_all(fill)
        run_all(mod_fill)
        flush()
        t_proj = so_far()

        r = rms_stats(lambda k: kvT[:, :], [0], P, 0, stat[:, 0, :], t_proj[1:2])
        t_kv = stt(kvT[:, :], kvT[:, :], column("dsa_kv_norm"), stat[:, 0, :], ALU.mult, ALU.mult, r)
        stat_free[:] = [t_kv]
        i, b, free = att.take()
        for t_ in range(NT):
            t = turn(b[:, t_ * P:(t_ + 1) * P], kvT[:, t_ * P:(t_ + 1) * P], t_kv, free, signal=t_ == NT - 1)
        t_kv = att.free[i] = copy(act, kv, b[:, :].rearrange("p (a b) -> p a b", b=P), t)

        def index_scores():
            for qt in range(1, NT):
                L = (qt + 1) * P
                acc = pick[:, qt - 1, 0:L]
                t_acc = None
                for h in range(IDX_HEADS):
                    i, b, free = att.take()
                    r0 = IDX_DIM * (h % 4)
                    t = mm(b[:, 0:L], iq[r0:r0 + IDX_DIM, h // 4, qt * P:(qt + 1) * P],
                           ik[r0:r0 + IDX_DIM, 0:L], True, True, free, *t_proj, signal=True)
                    wi, w, wf = ws_ring.take()
                    t = att.free[i] = fn(w[:, 0:L], b[:, 0:L], ACT.Relu, t, wf)
                    if h == 0:
                        prev = causal[:, S - L:S]
                        t_acc = ts(dve, acc, w[:, 0:L], iw[:, qt, h:h + 1], ALU.mult, t, t_iw[0])
                    else:
                        t_acc = stt(acc, w[:, 0:L], iw[:, qt, h:h + 1], acc, ALU.mult, ALU.add, t, t_acc)
                    ws_ring.free[wi] = t_acc
                    if h % 4 == 3:
                        yield
                t_acc = tt(dve, acc, acc, causal[:, S - L:S], ALU.add, t_acc)
                t_pick[qt] = t_acc

        t_pick = [None] * NT

        def topk_rounds():
            for qt in range(1, NT):
                L = (qt + 1) * P
                acc = pick[:, qt - 1, 0:L]
                t = t_pick[qt]
                for r in range(TOPK // 8):
                    t = dve.do(lambda e, acc=acc: e.max(top8[:, :], acc), t)
                    t = dve.do(lambda e, acc=acc: e.match_replace(acc, top8[:, :], acc, TAKEN), t)
                    yield
                t_pick[qt] = ts(dve, acc, acc, 2.0 * NEG * 1e8, ALU.is_gt, t, s2=NEG, op1=ALU.mult)

        merged = arena[:, 2048:2048 + 8 * S].rearrange("p (a b) -> p a b", a=KC)
        gate_ring = Ring([gates[:, j, :] for j in range(2)])
        t_merged = [None] * KC

        def branch(n, weights, x_chunks):
            for m in range(KC):
                    c0 = COL_G + n * D + m * P
                    bi, b, free = lin.take()
                    done, hi, lo, t_w = unit(w_in[:, c0:c0 + P])
                    t = products(b[:, :], hi, lo, X, True, True, t_w, free)
                    done(t)
                    gi, g, gf = gate_ring.take()
                    tg = lin.free[bi] = fn(g, b[:, :], ACT.Tanh, t, gf, t_half, bias=gbh[:, n * 8 + m:n * 8 + m + 1], scale=0.5)
                    tg = ts(pool, g, g, 0.5, ALU.mult, tg, s2=0.5, op1=ALU.add)
                    yield
                    bi, b, free = lin.take()
                    done, hi, lo, t_w = unit(weights[:, m * P:(m + 1) * P])
                    t = products(b[:, :], hi, lo, x_chunks, True, True, t_w, free)
                    done(t)
                    if n == 0:
                        t = tt(dve, merged[:, m, :], b[:, :], g, ALU.mult, t, tg)
                        t_merged[m] = gate_ring.free[gi] = lin.free[bi] = t
                    else:
                        t = lin.free[bi] = tt(dve, g, b[:, :], g, ALU.mult, t, tg)
                        t_merged[m] = gate_ring.free[gi] = tt(pool, merged[:, m, :], merged[:, m, :], g, ALU.add,
                                                              t, t_merged[m])
                    yield

        gbh = sb("gbh", [P, 24])
        t_half = ts(dve, gbh[:, :], columns("gate_b", 0, 24), 0.5, ALU.mult)

        def block_tiles():
            for g in range(2):
                oi, ob, of = att_out.take()
                for par in range(2):
                    h = 2 * g + par
                    for qt in range(NT):
                        w, wi, st, si, t = causal_softmax(
                            cq[DH * par:DH * (par + 1), g, qt * P:(qt + 1) * P],
                            ck[DH * par:DH * (par + 1), g, 0:(qt + 1) * P], qt, DH ** -0.5, 8 + h, *t_proj)
                        t = fn(w, w, ACT.Copy, t, scale=st[:, 2:3])
                        st_ring.free[si] = t
                        yield
                        t_pt = turn_rows(w, wi, qt, t, qt == 0)
                    t = weigh(ob, lambda kt: cv[:, kt, h, :], of if par == 0 else None, par == 0, par == 1, t_pt)
                t_c[g] = split_of(ob[:, :], bias_r[:, 8 + g, :], cq_r[:, g, :], t)
                att_out.free[oi] = t_c[g]

        att.bufs, att.free = banks[4:7], att.free[:3]
        att.n = 0
        att.free = [so_far()] * 3
        att_out = Ring([banks[7]])
        att_out.free = [so_far()]
        t_c = [None, None]
        t_b = [None] * 4

        def latent_tiles():
            for h in range(HEADS_B):
                for qt in range(NT):
                    extra = pick[:, qt - 1, 0:(qt + 1) * P] if qt else None
                    w, wi, st, si, t = causal_softmax(
                        bq[:, h, qt * P:(qt + 1) * P], kvT[:, 0:(qt + 1) * P], qt, P ** -0.5, 4 + h,
                        *t_proj, t_kv, t_pick[qt] if qt else None, extra=extra)
                    t = fn(w, w, ACT.Copy, t, scale=st[:, 2:3])
                    st_ring.free[si] = t
                    yield
                    t_pt = turn_rows(w, wi, qt, t, qt == 0)
                oi, ob, of = att_out.take()
                t = weigh(ob, lambda kt: kv[:, kt, :], of, True, True, t_pt)
                t_b[h] = att_out.free[oi] = copy(dve, bq[:, h, :], ob[:, :], t)

        filler = branch(0, A["w_br_a"][0], lambda k: (bias_r[:, k, :], aq_r[:, k, :], t_ya[k]))
        tops = topk_rounds()
        for _ in index_scores():
            step(filler)
        for _ in block_tiles():
            step(tops, 3)
            step(filler)
        run_all(tops)
        filler = chain(filler, branch(2, A["w_br_c"][0], lambda k: (bias_r[:, 8 + k, :], cq_r[:, k, :], t_c[k])))
        for _ in latent_tiles():
            step(filler)
        run_all(filler)
        wuv = sq[:, 0, :].rearrange("p (a b) -> p a b", a=4)
        t_z = memset(pool, wuv, 0.0, *so_far())
        t_wuv = [small_dma(pool, wuv[:, h, (h % 2) * DH:(h % 2) * DH + DH], A["dsa_w_uv"][0, h], t_z) for h in range(4)]
        t_ob = [None] * 2
        for g in range(2):
            bi, b, free = lin.take()
            t = mm_group(b[:, :], [(wuv[:, 2 * g + j, :], bq[:, 2 * g + j, :]) for j in range(2)], *t_wuv, t_b[3], free)
            t_ob[g] = lin.free[bi] = split_of(b[:, :], bias_r[:, 4 + g, :], ob_r[:, g, :], t)
        run_all(branch(1, A["w_br_b"][0], lambda k: (bias_r[:, 4 + k, :], ob_r[:, k, :], t_ob[k])))

        gate = lambda i, m: modc[:, 24 * i + 16 + m:24 * i + 17 + m]
        t_hs = [None] * KC

        def to_residual(i):
            def evac(m, b, t):
                t_hs[m] = stt(hT[:, m, :], b, gate(i, m), hT[:, m, :], ALU.mult, ALU.add, t, t_mod[0])
                sums.add(hT[:, m, :], t_hs[m])
                return t_hs[m]
            sums = Sums(False)
            return evac, sums

        for k in range(KC):
            t_X[k] = split_of(merged[:, k, :], XH[:, k, :], XL[:, k, :], t_merged[k], pe.now)
        evac, sums = to_residual(0)
        run_all(linear([(A["w_o"][0], X)], D, evac))
        att.bufs, att.free, att.n = banks[4:8], [so_far()] * 4, 0

        FC = FF // P
        ffn_h = area(0, FC, S)[0]
        ffn_low = area(0, FC, S, r=True)[0]
        EARLY = (ARENA - FC * S) // S
        early_high = area(FC * S, EARLY, S, r=True)[0]

        def mlp(w1, w2, evac2):
            stage()
            t_f = [None] * FC

            def high(m):
                if m < EARLY:
                    return early_high[:, m, :]
                m -= EARLY
                return (XH if m < KC else XL)[:, m % KC, :]

            def evac1(m, b, t):
                t = fn(ffn_h[:, m, :], b, ACT.Relu, t)
                t2 = tt(pool if m % 2 else dve, ffn_h[:, m, :], ffn_h[:, m, :], ffn_h[:, m, :], ALU.mult, t)
                t_f[m] = split_of(ffn_h[:, m, :], high(m), ffn_low[:, m, :], t2) if m < EARLY else t2
                return t

            run_all(linear([(w1, X)], FF, evac1))
            t_x_read = pe.now
            todo = list(range(EARLY, FC))

            def rest():
                for _ in range(2):
                    if todo:
                        m = todo.pop(0)
                        t_f[m] = split_of(ffn_h[:, m, :], high(m), ffn_low[:, m, :], t_f[m], t_x_read)

            rest()
            for _ in linear([(w2[i * D:(i + 1) * D, :],
                              lambda k, i=i: (high(i * KC + k), ffn_low[:, i * KC + k, :], t_f[i * KC + k]))
                             for i in range(4)], D, evac2):
                rest()

        modulated_norm(1, "norm_mlp", sums)
        evac, sums = to_residual(1)
        mlp(A["w_ff1"][0], A["w_ff2"][0], evac)

        r = rms_of(sums, D, 0, stat[:, 0, :])
        for k in range(KC):
            t_hs[k] = stt(hT[:, k, :], hT[:, k, :], column("norm_final", k), stat[:, 0, :], ALU.mult, ALU.mult, r)
            stat_free[:] = [t_hs[k]]
            t_X[k] = split_of(hT[:, k, :], XH[:, k, :], XL[:, k, :], t_hs[k])

        h = lambda k: hT[:, k, :]

        def to_deepnorm():
            sums = Sums(True)

            def evac(m, b, t):
                t_hs[m] = stt(hT[:, m, :], hT[:, m, :], ALPHA, b, ALU.mult, ALU.add, t)
                sums.add(hT[:, m, :], t_hs[m])
                return t_hs[m]
            return evac, sums

        def block_norm(i, j, sums, last=False):
            c = (i * 3 + j) * 8

            def finish(k, s, t):
                bias_ = column("ln_b_2", c + k)
                if not last:
                    t_h = act.do(lambda e: e.activation(XH[:, k, :], s, ACT.Identity, bias=bias_, scale=1.0), t)
                t = ts(dve, s, s, bias_, ALU.add, t, None if last else t_h)
                if not last:
                    t_X[k] = [t_h, dve.do(lambda e: e.tensor_tensor(XL[:, k, :], s, XH[:, k, :].bitcast(F32), ALU.subtract), t, t_h)]
                return t
            t_hs[:] = layer_norm(h, sums, lambda k: column("ln_g_2", c + k), finish)

        def silu_of(o, b, scratch, t, *tokens, half_bias=None):
            hb = 0.0 if half_bias is None else half_bias
            t1 = fn(scratch, b, ACT.Tanh, t, *tokens, bias=hb, scale=0.5)
            t2 = ts(dve, o, b, 0.5, ALU.mult, t1, s2=hb, op1=ALU.add)
            return stt(o, scratch, 1.0, o, ALU.add, ALU.mult, t1, t2), t2

        stage()
        w_even = A["even_w_in_2"][0]
        o = 0
        VALW = S + CONV_W - 1
        XW_ = S + SSM_CONV - 1
        val, o = area(o, KC, VALW)
        conv, o = area(o, KC, S)
        O_XBC = o
        xbc, o = area(o, XBC_C, S)
        raw, o = area(o, 3, XW_)
        zT, _ = area(o, KC, S)
        XP, o = area(o, SSM_HEADS, P)
        XW, o = area(o, SSM_HEADS, DH)
        ST, o = area(o, SSM_HEADS, P)
        BM, o = area(o, 2, P)
        CB, o = area(o, 2, P)
        E1, o = area(o, 4, P)
        DEC, o = area(o, 4, P)
        CE, o = area(o, 4, P)
        tmp4, o = area(o, 2, S)
        dts, o = area(o, 8, 64)
        DE, o = area(o, SSM_HEADS)
        dsk, o = area(o, KC)
        hb12, o = area(o, XBC_C)
        prm, o = area(o, 3, 16)
        dt_, adt, nacs, dte, sc1, sc2, sc3, sc4 = (dts[:, j, :] for j in range(8))
        y_high = area(0, KC, S, r=True)[0]
        y_low = area(O_XBC, KC, S, r=True)[0]

        ev = so_far()
        t_p = [small_dma(act, prm[:, 0, :], A["even_dt_bias_2"].to_broadcast([P, 16])),
               small_dma(act, prm[:, 1, :], A["even_a_log_2"].to_broadcast([P, 16])),
               small_dma(act, prm[:, 2, :], A["even_d_skip_2"].to_broadcast([P, 16]))]
        t_wdt = small_dma(act, wsmall[:, :, :], w_even[:, EV_DT:EV_DT + 16].rearrange("(k p) n -> p k n", p=P), *ev)
        t_a = fn(prm[:, 1, :], prm[:, 1, :], ACT.Exp, *t_p)
        pd = prm[:, 2, :].rearrange("p (m two) -> p m two", two=2)
        t1 = copy(dve, dsk[0:DH, :], pd[0:DH, :, 0], *t_p)
        t_dsk = copy(dve, dsk[DH:P, :], pd[DH:P, :, 1], t1)
        t_hb = ts(dve, hb12, columns("even_ssm_conv_b_2", 0, XBC_C), 0.5, ALU.mult)
        t_pad = [memset(pool, val[:, :, 0:CONV_W - 1], 0.0), memset(pool, raw[:, :, 0:SSM_CONV - 1], 0.0),
                 memset(pool, XP, 0.0), memset(pool, ST, 0.0)]

        bi, b, free = lin.take()
        for c in range(NT):
            t = mm_group(b[:, c * 16:(c + 1) * 16],
                         [(h(k)[:, c * P:(c + 1) * P], wsmall[:, k, :]) for k in range(KC)], t_wdt, free, *t_hs)
        b4 = b[:, 0:64].rearrange("p (c h) -> p c h", c=NT)
        v4 = lambda a: a.rearrange("p (c h) -> p c h", c=NT)
        t = lin.free[bi] = tt(dve, v4(dt_), b4, prm[:, 0, :].unsqueeze(1).to_broadcast([P, NT, 16]), ALU.add, t, *t_p)

        def log1p_exp_minus(x, e, uu, ln, o, t):
            t1 = ts(dve, e, x, -1.0, ALU.mult, t)
            t1 = tt(dve, e, e, x, ALU.min, t1)
            t1 = fn(e, e, ACT.Exp, t1)
            t2 = ts(dve, uu, e, 1.0, ALU.add, t1)
            t3 = fn(ln, uu, ACT.Ln, t2)
            t1 = stt(e, uu, -1.0, e, ALU.add, ALU.subtract, t1, t2)
            t2 = recip(uu, uu, t2, t3, t1)
            t1 = tt(dve, e, e, uu, ALU.mult, t1, t2)
            return tt(dve, o, ln, e, ALU.subtract, t3, t1)

        t = log1p_exp_minus(dt_, sc1, sc2, sc3, sc4, t)
        t_dt = stt(dt_, dt_, 0.0, sc4, ALU.max, ALU.add, t)
        a_b = prm[:, 1, :].unsqueeze(1).to_broadcast([P, NT, 16])
        t = tt(dve, v4(adt), v4(dt_), a_b, ALU.mult, t_dt, t_a)
        t_adt = ts(dve, adt, adt, -1.0, ALU.mult, t)
        i, b, free = att.take()
        t = mm_group(b[:, 0:64], [(upper, adt)], t_adt, free)
        t = mm_group(b[:, 64:128], [(ones[:, :], adt)])
        t_n = ts(dve, nacs, b[:, 0:64], -1.0, ALU.mult, t)
        t = att.free[i] = tt(dve, dte, b[:, 64:128], nacs, ALU.add, t_n)
        t_dte = fn(dte, dte, ACT.Exp, t)

        raw_ring = Ring([raw[:, j, :] for j in range(3)])
        sil = Ring([tmp4[:, j, :] for j in range(2)])
        t_xbc = [None] * XBC_C

        def evac_xbc(m, b, t):
            i, r, f = raw_ring.take()
            te = copy(act, r[:, SSM_CONV - 1:], b, t, f, t_pad[1])
            wcol = lambda j: column("even_ssm_conv_w_2", j * XBC_C + m)
            o = xbc[:, m, :]
            tc = ts(dve, o, r[:, 0:S], wcol(0), ALU.mult, te)
            for j in range(1, SSM_CONV):
                tc = stt(o, r[:, j:j + S], wcol(j), o, ALU.mult, ALU.add, tc)
            raw_ring.free[i] = tc
            si, s, sf = sil.take()
            t1 = fn(s, o, ACT.Tanh, tc, sf, t_hb, bias=hb12[:, m:m + 1], scale=0.5)
            t2 = ts(dve, o, o, 0.5, ALU.mult, t1, t_hb, s2=hb12[:, m:m + 1], op1=ALU.add)
            t_xbc[m] = sil.free[si] = stt(o, s, 1.0, o, ALU.add, ALU.mult, t1, t2)
            return te

        def evac_z(m, b, t):
            si, s, sf = sil.take()
            sil.free[si], t2 = silu_of(zT[:, m, :], b, s, t, sf)
            return t2

        run_all(linear([(w_even[:, EV_XBC:EV_XBC + XBC], X)], XBC, evac_xbc))

        t_conv = [None] * KC

        def conv_units():
            for m in range(KC):
                    b1i, b1, f1 = lin.take()
                    done, hi, lo, t_w = unit(w_even[:, EV_GATE + m * P:EV_GATE + (m + 1) * P])
                    t1 = products(b1[:, :], hi, lo, X, True, True, t_w, f1)
                    done(t1)
                    gi, g, gf = gate_ring.take()
                    tg = lin.free[b1i] = fn(g, b1[:, :], ACT.Tanh, t1, gf, scale=0.5)
                    tg = ts(pool, g, g, 0.5, ALU.mult, tg, s2=0.5, op1=ALU.add)
                    yield
                    b2i, b2, f2 = lin.take()
                    done, hi, lo, t_w = unit(w_even[:, EV_VAL + m * P:EV_VAL + (m + 1) * P])
                    t2 = products(b2[:, :], hi, lo, X, True, True, t_w, f2)
                    done(t2)
                    t = tt(dve, val[:, m, CONV_W - 1:], b2[:, :], g, ALU.mult, t2, tg, t_pad[0])
                    lin.free[b2i] = gate_ring.free[gi] = t
                    o = conv[:, m, :]
                    t = ts(dve, o, val[:, m, 0:S], conv_tap(0, m), ALU.mult, t, s2=column("even_conv_b_2", m), op1=ALU.add)
                    for tap in range(1, CONV_W):
                        t = stt(o, val[:, m, tap:tap + S], conv_tap(tap, m), o, ALU.mult, ALU.add, t)
                        if tap == 15:
                            yield
                    t_conv[m] = t
                    yield

        def ssm_steps():
            pair = lambda a: a.rearrange("p (g two) d -> p g two d", two=2)
            t_y = None
            t_st = None
            for c in range(NT):
                cs = slice(c * P, (c + 1) * P)
                dtc = dt_[:, c * 16:(c + 1) * 16].rearrange("p (g two) -> p g two", two=2)
                t_xp = []
                for half in range(2):
                    i, b, free = att.take()
                    for j in range(4):
                        t = turn(b[:, j * P:(j + 1) * P], xbc[:, half * 4 + j, cs], free, *t_xbc, t_y, signal=j == 3)
                    bb = b[:, :].rearrange("p (g two d) -> p g two d", two=2, d=DH)
                    for par in range(2):
                        t2 = tt(dve, pair(XP)[:, half * 4:half * 4 + 4, par, par * DH:(par + 1) * DH], bb[:, :, par, :],
                                dtc[:, half * 4:half * 4 + 4, par].unsqueeze(2).to_broadcast([P, 4, DH]), ALU.mult,
                                t, t_dt, t_pad[2], t_y)
                        t_xp.append(t2)
                    att.free[i] = t2
                t_xw = None
                dtec = dte[:, c * 16:(c + 1) * 16].rearrange("p (g two) -> p g two", two=2)
                for par in range(2):
                    t_xw = tt(pool, pair(XW)[:, :, par, :], pair(XP)[:, :, par, par * DH:(par + 1) * DH],
                              dtec[:, :, par].unsqueeze(2).to_broadcast([P, 8, DH]), ALU.mult, *t_xp, t_dte, t_st)
                i, b, free = att.take()
                for g in range(2):
                    t = turn(b[:, g * P:(g + 1) * P], xbc[:, 8 + g, cs], free, signal=False)
                for g in range(2):
                    t = mm(b[:, 256 + g * P:256 + (g + 1) * P], xbc[:, 8 + g, cs], xbc[:, 10 + g, cs], True, True,
                           signal=g == 1)
                t_bm = copy(act, BM, b[:, 0:256].rearrange("p (a b) -> p a b", a=2), t, t_st)
                t_cb = att.free[i] = copy(act, CB, b[:, 256:512].rearrange("p (a b) -> p a b", a=2), t, dve.now)
                yield
                for q4 in range(4):
                    g = q4 // 2
                    i, b, free = att.take()
                    for j in range(4):
                        hd = c * 16 + q4 * 4 + j
                        t = mm(b[:, j * P:(j + 1) * P], adt[:, hd:hd + 1].to_broadcast([P, P]), upper, True, True,
                               free, t_adt, signal=j == 3)
                    bb = b[:, :].rearrange("p (a b) -> p a b", a=4)
                    t_e = fn(E1, bb, ACT.Exp, t, pool.now, t_y, t_st)
                    t_seg = att.free[i] = tt(dve, DEC, bb, seg_mask.unsqueeze(1).to_broadcast([P, 4, P]), ALU.add, t, t_y, t_e)
                    t_de = copy(dve, DE[:, q4 * 4:q4 * 4 + 4], E1[:, :, P - 1], t_e, t_st)
                    for j in range(4):
                        hd = c * 16 + q4 * 4 + j
                        t = fn(DEC[:, j, :], DEC[:, j, :], ACT.Exp, t_seg, t_n, bias=nacs[:, hd:hd + 1])
                    t_g = tt(dve, DEC, DEC, CB[:, g, :].unsqueeze(1).to_broadcast([P, 4, P]), ALU.mult, t, t_cb)
                    t_ce = tt(pool, CE, E1, xbc[:, 10 + g, cs].unsqueeze(1).to_broadcast([P, 4, P]), ALU.mult, t_e, t_y)
                    yield
                    i, b, free = att.take()
                    for pr_ in range(2):
                        ops = []
                        for par in range(2):
                            hh = q4 * 4 + pr_ * 2 + par
                            ops.append((XP[:, hh, :], DEC[:, pr_ * 2 + par, :]))
                        for par in range(2):
                            hh = q4 * 4 + pr_ * 2 + par
                            ops.append((ST[:, hh, :], CE[:, pr_ * 2 + par, :]))
                        t = mm_group(b[:, pr_ * P:(pr_ + 1) * P], ops, free, t_g, t_ce, t_st, *t_xp, t_pad[3])
                    for pr_ in range(2):
                        m = q4 * 2 + pr_
                        t_y = stt(xbc[:, m, cs], xbc[:, m, cs], dsk[:, m:m + 1], b[:, pr_ * P:(pr_ + 1) * P],
                                  ALU.mult, ALU.add, t, t_dsk)
                    att.free[i] = t_y
                for g in range(2):
                    i, b, free = att.take()
                    t = mm_group(b[:, :], [(BM[:, g, :], XW[:, g * 8:(g + 1) * 8, :].rearrange("p a b -> p (a b)"))],
                                 t_bm, t_xw, free)
                    bb = b[:, :].rearrange("p (g two d) -> p g two d", two=2, d=DH)
                    de = DE.rearrange("p (g two) -> p g two", two=2)
                    for par in range(2):
                        s_ = pair(ST)[:, g * 4:(g + 1) * 4, par, par * DH:(par + 1) * DH]
                        t2 = tt(dve, s_, s_, de[:, g * 4:(g + 1) * 4, par].unsqueeze(2).to_broadcast([P, 4, DH]),
                                ALU.mult, t_de, t, t_y)
                        t_st = tt(dve, s_, s_, bb[:, :, par, :], ALU.add, t2)
                    att.free[i] = t_st
            t_yend[0] = t_y

        t_yend = [None]
        cu = conv_units()
        for _ in ssm_steps():
            step(cu, 2)
        run_all(cu)
        t_ssm = so_far()
        act.wait(*t_ssm)
        dve.wait(*t_ssm)
        run_all(linear([(w_even[:, EV_Z:EV_Z + D], X)], D, evac_z))

        ty = []
        for m in range(KC):
            ty.append(tt(dve, xbc[:, m, :], xbc[:, m, :], zT[:, m, :], ALU.mult, t_yend[0], dve.now))
        t_y2 = [None] * KC
        for g in range(2):
            r = rms_stats(lambda k: xbc[:, k, :], range(g * 4, g * 4 + 4), 4 * P, 1, stat[:, 2, :], ty)
            for m in range(g * 4, g * 4 + 4):
                t = stt(xbc[:, m, :], xbc[:, m, :], column("even_ssm_norm_g_2", m), stat[:, 2, :],
                        ALU.mult, ALU.mult, r)
                t_y2[m] = split_of(xbc[:, m, :], y_high[:, m, :], y_low[:, m, :], t)
                stat_free[:] = [t]

        sil2 = Ring([tmp4[:, j, :] for j in range(2)])
        sil2.free = [dve.now] * 2

        def ln_silu(k, s, t):
            bcol = column("even_conv_ln_b_2", k)
            i, w, f = sil2.take()
            t = fn(s, s, ACT.Identity, t, bias=bcol)
            t1 = fn(w, s, ACT.Tanh, t, f, scale=0.5)
            t2 = stt(s, w, 1.0, s, ALU.add, ALU.mult, t1)
            sil2.free[i] = t2
            t = ts(dve, s, s, 0.5, ALU.mult, t2)
            t_X[k] = split_of(s, XH[:, k, :], XL[:, k, :], t)
            return t

        sums = Sums(True)
        for k in range(KC):
            sums.add(conv[:, k, :], t_conv[k])
        layer_norm(lambda k: conv[:, k, :], sums, lambda k: column("even_conv_ln_g_2", k), ln_silu)
        w_out = A["even_w_out_2"][0]
        evac, sums = to_deepnorm()
        run_all(linear([(w_out[D:2 * D, :], lambda k: (y_high[:, k, :], y_low[:, k, :], t_y2[k])),
                        (w_out[0:D, :], X)], D, evac))
        block_norm(0, 0, sums)

        def cross_attention(li):
            stage()
            o = 0
            qT, o = area(o, KC, S)
            kT, o = area(o, KC, MEM)
            vv, o = area(o, 2, D)
            mem_high, o = area(o, KC, MEM, r=True)
            mem_low, o = area(o, KC, MEM, r=True)
            mem, o = area(o, 2, D)
            ws2, o = area(o, 4, MEM)
            PT2, o = area(o, 2, 2, S)
            t_m = small_dma(act, mem, A["mem_2"][0].rearrange("(t p) n -> p t n", p=P), *so_far())
            for k in range(0, KC, 2):
                i, b, free = att.take()
                for kk in range(2):
                    for t_ in range(2):
                        t = turn(b[:, kk * MEM + t_ * P:kk * MEM + (t_ + 1) * P], mem[:, t_, (k + kk) * P:(k + kk + 1) * P],
                                 t_m, free, signal=kk + t_ == 2)
                t_mt = att.free[i] = split_of(b[:, :].rearrange("p (a b) -> p a b", a=2), mem_high[:, k:k + 2, :],
                                              mem_low[:, k:k + 2, :], t)
            def to_vv(m, b, t):
                return copy(act, vv[:, :, m * P:(m + 1) * P], b[:, 0:MEM].rearrange("p (t c) -> p t c", t=2), t)

            M = lambda k: (mem_high[:, k, :], mem_low[:, k, :], t_mt)
            run_all(linear([(A["xa_w_v_2"][li], M)], D, by_tokens(to_vv, MEM), MEM))
            run_all(linear([(A["xa_w_k_2"][li], M)], D, to(kT), MEM))
            flush()
            run_all(linear([(A["xa_w_q_2"][li], X)], D, to(qT)))
            t_q = act.now
            ring = Ring([ws2[:, j, :] for j in range(4)])
            ptr = Ring([PT2[:, j, :, :] for j in range(2)])
            tiles = [(hd, qt) for hd in range(XA_HEADS) for qt in range(NT)]
            state = {}

            def first_half(hd, qt):
                i, b, free = att.take()
                t = mm_group(b[:, 0:MEM], [(qT[:, 2 * hd + j, qt * P:(qt + 1) * P], kT[:, 2 * hd + j, :]) for j in range(2)],
                             t_q, free)
                wi, w, wf = ring.take()
                si, st, sf = st_ring.take()
                t = dve.do(lambda e: e.tensor_reduce(st[:, 0:1], b[:, 0:MEM], AX.X, ALU.max, negate=True), t, sf)
                t = ts(dve, st[:, 1:2], st[:, 0:1], 256 ** -0.5, ALU.mult, t)
                t = att.free[i] = fn(w, b[:, 0:MEM], ACT.Exp, t, wf, bias=st[:, 1:2], scale=256 ** -0.5, accum=st[:, 2:3])
                t = recip(st[:, 3:4], st[:, 2:3], t)
                t = st_ring.free[si] = ts(dve, w, w, st[:, 3:4], ALU.mult, t)
                state[hd, qt] = (wi, w, t)

            def second_half(hd, qt):
                wi, w, tw = state.pop((hd, qt))
                if qt == 0:
                    state["pt"] = ptr.take()
                pi, pt, pf = state["pt"]
                i, b, free = att.take()
                for kt in range(2):
                    t = turn(b[:, kt * P:(kt + 1) * P], w[:, kt * P:(kt + 1) * P], tw, free, signal=kt == 1)
                ring.free[wi] = t
                t = att.free[i] = copy(act, pt[:, :, qt * P:(qt + 1) * P],
                                       b[:, 0:MEM].rearrange("p (a b) -> p a b", a=2), t, pf)
                if qt == NT - 1:
                    for e_ in range(2):
                        bi, b, free = lin.take()
                        m = 2 * hd + e_
                        t2 = mm_group(b[:, :], [(vv[:, kt, m * P:(m + 1) * P], pt[:, kt, :]) for kt in range(2)], t, free)
                        t_X[m] = lin.free[bi] = split_of(b[:, :], XH[:, m, :], XL[:, m, :], t2)
                    ptr.free[pi] = t2

            first_half(*tiles[0])
            for n in range(1, len(tiles)):
                first_half(*tiles[n])
                second_half(*tiles[n - 1])
            second_half(*tiles[-1])
            evac, sums = to_deepnorm()
            run_all(linear([(A["xa_w_o_2"][li], X)], D, evac))
            return sums

        def block_mlp(li):
            evac, sums = to_deepnorm()
            mlp(A["mlp_w1_2"][li], A["mlp_w2_2"][li], evac)
            return sums

        block_norm(0, 1, cross_attention(0))
        block_norm(0, 2, block_mlp(0))

        stage()
        w_odd = A["odd_w_in_2"][0]
        o = 0
        q_, o = area(o, 4, S)
        k_, o = area(o, 4, S)
        gv, o = area(o, NT, D)
        go, o = area(o, KC, S)
        kend, o = area(o, 4, S)
        kt_ = k_
        lg, o = area(o, S)
        bcs, o = area(o, 4, S)
        sca, o = area(o, 3, S)
        SG, o = area(o, 2, GLA_HEADS, 256)
        low, o = area(o, S)
        wg2, o = area(o, 512)
        KE = bcs
        gT, o = area(o, KC, S)
        dec, o = area(o, 4, 8)
        ATT = kend
        ev = so_far()
        t_wl = small_dma(act, wsmall[:, :, :], w_odd[:, OD_LOW:OD_LOW + GLA_RANK].rearrange("(k p) n -> p k n", p=P), *ev)
        t_wg = small_dma(act, wg2[0:GLA_RANK, :], A["odd_w_gate2_2"][0], *ev)
        bi, b, free = lin.take()
        t = mm_group(b[0:GLA_RANK, :], [(wsmall[:, k, :], h(k)) for k in range(KC)], t_wl, free, *t_hs)
        t_low = lin.free[bi] = copy(act, low[0:GLA_RANK, :], b[0:GLA_RANK, :], t)

        t_qk = {}

        def evac_q(m, b, t):
            t_qk["q", m] = copy(act, q_[:, m, :], b, t)
            return t_qk["q", m]

        def evac_k(m, b, t):
            t_qk["k", m] = copy(act, k_[:, m, :], b, t)
            return t_qk["k", m]

        odd_fill = chain(linear([(w_odd[:, OD_Q:OD_Q + 512], X)], 512, evac_q),
                         linear([(w_odd[:, OD_K:OD_K + 512], X)], 512, evac_k))
        t_b4 = [None] * 4
        for hd in range(4):
            i, b, free = att.take()
            t = mm_group(b[:, :], [(wg2[0:GLA_RANK, hd * P:(hd + 1) * P], low[0:GLA_RANK, :])], t_wg, t_low, free)
            x_ = lg[:, :]
            t = att.free[i] = ts(dve, x_, b[:, :], column("odd_b_gate_2", hd), ALU.add, t, t_b4[hd - 1] if hd else None)
            t = log1p_exp_minus(x_, sca[:, 0, :], sca[:, 1, :], sca[:, 2, :], sca[:, 2, :], t)
            t = stt(x_, x_, 0.0, sca[:, 2, :], ALU.min, ALU.subtract, t)
            t = ts(dve, x_, x_, 1.0 / 16.0, ALU.mult, t)
            t_b4[hd] = dve.do(lambda e, hd=hd: e.tensor_tensor_scan(bcs[:, hd, :], again, lg[:, :], 0.0, ALU.mult, ALU.add), t)
            step(odd_fill, 2)
        run_all(odd_fill)
        t_dec = copy(dve, dec, bcs.rearrange("p h (n c) -> p h n c", c=GLA_C)[:, :, :, GLA_C - 1], *t_b4)
        t_qt = [None] * 4
        t_kt = [None] * 4
        t_ke = [None] * 4
        def to_gv(m, b, t):
            return copy(act, gv[:, :, m * P:(m + 1) * P], b[:, :].rearrange("p (t c) -> p t c", t=NT), t)

        vfill = linear([(w_odd[:, OD_V:OD_V + D], X)], D, by_tokens(to_gv))
        for hd in range(4):
            s0, s1, s2 = (sca[:, j, :] for j in range(3))
            bh = bcs[:, hd, :]
            t0 = fn(s0, bh, ACT.Exp, *t_b4, dve.now)
            t_qt[hd] = stt(q_[:, hd, :], q_[:, hd, :], P ** -0.5, s0, ALU.mult, ALU.mult, t0, t_qk["q", hd])
            t_e = fn(s1, bh, ACT.Exp, scale=-1.0)
            t0 = tt(dve, s2.rearrange("p (n c) -> p n c", c=GLA_C), dec[:, hd, :].unsqueeze(2).to_broadcast([P, 8, GLA_C]),
                    bh.rearrange("p (n c) -> p n c", c=GLA_C), ALU.subtract, t_dec, act.now)
            t0 = fn(s2, s2, ACT.Exp, t0)
            t_ke[hd] = tt(dve, kend[:, hd, :], k_[:, hd, :], s2, ALU.mult, t0, t_qk["k", hd])
            t_kt[hd] = tt(dve, kt_[:, hd, :], k_[:, hd, :], s1, ALU.mult, t_e, t_ke[hd])
            step(vfill, 2)
        t_dec = fn(dec, dec, ACT.Exp, t_dec, *t_ke)
        run_all(vfill)
        flush()
        t_v = act.now
        t_g = {}

        def evac_go(m, b, t):
            t_g[m], t2 = silu_of(go[:, m, :], b, sca[:, m % 2, :], t, dve.now)
            return t2

        gfill = linear([(w_odd[:, OD_G:OD_G + D], X)], D, evac_go)
        for tt_ in range(NT):
            i, b, free = att.take()
            for hd in range(4):
                t = turn(b[:, hd * P:(hd + 1) * P], kend[:, hd, tt_ * P:(tt_ + 1) * P], free, t_ke[hd], signal=hd == 3)
            t_KE = att.free[i] = copy(act, KE[:, tt_, :], b[:, :], t, dve.now)
        t_at = [None] * NT
        for tt_ in range(NT):
            ts_ = slice(tt_ * P, (tt_ + 1) * P)
            i, b, free = att.take()
            for hd in range(4):
                t = mm(b[:, hd * P:(hd + 1) * P], kt_[:, hd, ts_], q_[:, hd, ts_], True, True,
                       t_kt[hd], t_qt[hd], free, signal=hd == 3)
            a4 = ATT[:, tt_, :].rearrange("p (a b) -> p a b", a=4)
            t = att.free[i] = copy(act, ATT[:, tt_, :], b[:, :], t, t_KE)
            t = pool.do(lambda e, a4=a4: e.affine_select(out=a4, in_=a4, compare_op=ALU.is_ge, fill=0.0, base=0,
                                                         pattern=[[0, 4], [1, P]], channel_multiplier=-1), t)
            a5 = a4[:, :, GLA_C:P]
            t_at[tt_] = pool.do(lambda e, a5=a5: e.affine_select(out=a5, in_=a5, compare_op=ALU.is_ge, fill=0.0, base=-GLA_C,
                                                                 pattern=[[0, 4], [0, GLA_C]], channel_multiplier=1), t)
            step(gfill)
        t_s = memset(dve, SG[:, 0, :, :], 0.0)
        t_og = [None] * NT
        rd = None
        t_cur = [t_s] * 4
        for tt_ in range(NT):
            ts_ = slice(tt_ * P, (tt_ + 1) * P)
            outs = [att.take(), att.take()]
            for half in range(2):
                n = 2 * tt_ + half
                hs = slice(half * GLA_C, (half + 1) * GLA_C)
                for e_ in range(8):
                    hd, vh = e_ // 2, e_ % 2
                    i, b, free = outs[e_ // 4]
                    dst = b[:, (e_ % 4) * P + half * GLA_C:(e_ % 4) * P + (half + 1) * GLA_C]
                    t = mm_group(dst, [
                        (gv[:, tt_, hd * 256 + vh * P:hd * 256 + (vh + 1) * P], ATT[:, tt_, hd * P + half * GLA_C:hd * P + (half + 1) * GLA_C]),
                        (SG[:, n % 2, hd, vh * P:(vh + 1) * P], q_[:, hd, tt_ * P + half * GLA_C:tt_ * P + (half + 1) * GLA_C]),
                    ], t_v, t_at[tt_], free, t_cur[hd])
                rd = t
                if n < 7:
                    for pr_ in range(2):
                        bi, b, free = lin.take()
                        for j in range(2):
                            hd = pr_ * 2 + j
                            t = mm(b[:, j * 256:(j + 1) * 256], KE[hs, tt_, hd * P:(hd + 1) * P],
                                   gv[hs, tt_, hd * 256:(hd + 1) * 256], True, True, free, t_KE, signal=j == 1)
                        for j in range(2):
                            hd = pr_ * 2 + j
                            t_cur[hd] = stt(SG[:, (n + 1) % 2, hd, :], SG[:, n % 2, hd, :], dec[:, hd, n:n + 1],
                                            b[:, j * 256:(j + 1) * 256], ALU.mult, ALU.add, t, t_dec, rd, t_cur[hd])
                        lin.free[bi] = t_cur[hd]
                step(gfill)
            for z in range(2):
                i, b, free = outs[z]
                t_og[tt_] = att.free[i] = copy(dve, gT[:, 4 * z:4 * z + 4, ts_], b[:, :].rearrange("p (a b) -> p a b", a=4), rd)
        run_all(gfill)
        for hd in range(4):
            r = rms_stats(lambda k: gT[:, k, :], [2 * hd, 2 * hd + 1], 256, 1, stat[:, 2, :], [t_og[-1]] * KC)
            for j in range(2):
                m = 2 * hd + j
                t = stt(gT[:, m, :], gT[:, m, :], column("odd_head_norm_g_2", j), stat[:, 2, :], ALU.mult, ALU.mult, r)
                stat_free[:] = [t]
                t = tt(dve, gT[:, m, :], gT[:, m, :], go[:, m, :], ALU.mult, t, t_g[m])
                t_X[m] = split_of(gT[:, m, :], XH[:, m, :], XL[:, m, :], t)
        evac, sums = to_deepnorm()
        run_all(linear([(A["odd_w_out_2"][0], X)], D, evac))
        block_norm(1, 0, sums)
        block_norm(1, 1, cross_attention(1))
        block_norm(1, 2, block_mlp(1), last=True)

        stage()
        ot, _ = area(0, NT, D)
        outs = []
        for t_ in range(NT):
            for half in range(2):
                i, b, free = att.take()
                for j in range(4):
                    t = turn(b[:, j * P:(j + 1) * P], hT[:, half * 4 + j, t_ * P:(t_ + 1) * P], *t_hs, free, signal=j == 3)
                t_o = att.free[i] = copy(act if half else dve, ot[:, t_, half * 512:(half + 1) * 512], b[:, :], t)
                outs.append(small_dma(sp, out[0, t_ * P:(t_ + 1) * P, half * 512:(half + 1) * 512],
                                      ot[:, t_, half * 512:(half + 1) * 512], t_o))
        sp.wait(*outs, t_sd)

        if schedule is None:
            return noted

        with nc.Block() as block:
            @block.sync
            def _(e):
                sp.run(e)

            @block.scalar
            def _(e):
                act.run(e)

            @block.vector
            def _(e):
                dve.run(e)

            @block.gpsimd
            def _(e):
                pool.run(e)

            @block.tensor
            def _(e):
                pe.run(e)


_INS = ['x', 'c', 'rel_bias', 'ada_w', 'ada_b', 'norm_mix', 'w_in', 'gate_b', 'diff_lambda', 'diff_subln',
        'dsa_kv_norm', 'dsa_w_uv', 'w_br_a', 'w_br_b', 'w_br_c', 'w_o', 'norm_mlp', 'w_ff1', 'w_ff2', 'norm_final',
        'mem_2', 'even_w_in_2', 'even_conv_w_2', 'even_conv_b_2', 'even_conv_ln_g_2', 'even_conv_ln_b_2',
        'even_ssm_conv_w_2', 'even_ssm_conv_b_2', 'even_dt_bias_2', 'even_a_log_2', 'even_d_skip_2',
        'even_ssm_norm_g_2', 'even_w_out_2', 'odd_w_in_2', 'odd_w_gate2_2', 'odd_b_gate_2', 'odd_head_norm_g_2',
        'odd_w_out_2', 'xa_w_q_2', 'xa_w_k_2', 'xa_w_v_2', 'xa_w_o_2', 'mlp_w1_2', 'mlp_w2_2', 'ln_g_2', 'ln_b_2']


def kernel(**inputs):
    import concourse.bacc as bacc
    from concourse.bass_utils import run_bass_kernel_spmd

    square, onehot = shape_constants()
    arrays = {f"in_{name}": np.ascontiguousarray(inputs[name]) for name in _INS}
    arrays["in_c_square"], arrays["in_c_onehot"] = square, onehot

    def described(schedule):
        nc = bacc.Bacc("TRN2", target_bir_lowering=False, num_devices=1)
        A = {key[3:]: nc.dram_tensor(key, a.shape, mybir.dt.from_np(a.dtype), kind="ExternalInput").ap()
             for key, a in arrays.items()}
        A["strip"] = nc.dram_tensor("strip", (12, 640), F32, kind="Internal").ap()
        out = nc.dram_tensor("out", (1, S, D), F32, kind="ExternalOutput").ap()
        return nc, program(nc, A, out, schedule)

    nc, _ = described(described(None)[1])
    r = run_bass_kernel_spmd(nc, [arrays], core_ids=[0])
    return r.results[0]["out"]
```

```python
import math
from contextlib import ExitStack

import numpy as np

import concourse.bass as bass
from concourse import mybir

F32 = mybir.dt.float32
F32R = mybir.dt.float32r
ALU = mybir.AluOpType
ACT = mybir.ActivationFunctionType
AX = mybir.AxisListType

P = 128
D = 1024
S = 512
KC = D // P
NT = S // P
NEG = -1.0e30
TAKEN = -3.0e38

HEADS_A = HEADS_B = HEADS_C = 4
DH = 64
IDX_HEADS = 8
IDX_DIM = 32
BUCKETS = 32
TOPK = min(256, S // 4)
FF = 4 * D
LAM_INIT = 0.8 - 0.6 * math.exp(0.0)

COL_AQ, COL_AK, COL_AV, COL_BQ = 0, 512, 1024, 1536
COL_BKV = 2048
COL_IQ = COL_BKV + 128
COL_IK = COL_IQ + 256
COL_IW = COL_IK + 32
COL_CQ = COL_IW + 8
COL_CK = COL_CQ + 256
COL_CV = COL_CK + 256
COL_G = COL_CV + 256

ALPHA = 4 ** 0.25
CONV_W = 31
SSM_CONV = 4
SSM_HEADS = 16
XBC = D + 2 * 2 * 128
XBC_C = XBC // P
EV_VAL, EV_GATE, EV_Z, EV_XBC, EV_DT = 0, D, 2 * D, 3 * D, 3 * D + XBC
GLA_HEADS = 4
GLA_C = 64
OD_Q, OD_K, OD_V, OD_G, OD_LOW = 0, 512, 1024, 2048, 3072
GLA_RANK = 16
MEM = 256
XA_HEADS = 4
WC = 128
RAW_SLOTS = 5
HIGH_SLOTS = 3
LOAD_AHEAD = RAW_SLOTS - 1
SPLIT_AHEAD = HIGH_SLOTS - 1
LEAD = 2
ARENA = 25728


def t5_bucket(n):
    n = np.maximum(n, 0)
    nf = np.maximum(n, 1).astype(np.float32)
    half = BUCKETS // 2
    large = half + (np.log(nf / np.float32(half)) / np.float32(math.log(128 / half)) * np.float32(half)).astype(np.int32)
    return np.where(n < half, n, np.minimum(large, BUCKETS - 1))


def shape_constants():
    i = np.arange(P)
    ident = np.eye(P, dtype=np.float32)
    upper = (i[:, None] <= i[None, :]).astype(np.float32)
    seg_mask = np.where(i[:, None] <= i[None, :], 0.0, NEG).astype(np.float32)
    again = np.tile((np.arange(S) % GLA_C != 0).astype(np.float32), (P, 1))
    causal = np.zeros((P, S), np.float32)
    causal[:, S - P:] = np.where(i[:, None] >= i[None, :], 0.0, NEG)
    square = np.concatenate([ident, upper, seg_mask, again, causal, ident[::-1]], axis=1)
    width = 640
    dist = (S - 1) - np.arange(width)
    onehot = np.zeros((BUCKETS + 1, width), np.float32)
    bucket = t5_bucket(dist)
    for m in range(width):
        onehot[bucket[m], m] = 1.0
    onehot[BUCKETS] = np.where(dist < 0, NEG, 0.0)
    return np.ascontiguousarray(square), onehot


class Queue:

    def __init__(self, sem):
        self.sem, self.count, self.jobs, self.waited = sem, 0, [], {}

    def wait(self, *tokens):
        for t in tokens:
            if t is None:
                continue
            if isinstance(t, list):
                self.wait(*t)
                continue
            sem, value = t
            if self.waited.get(id(sem), 0) < value:
                self.waited[id(sem)] = value
                self.jobs.append((sem, value, None))

    def do(self, make, *tokens, signal=True):
        self.wait(*tokens)
        if signal:
            self.count += 1
        self.jobs.append((self.sem if signal else None, 1, make))
        return (self.sem, self.count)

    def dma(self, sem, make, *tokens):
        self.wait(*tokens)
        sem.count += 16
        self.jobs.append((sem.sem, 16, make))
        return (sem.sem, sem.count)

    @property
    def now(self):
        return (self.sem, self.count) if self.count else None

    def run(self, eng):
        for sem, value, make in self.jobs:
            if make is None:
                eng.wait_ge(sem, value)
            elif sem is None:
                make(eng)
            else:
                make(eng).then_inc(sem, value)


class DmaCount:
    def __init__(self, sem):
        self.sem, self.count = sem, 0


class Ring:

    def __init__(self, bufs):
        self.bufs, self.free, self.n = bufs, [None] * len(bufs), 0

    def take(self):
        i = self.n % len(self.bufs)
        self.n += 1
        return i, self.bufs[i], self.free[i]


def program(nc, A, out, schedule):
    ctx = ExitStack()
    with ctx:
        def sb(name, shape):
            return ctx.enter_context(nc.sbuf_tensor(name, shape, F32))

        def semaphore(name):
            return ctx.enter_context(nc.semaphore(name))

        pe, act, dve, pool, sp = (Queue(semaphore("s_" + n)) for n in ("pe", "act", "dve", "pool", "sp"))

        def so_far():
            return [q.now for q in (pe, act, dve, pool)]

        def stage():
            t = so_far()
            for q in (act, dve, pool):
                q.wait(*t)

        hT = sb("hT", [P, KC, S])
        def sb_r(name, shape):
            return ctx.enter_context(nc.sbuf_tensor(name, shape, F32R))

        XH = sb_r("XH", [P, KC, S])
        XL = sb_r("XL", [P, KC, S])
        high_slots = [sb_r(f"wh{i}", [P, KC, WC]) for i in range(HIGH_SLOTS)]
        adat = sb("adat", [P, 2, P])

        def two_views(name, words):
            start = -(-nc.sbuf_base // 32) * 32
            sb(name, [P, words + 8])
            return (nc.alloc_sbuf_tensor_at(name + "_f", [P, words], F32, offset=start),
                    nc.alloc_sbuf_tensor_at(name + "_r", [P, words], F32R, offset=start))

        arena, arena_r = two_views("arena", ARENA)
        raw_slots = [two_views(f"w{i}", KC * WC) for i in range(RAW_SLOTS)]
        const = sb("const", [P, 4 * P + 2 * S])
        ones = sb("ones", [P, P])
        vec = sb("vec", [P, 6, P])
        wsmall = sb("wsmall", [P, KC, 16])
        stat = sb("stat", [P, 3, S])
        sq = sb("sq", [P, 2, S])
        eps_t = sb("eps", [P, 4])
        lamb = sb("lamb", [P, 3 * P])
        modc = sb("modc", [P, 7 * KC])
        soft = sb("soft", [P, 64])
        gates = sb("gates", [P, 2, S])[:, :, :]

        ident = const[:, 0:P]
        upper = const[:, P:2 * P]
        seg_mask = const[:, 2 * P:3 * P]
        again = const[:, 3 * P:3 * P + S]
        causal = const[:, 3 * P + S:3 * P + 2 * S]
        flip = const[:, 3 * P + 2 * S:4 * P + 2 * S]

        def area(off, *shape, r=False):
            n = int(np.prod(shape))
            assert off + n <= ARENA, (off, shape)
            v = (arena_r if r else arena)[:, off:off + n]
            if len(shape) == 2:
                v = v.rearrange("p (a b) -> p a b", a=shape[0])
            if len(shape) == 3:
                v = v.rearrange("p (a b c) -> p a b c", a=shape[0], b=shape[1])
            return v, off + n

        banks = [ctx.enter_context(nc.psum_tensor(f"ps{i}", [P, 512], F32)) for i in range(8)]
        lin = Ring(banks[0:4])
        att = Ring(banks[4:8])

        raw_sem = [DmaCount(semaphore(f"s_w{i}")) for i in range(RAW_SLOTS)]
        raw_free = [None] * RAW_SLOTS
        high_free = [None] * HIGH_SLOTS
        noted, loaded, split_done = [], [], []
        low_engine = [dve]
        tensors = {a.tensor.name: a.tensor for a in A.values()}

        def view(a, kc, cols):
            return a[:, 0:kc * cols].rearrange("p (k c) -> p k c", k=kc)

        def load_unit(n):
            dram = [bass.AP(tensors[name], offset, ap) for name, offset, ap in schedule[n][0]]
            i = n % RAW_SLOTS
            kc, cols = dram[0].shape[0] // P, sum(d.shape[1] for d in dram)
            c = 0
            for d in dram:
                dst = view(raw_slots[i][0], kc, cols)[:, :, c:c + d.shape[1]]
                src = d.rearrange("(k p) n -> p k n", p=P)
                t = sp.dma(raw_sem[i], lambda e, dst=dst, src=src: e.dma_start(dst, src), raw_free[i])
                c += d.shape[1]
            loaded.append((i, kc, cols, t))

        def split_unit(n):
            i, kc, cols, t = loaded[n]
            if not schedule[n][1]:
                split_done.append(None)
                return
            j = sum(1 for x in split_done if x) % HIGH_SLOTS
            hi = high_slots[j][:, :, :].rearrange("p k c -> p (k c)")[:, 0:kc * cols]
            t_h = act.do(lambda e: e.activation(hi, raw_slots[i][0][:, 0:kc * cols], ACT.Copy), t, high_free[j])
            t_l = low_engine[0].do(lambda e: e.tensor_tensor(raw_slots[i][1][:, 0:kc * cols], raw_slots[i][0][:, 0:kc * cols],
                                                             hi.bitcast(F32), ALU.subtract), t, t_h)
            split_done.append((j, [t_h, t_l]))

        def unit(*dram, split=True, ahead=True):
            n = len(noted)
            noted.append(([(d.tensor.name, d.offset, [list(x) for x in d.ap]) for d in dram], split))
            if schedule is None:
                kc, cols = dram[0].shape[0] // P, sum(d.shape[1] for d in dram)
                if not split:
                    return (lambda t: None), view(raw_slots[0][0], kc, cols), None
                return (lambda t: None), view(high_slots[0][:, :, :].rearrange("p k c -> p (k c)"), kc, cols), \
                    view(raw_slots[0][1], kc, cols), None
            while len(loaded) < min(n + 1 + LOAD_AHEAD * ahead, len(schedule)):
                load_unit(len(loaded))
            splits = sum(1 for _, is_split in schedule[n + 1:len(split_done)] if is_split)
            while len(split_done) < len(loaded) and (len(split_done) <= n or ahead and splits < SPLIT_AHEAD):
                splits += len(split_done) > n and schedule[len(split_done)][1]
                split_unit(len(split_done))
            i, kc, cols, t = loaded[n]
            if not split:
                def free_raw(t):
                    raw_free[i] = t
                return free_raw, view(raw_slots[i][0], kc, cols), t
            j, t = split_done[n]

            def free_both(t):
                raw_free[i] = high_free[j] = t
            return free_both, view(high_slots[j][:, :, :].rearrange("p k c -> p (k c)"), kc, cols), \
                view(raw_slots[i][1], kc, cols), t

        n_small = [0]

        def small_dma(q, dst, src, *tokens):
            n_small[0] += 1
            c = DmaCount(semaphore(f"s_d{n_small[0]}"))
            return q.dma(c, lambda e: e.dma_start(dst, src), *tokens)

        def mm(o, l, r, start, stop, *tokens, signal=False):
            return pe.do(lambda e: e.matmul(o, l, r, start=start, stop=stop), *tokens, signal=signal)

        def mm_group(o, pairs, *tokens):
            t = None
            for n, (l, r) in enumerate(pairs):
                last = n == len(pairs) - 1
                t = mm(o, l, r, n == 0, last, *(tokens if n == 0 else ()), signal=last)
            return t

        def turn(o, i, *tokens, signal=True):
            return pe.do(lambda e: e.transpose(o, i, ident[0:i.shape[0], 0:i.shape[0]]), *tokens, signal=signal)

        def copy(q, o, i, *t):
            if q is act:
                return q.do(lambda e: e.activation(o, i, ACT.Copy), *t)
            return q.do(lambda e: e.tensor_copy(o, i), *t)

        def fn(o, i, f, *t, bias=0.0, scale=1.0, accum=None):
            if accum is None:
                return act.do(lambda e: e.activation(o, i, f, bias=bias, scale=scale), *t)
            return act.do(lambda e: e.activation(o, i, f, bias=bias, scale=scale, accum_out=accum), *t)

        def tt(q, o, a, b, op, *t):
            return q.do(lambda e: e.tensor_tensor(o, a, b, op), *t)

        def ts(q, o, a, s1, op0, *t, s2=None, op1=None):
            if op1 is None:
                return q.do(lambda e: e.tensor_scalar(o, a, s1, None, op0), *t)
            return q.do(lambda e: e.tensor_scalar(o, a, s1, s2, op0, op1), *t)

        def stt(o, a, s, b, op0, op1, *t):
            return dve.do(lambda e: e.scalar_tensor_tensor(out=o, in0=a, scalar=s, in1=b, op0=op0, op1=op1), *t)

        def recip(o, i, *t):
            return dve.do(lambda e: e.reciprocal(o, i), *t)

        def memset(q, o, v, *t):
            return q.do(lambda e: e.memset(o, v), *t)

        t_const = small_dma(act, const[:, :], A["c_square"])
        t_ones = memset(dve, ones[:, :], 1.0)
        t_e1 = memset(dve, eps_t[:, 0:1], 1e-6)
        t_e2 = memset(dve, eps_t[:, 1:2], 1e-5)
        for q in (act, dve, pe):
            q.wait(t_const, t_ones, t_e1, t_e2)

        xin, o1 = area(0, NT, D)
        packs, o2 = area(o1, 6, P)
        t_x = small_dma(sp, xin, A["x"][0].rearrange("(t p) n -> p t n", p=P))
        pack_lists = [
            [("norm_mix", 8), ("gate_b", 24), ("norm_mlp", 8), ("norm_final", 8), ("diff_subln", 1),
             ("dsa_kv_norm", 1), ("ada_b", 48), ("c", 8)],
            [("even_conv_b_2", 8), ("even_conv_ln_g_2", 8), ("even_conv_ln_b_2", 8),
             ("even_ssm_conv_b_2", 12), ("even_ssm_norm_g_2", 8), ("even_ssm_conv_w_2", 48),
             ("odd_b_gate_2", 4), ("odd_head_norm_g_2", 2)],
            [("ln_g_2", 48), ("ln_b_2", 48)],
        ]
        col = {}
        t_zero = memset(pool, packs, 0.0)
        t_packs = [[] for _ in range(5)]
        for n, names in enumerate(pack_lists):
            at = 0
            for name, rows in names:
                a = A[name]
                while len(a.shape) > 1:
                    a = a.rearrange("a b ... -> (a b) ...") if len(a.shape) > 2 else a.rearrange("a b -> (a b)")
                t_packs[n].append(small_dma(act if n else sp, packs[at:at + rows, n, :],
                                            a.rearrange("(r p) -> r p", p=P), t_zero))
                col[name] = (n, at)
                at += rows
        conv_rows = A["even_conv_w_2"][0].rearrange("t (m p) -> (t m) p", p=P)
        t_packs[3].append(small_dma(act, packs[:, 3, :], conv_rows[0:P, :], t_zero))
        t_packs[4].append(small_dma(act, packs[0:CONV_W * KC - P, 4, :], conv_rows[P:CONV_W * KC, :], t_zero))
        def turn_pack(n):
            i, b, free = att.take()
            t = turn(b[:, 0:P], packs[:, n, :], *t_packs[n], free)
            att.free[i] = copy(dve, vec[:, n, :], b[:, 0:P], t)
            return att.free[i]

        def column(name, m=0):
            n, at = col[name]
            return vec[:, n, at + m:at + m + 1]

        def columns(name, m, k):
            n, at = col[name]
            return vec[:, n, at + m:at + m + k]

        def conv_tap(t, m):
            r = t * KC + m
            return vec[:, 3 + r // P, r % P:r % P + 1]

        t_vec = turn_pack(0)
        cond = modc[:, 6 * KC:7 * KC].unsqueeze(2)
        ct = cond[:, :, 0]
        t = fn(ct, columns("c", 0, KC), ACT.Tanh, t_vec, scale=0.5)
        t = stt(ct, ct, 1.0, columns("c", 0, KC), ALU.add, ALU.mult, t)
        t_cond = ts(dve, ct, ct, 0.5, ALU.mult, t)

        t_hx = []
        for k in range(KC):
            i, b, free = att.take()
            for t in range(NT):
                tok = turn(b[:, t * P:(t + 1) * P], xin[:, t, k * P:(k + 1) * P], t_x, free, signal=t == NT - 1)
            att.free[i] = copy(act, hT[:, k, :], b[:, :], tok)
            t_hx.append(att.free[i])
        for n in range(1, 5):
            t_vec = turn_pack(n)
        for q in (act, dve, pe, pool):
            q.wait(t_vec)

        def products(bank, hi, lo, x, first, last, t_w, free, cols=None):
            kc = hi.shape[1]
            for k in range(kc):
                xh, xl, tx = x(k)
                start = first and k == 0
                end = last and k == kc - 1
                mm(bank, hi[:, k, :], xh, start, False, t_w, free if start else None, tx)
                mm(bank, hi[:, k, :], xl, False, False)
                t = mm(bank, lo[:, k, :], xh, False, end, signal=k == kc - 1)
            return t

        def linear(parts, n_cols, evac, n=S, lead=False):
            group = 1 if len(parts) == 1 else 4
            begin, ends = 0, []
            if lead:
                (dram, x), = parts
                begin = LEAD
                us = [unit(dram[:, m * P:(m + 1) * P], ahead=m == 0) for m in range(LEAD)]
                took = [lin.take() for _ in us]
                for k in range(dram.shape[0] // P):
                    xh, xl, tx = x(k)
                    last = k == dram.shape[0] // P - 1
                    for (done, hi, lo, t_w), (bi, b, free) in zip(us, took):
                        mm(b[:, 0:n], hi[:, k, :], xh, k == 0, False, t_w, free if k == 0 else None, tx)
                        mm(b[:, 0:n], hi[:, k, :], xl, False, False)
                        t = mm(b[:, 0:n], lo[:, k, :], xh, False, last, signal=last)
                        if last:
                            done(t)
                            ends.append(t)
                for m, (bi, b, free) in enumerate(took):
                    lin.free[bi] = evac(m, b[:, 0:n], ends[m])
                    yield
            for m0 in range(begin, n_cols // P, group):
                took = []
                for pi, (dram, x) in enumerate(parts):
                    for j in range(group):
                        m = m0 + j
                        if pi == 0:
                            took.append(lin.take())
                        bi, b, free = took[j]
                        done, hi, lo, t_w = unit(dram[:, m * P:(m + 1) * P])
                        t = products(b[:, 0:n], hi, lo, x, pi == 0, pi == len(parts) - 1, t_w, free)
                        done(t)
                        if pi == len(parts) - 1:
                            lin.free[bi] = evac(m, b[:, 0:n], t)
                        yield

        def split_of(src, hi, lo, *tokens):
            t_h = act.do(lambda e: e.activation(hi, src, ACT.Copy), *tokens)
            t_l = dve.do(lambda e: e.tensor_tensor(lo, src, hi.bitcast(F32), ALU.subtract), t_h, *tokens)
            return [t_h, t_l]

        t_X = [None] * KC
        X = lambda k: (XH[:, k, :], XL[:, k, :], t_X[k])

        turn_ring = Ring([gates[:, j, :] for j in range(2)])
        waiting = []

        def flush():
            while waiting:
                waiting.pop(0)()

        def by_tokens(store, n=S):
            def evac(m, b, t):
                gi, g, gf = turn_ring.take()
                t_g = copy(act, g[:, 0:n], b, t, gf)

                def later():
                    i, b2, free = att.take()
                    for j in range(n // P):
                        t2 = turn(b2[:, j * P:(j + 1) * P], g[:, j * P:(j + 1) * P], t_g, free, signal=j == n // P - 1)
                    turn_ring.free[gi] = t2
                    att.free[i] = store(m, b2, t2)
                if waiting:
                    waiting.pop(0)()
                waiting.append(later)
                return t_g
            return evac

        def run_all(gen):
            for _ in gen:
                pass

        def step(gen, n=1):
            for _ in range(n):
                if next(gen, "end") == "end":
                    return

        def chain(*gens):
            for g in gens:
                yield from g

        sq_ring = Ring([sq[:, 0, :], sq[:, 1, :]])

        def rstd_of(ss_bank, t_ss, n, eps_col, o, mean_sq=None, *tokens):
            if mean_sq is None:
                t = fn(o, ss_bank, ACT.Ln, t_ss, *tokens, bias=eps_t[0:o.shape[0], eps_col:eps_col + 1], scale=1.0 / n)
            else:
                t = stt(o, ss_bank, 1.0 / n, mean_sq, ALU.mult, ALU.subtract, t_ss, *tokens)
                t = fn(o, o, ACT.Ln, t, bias=eps_t[:, eps_col:eps_col + 1])
            return fn(o, o, ACT.Exp, t, scale=-0.5), t

        acc_s, acc_q = stat[:, 0, :], stat[:, 1, :]

        class Sums:

            def __init__(self, want_sum):
                self.n, self.want_sum, self.t_s, self.t_q = 0, want_sum, None, None
                self.first, self.free = None, None

            def add(self, src, tok):
                self.n += 1
                if self.n == 1:
                    self.first, self.free = (src, tok), list(stat_free)
                    self.t_q = fn(acc_q, src, ACT.Square, tok, *self.free)
                    self.t_s = tok
                    return
                i, s, f = sq_ring.take()
                t = fn(s, src, ACT.Square, tok, f)
                self.t_q = sq_ring.free[i] = tt(dve, acc_q, acc_q, s, ALU.add, t, self.t_q)
                if self.want_sum:
                    a = self.first[0] if self.n == 2 else acc_s
                    self.t_s = tt(pool, acc_s, a, src, ALU.add, tok, self.t_s, self.free)

            def over_partitions(self, acc, t):
                i, b, free = att.take()
                t = mm(b[:, :], ones[:, :], acc, True, True, t, free, signal=True)
                return i, b, t

        def rms_stats(src, chunks, n, eps_col, o, tokens):
            sums = Sums(False)
            for k in chunks:
                sums.add(src(k), tokens[k])
            return rms_of(sums, n, eps_col, o)

        def rms_of(sums, n, eps_col, o):
            i, b, t = sums.over_partitions(acc_q, sums.t_q)
            r, freed = rstd_of(b[:, :], t, n, eps_col, o)
            att.free[i] = freed
            return r

        def layer_norm(src, sums, g, finish):
            i1, b1, t_m = sums.over_partitions(acc_s, sums.t_s)
            i2, b2, t_v = sums.over_partitions(acc_q, sums.t_q)
            mean, msq, rstd = (stat[:, j, :] for j in range(3))
            tm = ts(dve, mean, b1[:, :], 1.0 / D, ALU.mult, t_m)
            att.free[i1] = tm
            t3 = tt(dve, msq, mean, mean, ALU.mult, tm, t_v)
            r, fr = rstd_of(b2[:, :], t_v, D, 1, rstd, msq, t3)
            att.free[i2] = fr
            t1s = [tt(dve if k < 3 else pool, src(k), src(k), mean, ALU.subtract, tm, t_m, t_v) for k in range(KC)]
            t2 = [None] * KC
            for k in range(KC):
                t2[k] = stt(src(k), src(k), g(k), rstd, ALU.mult, ALU.mult, t1s[k], r)
                if k:
                    finish(k - 1, src(k - 1), t2[k - 1])
                yield
            stat_free[:] = [t2[-1], t1s[-1]]
            finish(KC - 1, src(KC - 1), t2[-1])

        stat_free = []

        ada_ring = Ring([adat[:, j, :] for j in range(2)])

        def ada(m0, m1):
            summed = None

            def finish(m, ri, a, t):
                ai, ab, af = att.take()
                ada_ring.free[ri] = t = mm(ab[:, 0:1], a, ones[:, 0:1], True, True, t, af, signal=True)
                t_mod[0] = att.free[ai] = tt(dve, modc[:, m:m + 1], ab[:, 0:1], column("ada_b", m), ALU.add, t)

            for m in range(m0, m1):
                if summed:
                    finish(*summed)
                done, w, t = unit(A["ada_w"][0][:, m * P:(m + 1) * P], split=False)
                ri, a, rf = ada_ring.take()
                t = ts(dve, a, w[:, 0, :], cond[:, 0, :], ALU.mult, t, rf, t_cond)
                for k in range(1, KC):
                    t = stt(a, w[:, k, :], cond[:, k, :], a, ALU.mult, ALU.add, t)
                done(t)
                summed = m, ri, a, t
                yield
            finish(*summed)

        def ada_first(m1):
            ai, ab, af = lin.take()
            summed = None
            for m in range(m1):
                done, w, t = unit(A["ada_w"][0][:, m * P:(m + 1) * P], split=False)
                if m % 2:
                    done(mm_group(ab[:, m:m + 1], [(w[:, k, :], cond[:, k, :]) for k in range(KC)], t, t_cond, af))
                    ri, a, t = summed
                    ada_ring.free[ri] = t_last = mm(ab[:, m - 1:m], a, ones[:, 0:1], True, True, t, signal=True)
                else:
                    ri, a, rf = ada_ring.take()
                    t = ts(dve, a, w[:, 0, :], cond[:, 0, :], ALU.mult, t, rf, t_cond)
                    for k in range(1, KC):
                        t = stt(a, w[:, k, :], cond[:, k, :], a, ALU.mult, ALU.add, t)
                    done(t)
                    summed = ri, a, t
                yield
            t_mod[0] = lin.free[ai] = tt(dve, modc[:, 0:m1], ab[:, 0:m1], columns("ada_b", 0, m1), ALU.add, t_last)

        t_mod = [None]
        shift = lambda i, m: modc[:, 24 * i + m:24 * i + m + 1]

        def modulated_gain(i, name):
            s = modc[:, 24 * i + 8:24 * i + 16]
            return stt(s, s, 1.0, columns(name, 0, 8), ALU.add, ALU.mult, t_mod[0])

        def modulated_norm(i, name, r):
            t_g = modulated_gain(i, name)
            def scaled(k):
                si, s_, sf = sq_ring.take()
                t = stt(s_, hT[:, k, :], modc[:, 24 * i + 8 + k:24 * i + 9 + k], stat[:, 0, :],
                        ALU.mult, ALU.mult, r, t_g, sf)
                stat_free[:] = [t]
                return si, s_, t

            ahead = scaled(0)
            for k in range(KC):
                si, s_, t = ahead
                if k < KC - 1:
                    ahead = scaled(k + 1)
                sh = shift(i, k)
                t_h = act.do(lambda e, s_=s_, sh=sh, k=k: e.activation(XH[:, k, :], s_, ACT.Identity, bias=sh, scale=1.0), t)
                t_l = dve.do(lambda e, s_=s_, sh=sh, k=k: e.scalar_tensor_tensor(
                    out=XL[:, k, :], in0=s_, scalar=sh, in1=XH[:, k, :].bitcast(F32), op0=ALU.add, op1=ALU.subtract), t_h)
                t_X[k] = sq_ring.free[si] = [t_h, t_l]

        sums = Sums(False)
        for k in range(KC):
            sums.add(hT[:, k, :], t_hx[k])
        r_mix = rms_of(sums, D, 0, stat[:, 0, :])

        o = 0
        aq, o = area(o, 4, S)
        ak, o = area(o, 4, S)
        av, o = area(o, NT, 512)
        bq, o = area(o, 4, S)
        kvT, o = area(o, S)
        kv, o = area(o, NT, P)
        O_IQ = o
        iq, o = area(o, 2, S)
        ik, o = area(o, S)
        O_CQ = o
        cq, o = area(o, 2, S)
        ck, o = area(o, 2, S)
        cv, o = area(o, NT, 4, P)
        O_BIAS = o
        bias, o = area(o, 12, S)
        ws, o = area(o, 4, S)
        PT, o = area(o, NT, S)
        iw, o = area(o, NT, 8)
        top8, o = area(o, 8)
        w_in = A["w_in"][0]
        pick = stat

        table = lamb[0:BUCKETS + 1, 0:12]
        t0 = memset(dve, lamb[BUCKETS:BUCKETS + 1, 0:12], 1.0)
        t_tab = small_dma(sp, lamb[0:BUCKETS, 0:12], A["rel_bias"])
        oneh = ws[0:BUCKETS + 1, 0:2, :].rearrange("p a b -> p (a b)")[:, 0:640]
        t_one = small_dma(sp, oneh, A["c_onehot"])
        strip = PT[0:12, 0:2, :].rearrange("p a b -> p (a b)")[:, 0:640]
        for c0, c1 in ((0, 512), (512, 640)):
            i, b, free = att.take()
            t = mm_group(b[0:12, 0:c1 - c0], [(table, oneh[:, c0:c1])], t_tab, t_one, t0, free)
            t_s = att.free[i] = copy(act, strip[:, c0:c1], b[0:12, 0:c1 - c0], t)
        t_sd = small_dma(pool, A["strip"], strip, t_s)
        first = ada_first(16)
        flip_ring = Ring([cv[:, j, :, :].rearrange("p a b -> p (a b)") for j in range(NT)])
        flips = []
        t_bias = [None]

        def flip_over(fi, fb, t, h):
            i, b, free = att.take()
            t = flip_ring.free[fi] = mm_group(b[:, :], [(flip, fb)], t, free)
            t_bias[0] = att.free[i] = copy(act, bias[:, h, :], b[:, :], t)

        for h in range(12):
            src = bass.AP(A["strip"].tensor, h * 640, [[1, P], [1, S]])
            fi, fb, ff = flip_ring.take()
            flips.append((fi, fb, small_dma(pool, fb, src, t_sd, ff), h))
            step(first)
            if h == 0:
                step(first, 3)
            else:
                flip_over(*flips.pop(0))
        flip_over(*flips.pop(0))
        run_all(first)
        dve.wait(t_bias[0])
        modulated_norm(0, "norm_mix", r_mix)
        act.wait(t_sd)

        dl = lamb[:, P:P + 256]
        t = small_dma(pool, dl, A["diff_lambda"].rearrange("a b c -> a (b c)").to_broadcast([P, 256]))
        pr = lamb[:, 32:96]
        lam = lamb[:, 96:100]
        for j in range(2):
            t = tt(dve, pr, dl[:, j * 128:j * 128 + 64], dl[:, j * 128 + 64:j * 128 + 128], ALU.mult, t)
            t = dve.do(lambda e, j=j: e.tensor_reduce(lam[:, j:j + 1], pr, AX.X, ALU.add), t)
        t = fn(lam[:, 0:2], lam[:, 0:2], ACT.Exp, t)
        t = tt(dve, lam[:, 2:3], lam[:, 1:2], lam[:, 0:1], ALU.subtract, t)
        t_lam = ts(dve, lam[:, 2:3], lam[:, 2:3], -LAM_INIT, ALU.add, t)
        sub_g = lam[:, 3:4]
        t_subg = ts(dve, sub_g, column("diff_subln"), 1.0 - LAM_INIT, ALU.mult)

        def to(dst, q=None):
            def evac(m, b, t):
                return copy(q or act, dst[:, m, :], b, t)
            return evac

        def to_av(m, b, t):
            return copy(act, av[:, :, m * P:(m + 1) * P], b[:, :].rearrange("p (t c) -> p t c", t=NT), t)

        mod_fill = ada(16, 48)
        for n, _ in enumerate(chain(linear([(w_in[:, COL_AV:COL_AV + 512], X)], 512, by_tokens(to_av), lead=True),
                                    linear([(w_in[:, COL_AQ:COL_AQ + 512], X)], 512, to(aq)),
                                    linear([(w_in[:, COL_AK:COL_AK + 512], X)], 512, to(ak)))):
            if n > LEAD:
                step(mod_fill)
        flush()
        t_a = act.now

        t_cvz = memset(pool, cv, 0.0, pe.now)
        t_iw = [None]

        def evac_kv(m, b, t):
            return copy(act, kvT[:, :], b, t)

        def to_cv(m, b, t):
            src = b[:, :].rearrange("p (t c) -> p t c", t=NT)
            for par in range(2):
                last = copy(act, cv[:, :, 2 * m + par, par * DH:(par + 1) * DH], src[:, :, par * DH:(par + 1) * DH], t, t_cvz)
            return last

        def index_small():
            bi, b, free = lin.take()
            done, hi, lo, t_w = unit(*[w_in[:, COL_IK:COL_IK + IDX_DIM]] * 4)
            t = products(b[:, :], hi, lo, X, True, True, t_w, free)
            done(t)
            lin.free[bi] = copy(act, ik[:, :], b[:, :], t)
            yield
            bi, b, free = lin.take()
            done, hi, lo, t_w = unit(w_in[:, COL_IW:COL_IW + 8])
            for tt_ in range(NT):
                o_ = b[:, tt_ * 8:tt_ * 8 + 8]
                for k in range(KC):
                    xh, xl = (a[:, k, tt_ * P:(tt_ + 1) * P] for a in (XH, XL))
                    mm(o_, xh, hi[:, k, :], k == 0, False, t_w, free)
                    mm(o_, xl, hi[:, k, :], False, False)
                    t = mm(o_, xh, lo[:, k, :], False, k == KC - 1, signal=k == KC - 1)
            done(t)
            t_iw[0] = lin.free[bi] = ts(dve, iw, b[:, 0:32].rearrange("p (a b) -> p a b", a=NT),
                                        IDX_HEADS ** -0.5 * IDX_DIM ** -0.5, ALU.mult, t)
            yield

        fill = chain(
            linear([(w_in[:, COL_CV:COL_CV + 256], X)], 256, by_tokens(to_cv)),
            linear([(w_in[:, COL_BQ:COL_BQ + 512], X)], 512, to(bq)),
            linear([(w_in[:, COL_BKV:COL_BKV + P], X)], P, evac_kv),
            linear([(w_in[:, COL_IQ:COL_IQ + 256], X)], 256, to(iq)),
            index_small(),
            linear([(w_in[:, COL_CQ:COL_CQ + 256], X)], 256, to(cq)),
            linear([(w_in[:, COL_CK:COL_CK + 256], X)], 256, to(ck)),
        )

        ws_ring = Ring([ws[:, j, :] for j in range(4)])
        st_ring = Ring([soft[:, 4 * j:4 * j + 4] for j in range(8)])
        pt_free = [None]
        pt_written = {}

        def causal_softmax(q, k, qt, scale, hb, *tokens, extra=None):
            L = (qt + 1) * P
            i, b, free = att.take()
            t = mm(b[:, 0:L], q, k, True, True, free, *tokens, signal=True)
            wi, w, wf = ws_ring.take()
            si, st, sf = st_ring.take()
            w = w[:, 0:L]
            t = att.free[i] = stt(w, b[:, 0:L], scale, bias[:, hb, S - L:S], ALU.mult, ALU.add, t, wf, sf)
            if extra is not None:
                t = tt(dve, w, w, extra, ALU.add, t)
            t = dve.do(lambda e: e.tensor_reduce(st[:, 0:1], w, AX.X, ALU.max, negate=True), t)
            t = fn(w, w, ACT.Exp, t, bias=st[:, 0:1], accum=st[:, 1:2])
            t_r = recip(st[:, 2:3], st[:, 1:2], t)
            return w, wi, st, si, t_r

        def turn_rows(w, wi, qt, t_w, first):
            i, b, free = att.take()
            for kt in range(qt + 1):
                t = turn(b[:, kt * P:(kt + 1) * P], w[:, kt * P:(kt + 1) * P], t_w, free, signal=kt == qt)
            ws_ring.free[wi] = t
            t = att.free[i] = copy(act, PT[:, 0:qt + 1, qt * P:(qt + 1) * P],
                                   b[:, 0:(qt + 1) * P].rearrange("p (a b) -> p a b", b=P), t, pt_free[0])
            return t

        def weigh(b, v, free, first, last, t_pt):
            for kt in range(NT):
                t = mm(b[:, kt * P:S], v(kt), PT[:, kt, kt * P:S], first and kt == 0, last and kt == NT - 1,
                       t_pt, free if kt == 0 else None, signal=kt == NT - 1)
            pt_free[0] = t
            return t

        def pipelined(tiles, begin, end):
            before = None
            for tile in tiles:
                begin(tile)
                yield
                if before is not None:
                    end(before)
                before = tile
            yield
            end(before)

        live = {}
        post = []

        def diff_begin(tile):
            h, qt = tile
            while post:
                post.pop(0)()
            two = [causal_softmax(aq[DH * m:DH * (m + 1), h, qt * P:(qt + 1) * P],
                                  ak[DH * m:DH * (m + 1), h, 0:(qt + 1) * P], qt, DH ** -0.5, h, t_a)
                   for m in range(2)]
            (w0, i0, s0, j0, r0), (w1, i1, s1, j1, r1) = two
            t = tt(dve, s1[:, 3:4], s1[:, 2:3], lam[:, 2:3], ALU.mult, r1, t_lam)
            t0 = ts(dve, w0, w0, s0[:, 2:3], ALU.mult, r0)
            t = stt(w0, w1, s1[:, 3:4], w0, ALU.mult, ALU.add, t, t0)
            ws_ring.free[i1] = t
            st_ring.free[j0] = st_ring.free[j1] = t
            live[tile] = (w0, i0, t)

        def diff_end(tile):
            h, qt = tile
            w0, i0, t = live.pop(tile)
            t_pt = turn_rows(w0, i0, qt, t, qt == 0)
            if qt < NT - 1:
                return
            i, b, free = att.take()
            t = weigh(b, lambda kt: av[:, kt, h * P:(h + 1) * P], free, True, True, t_pt)
            t_o = att.free[i] = copy(dve, aq[:, h, :], b[:, :], t)

            def norm():
                r = rms_stats(lambda k: aq[:, h, :], [0], P, 0, stat[:, 0, :], [t_o])
                t = stt(aq[:, h, :], aq[:, h, :], sub_g, stat[:, 0, :], ALU.mult, ALU.mult, r, t_subg)
                stat_free[:] = [t]
                t_ya[h] = split_of(aq[:, h, :], bias_r[:, h, :], aq_r[:, h, :], t)
            post.append(norm)

        bias_r = area(O_BIAS, 12, S, r=True)[0]
        aq_r = area(0, 4, S, r=True)[0]
        cq_r = area(O_CQ, 2, S, r=True)[0]
        ob_r = area(O_IQ, 2, S, r=True)[0]
        t_ya = [None] * 4
        low_engine[0] = pool
        for _ in pipelined([(h, qt) for h in range(HEADS_A) for qt in range(NT)], diff_begin, diff_end):
            step(fill)
            step(mod_fill)
        post.pop(0)()
        run_all(fill)
        flush()
        t_proj = so_far()

        r = rms_stats(lambda k: kvT[:, :], [0], P, 0, stat[:, 0, :], t_proj[1:2])
        t_kv = stt(kvT[:, :], kvT[:, :], column("dsa_kv_norm"), stat[:, 0, :], ALU.mult, ALU.mult, r)
        stat_free[:] = [t_kv]
        i, b, free = att.take()
        for t_ in range(NT):
            t = turn(b[:, t_ * P:(t_ + 1) * P], kvT[:, t_ * P:(t_ + 1) * P], t_kv, free, signal=t_ == NT - 1)
        t_kv = att.free[i] = copy(act, kv, b[:, :].rearrange("p (a b) -> p a b", b=P), t)

        def index_scores():
            for qt in range(1, NT):
                L = (qt + 1) * P
                acc = pick[:, qt - 1, 0:L]
                t_acc = None
                for h in range(IDX_HEADS):
                    i, b, free = att.take()
                    r0 = IDX_DIM * (h % 4)
                    t = mm(b[:, 0:L], iq[r0:r0 + IDX_DIM, h // 4, qt * P:(qt + 1) * P],
                           ik[r0:r0 + IDX_DIM, 0:L], True, True, free, *t_proj, signal=True)
                    wi, w, wf = ws_ring.take()
                    t = att.free[i] = fn(w[:, 0:L], b[:, 0:L], ACT.Relu, t, wf)
                    if h == 0:
                        prev = causal[:, S - L:S]
                        t_acc = ts(dve, acc, w[:, 0:L], iw[:, qt, h:h + 1], ALU.mult, t, t_iw[0])
                    else:
                        t_acc = stt(acc, w[:, 0:L], iw[:, qt, h:h + 1], acc, ALU.mult, ALU.add, t, t_acc)
                    ws_ring.free[wi] = t_acc
                    if h % 4 == 3:
                        yield
                t_acc = tt(dve, acc, acc, causal[:, S - L:S], ALU.add, t_acc)
                t_pick[qt] = t_acc

        t_pick = [None] * NT

        def topk_rounds():
            for qt in range(1, NT):
                L = (qt + 1) * P
                acc = pick[:, qt - 1, 0:L]
                t = t_pick[qt]
                for r in range(TOPK // 8):
                    t = dve.do(lambda e, acc=acc: e.max(top8[:, :], acc), t)
                    t = dve.do(lambda e, acc=acc: e.match_replace(acc, top8[:, :], acc, TAKEN), t)
                    yield
                t_pick[qt] = ts(dve, acc, acc, 2.0 * NEG * 1e8, ALU.is_gt, t, s2=NEG, op1=ALU.mult)

        merged = arena[:, 2048:2048 + 8 * S].rearrange("p (a b) -> p a b", a=KC)
        gate_ring = Ring([gates[:, j, :] for j in range(2)])
        t_merged = [None] * KC

        def branch(n, weights, x_chunks):
            for m in range(KC):
                    c0 = COL_G + n * D + m * P
                    bi, b, free = lin.take()
                    done, hi, lo, t_w = unit(w_in[:, c0:c0 + P])
                    t = products(b[:, :], hi, lo, X, True, True, t_w, free)
                    done(t)
                    gi, g, gf = gate_ring.take()
                    tg = lin.free[bi] = fn(g, b[:, :], ACT.Tanh, t, gf, t_half, bias=gbh[:, n * 8 + m:n * 8 + m + 1], scale=0.5)
                    tg = ts(pool, g, g, 0.5, ALU.mult, tg, s2=0.5, op1=ALU.add)
                    yield
                    bi, b, free = lin.take()
                    done, hi, lo, t_w = unit(weights[:, m * P:(m + 1) * P])
                    t = products(b[:, :], hi, lo, x_chunks, True, True, t_w, free)
                    done(t)
                    if n == 0:
                        t = tt(dve, merged[:, m, :], b[:, :], g, ALU.mult, t, tg)
                        t_merged[m] = gate_ring.free[gi] = lin.free[bi] = t
                    else:
                        t = lin.free[bi] = tt(dve, g, b[:, :], g, ALU.mult, t, tg)
                        t_merged[m] = gate_ring.free[gi] = tt(pool, merged[:, m, :], merged[:, m, :], g, ALU.add,
                                                              t, t_merged[m])
                    yield

        gbh = sb("gbh", [P, 24])
        t_half = ts(dve, gbh[:, :], columns("gate_b", 0, 24), 0.5, ALU.mult)

        def block_begin(tile):
            h, qt = tile
            g, par = h // 2, h % 2
            w, wi, st, si, t = causal_softmax(
                cq[DH * par:DH * (par + 1), g, qt * P:(qt + 1) * P],
                ck[DH * par:DH * (par + 1), g, 0:(qt + 1) * P], qt, DH ** -0.5, 8 + h, *t_proj)
            t = st_ring.free[si] = fn(w, w, ACT.Copy, t, scale=st[:, 2:3])
            live[tile] = (w, wi, t)

        def block_end(tile):
            h, qt = tile
            g, par = h // 2, h % 2
            w, wi, t = live.pop(tile)
            t_pt = turn_rows(w, wi, qt, t, qt == 0)
            if qt < NT - 1:
                return
            if par == 0:
                live["out"] = att_out.take()
            oi, ob, of = live["out"]
            t = weigh(ob, lambda kt: cv[:, kt, h, :], of if par == 0 else None, par == 0, par == 1, t_pt)
            if par == 1:
                t_c[g] = att_out.free[oi] = split_of(ob[:, :], bias_r[:, 8 + g, :], cq_r[:, g, :], t)

        att.bufs, att.free = banks[4:7], att.free[:3]
        att.n = 0
        att.free = [so_far()] * 3
        att_out = Ring([banks[7]])
        att_out.free = [so_far()]
        t_c = [None, None]
        t_b = [None] * 4

        def latent_begin(tile):
            h, qt = tile
            extra = pick[:, qt - 1, 0:(qt + 1) * P] if qt else None
            w, wi, st, si, t = causal_softmax(
                bq[:, h, qt * P:(qt + 1) * P], kvT[:, 0:(qt + 1) * P], qt, P ** -0.5, 4 + h,
                *t_proj, t_kv, t_pick[qt] if qt else None, extra=extra)
            t = st_ring.free[si] = fn(w, w, ACT.Copy, t, scale=st[:, 2:3])
            live[tile] = (w, wi, t)

        def latent_end(tile):
            h, qt = tile
            w, wi, t = live.pop(tile)
            t_pt = turn_rows(w, wi, qt, t, qt == 0)
            if qt == NT - 1:
                oi, ob, of = att_out.take()
                t = weigh(ob, lambda kt: kv[:, kt, :], of, True, True, t_pt)
                t_b[h] = att_out.free[oi] = copy(dve, bq[:, h, :], ob[:, :], t)

        tiles = [(h, qt) for h in range(4) for qt in range(NT)]
        filler = branch(0, A["w_br_a"][0], lambda k: (bias_r[:, k, :], aq_r[:, k, :], t_ya[k]))
        tops = topk_rounds()
        for _ in index_scores():
            step(filler)
        for _ in pipelined(tiles, block_begin, block_end):
            step(tops, 3)
            step(filler)
        run_all(tops)
        filler = chain(filler, branch(2, A["w_br_c"][0], lambda k: (bias_r[:, 8 + k, :], cq_r[:, k, :], t_c[k])))
        for _ in pipelined(tiles, latent_begin, latent_end):
            step(filler)
            step(mod_fill)
        run_all(filler)
        run_all(mod_fill)
        low_engine[0] = dve
        wuv = sq[:, 0, :].rearrange("p (a b) -> p a b", a=4)
        t_z = memset(pool, wuv, 0.0, *so_far())
        t_wuv = [small_dma(pool, wuv[:, h, (h % 2) * DH:(h % 2) * DH + DH], A["dsa_w_uv"][0, h], t_z) for h in range(4)]
        t_ob = [None] * 2
        for g in range(2):
            bi, b, free = lin.take()
            t = mm_group(b[:, :], [(wuv[:, 2 * g + j, :], bq[:, 2 * g + j, :]) for j in range(2)], *t_wuv, t_b[3], free)
            t_ob[g] = lin.free[bi] = split_of(b[:, :], bias_r[:, 4 + g, :], ob_r[:, g, :], t)
        run_all(branch(1, A["w_br_b"][0], lambda k: (bias_r[:, 4 + k, :], ob_r[:, k, :], t_ob[k])))

        gate = lambda i, m: modc[:, 24 * i + 16 + m:24 * i + 17 + m]
        t_hs = [None] * KC

        def to_residual(i):
            def evac(m, b, t):
                t_hs[m] = stt(hT[:, m, :], b, gate(i, m), hT[:, m, :], ALU.mult, ALU.add, t, t_mod[0])
                sums.add(hT[:, m, :], t_hs[m])
                return t_hs[m]
            sums = Sums(False)
            return evac, sums

        for k in range(KC):
            t_X[k] = split_of(merged[:, k, :], XH[:, k, :], XL[:, k, :], t_merged[k], pe.now)
        evac, sums = to_residual(0)
        run_all(linear([(A["w_o"][0], X)], D, evac, lead=True))
        att.bufs, att.free, att.n = banks[4:8], [so_far()] * 4, 0

        FC = FF // P
        ffn_h = area(0, FC, S)[0]
        ffn_low = area(0, FC, S, r=True)[0]
        EARLY = (ARENA - FC * S) // S
        early_high = area(FC * S, EARLY, S, r=True)[0]

        def mlp(w1, w2, evac2):
            t_f = [None] * FC

            def high(m):
                if m < EARLY:
                    return early_high[:, m, :]
                m -= EARLY
                return (XH if m < KC else XL)[:, m % KC, :]

            def evac1(m, b, t):
                t = fn(ffn_h[:, m, :], b, ACT.Relu, t)
                t2 = tt(pool if m % 2 else dve, ffn_h[:, m, :], ffn_h[:, m, :], ffn_h[:, m, :], ALU.mult, t)
                t_f[m] = split_of(ffn_h[:, m, :], high(m), ffn_low[:, m, :], t2) if m < EARLY else t2
                return t

            run_all(linear([(w1, X)], FF, evac1, lead=True))
            t_x_read = pe.now
            todo = list(range(EARLY, FC))

            def rest():
                for _ in range(2):
                    if todo:
                        m = todo.pop(0)
                        t_f[m] = split_of(ffn_h[:, m, :], high(m), ffn_low[:, m, :], t_f[m], t_x_read)

            rest()
            for _ in linear([(w2[i * D:(i + 1) * D, :],
                              lambda k, i=i: (high(i * KC + k), ffn_low[:, i * KC + k, :], t_f[i * KC + k]))
                             for i in range(4)], D, evac2):
                rest()

        w_even = A["even_w_in_2"][0]
        prm = lamb[:, P:P + 48].rearrange("p (a b) -> p a b", a=3)
        dsk = lamb[:, P + 48:P + 48 + KC]
        hb12 = lamb[:, P + 64:P + 64 + XBC_C]
        t_p = [small_dma(pool, prm[:, 0, :], A["even_dt_bias_2"].to_broadcast([P, 16])),
               small_dma(pool, prm[:, 1, :], A["even_a_log_2"].to_broadcast([P, 16])),
               small_dma(pool, prm[:, 2, :], A["even_d_skip_2"].to_broadcast([P, 16]))]
        t_wdt = small_dma(pool, wsmall[:, :, :], w_even[:, EV_DT:EV_DT + 16].rearrange("(k p) n -> p k n", p=P))

        modulated_norm(1, "norm_mlp", rms_of(sums, D, 0, stat[:, 0, :]))
        evac, sums = to_residual(1)
        mlp(A["w_ff1"][0], A["w_ff2"][0], evac)

        r = rms_of(sums, D, 0, stat[:, 0, :])
        for k in range(KC + 1):
            if k < KC:
                t_hs[k] = stt(hT[:, k, :], hT[:, k, :], column("norm_final", k), stat[:, 0, :], ALU.mult, ALU.mult, r)
                stat_free[:] = [t_hs[k]]
            if k:
                t_X[k - 1] = split_of(hT[:, k - 1, :], XH[:, k - 1, :], XL[:, k - 1, :], t_hs[k - 1])

        t_a = fn(prm[:, 1, :], prm[:, 1, :], ACT.Exp, *t_p)
        pd = prm[:, 2, :].rearrange("p (m two) -> p m two", two=2)
        t1 = copy(dve, dsk[0:DH, :], pd[0:DH, :, 0], *t_p)
        t_dsk = copy(dve, dsk[DH:P, :], pd[DH:P, :, 1], t1)
        t_hb = ts(dve, hb12, columns("even_ssm_conv_b_2", 0, XBC_C), 0.5, ALU.mult)

        h = lambda k: hT[:, k, :]

        def to_deepnorm():
            sums = Sums(True)

            def evac(m, b, t):
                t_hs[m] = stt(hT[:, m, :], hT[:, m, :], ALPHA, b, ALU.mult, ALU.add, t)
                sums.add(hT[:, m, :], t_hs[m])
                return t_hs[m]
            return evac, sums

        def block_norm(i, j, sums, last=False, fill=iter(())):
            c = (i * 3 + j) * 8
            g = lambda k: column("ln_g_2", c + k)
            bias_ = lambda k: column("ln_b_2", c + k)

            def finish(k, s, t):
                t_hs[k] = t
                if not last:
                    t_h = act.do(lambda e: e.activation(XH[:, k, :], s, ACT.Identity, bias=bias_(k), scale=1.0), t)
                    t_l = dve.do(lambda e: e.scalar_tensor_tensor(out=XL[:, k, :], in0=s, scalar=bias_(k),
                                                                  in1=XH[:, k, :].bitcast(F32), op0=ALU.add,
                                                                  op1=ALU.subtract), t, t_h)
                    t_X[k] = [t_h, t_l]

            for _ in layer_norm(h, sums, g, finish):
                step(fill)
            for k in range(KC):
                t_hs[k] = fn(h(k), h(k), ACT.Identity, t_hs[k], t_X[k], bias=bias_(k))

        def silu_of(o, b, scratch, t, *tokens, half_bias=None):
            hb = 0.0 if half_bias is None else half_bias
            t1 = fn(scratch, b, ACT.Tanh, t, *tokens, bias=hb, scale=0.5)
            t2 = ts(dve, o, b, 0.5, ALU.mult, t1, s2=hb, op1=ALU.add)
            return stt(o, scratch, 1.0, o, ALU.add, ALU.mult, t1, t2), t2

        pool.wait(*so_far())
        low_engine[0] = pool
        o = 0
        VALW = S + CONV_W - 1
        XW_ = S + SSM_CONV - 1
        val, o = area(o, KC, VALW)
        conv, o = area(o, KC, S)
        O_XBC = o
        xbc, o = area(o, XBC_C, S)
        O_RAW = o
        raw, o = area(o, 3, XW_)
        zT = area(0, KC, S)[0]
        XP, o = area(o, SSM_HEADS, P)
        XW, o = area(o, SSM_HEADS, DH)
        ST, o = area(o, SSM_HEADS, P)
        BM, o = area(o, 2, P)
        CB, o = area(o, 2, P)
        sets = [area(o, 3, 4, P)[0], area(O_RAW, 3, 4, P)[0]]
        o += 12 * P
        tmp4, o = area(o, 2, S)
        dts, o = area(o, 8, 64)
        DE, o = area(o, SSM_HEADS)
        dt_, adt, nacs, dte, sc1, sc2, sc3, sc4 = (dts[:, j, :] for j in range(8))
        y_high = area(0, KC, S, r=True)[0]
        y_low = area(O_XBC, KC, S, r=True)[0]

        t_pad = [memset(pool, val[:, :, 0:CONV_W - 1], 0.0), memset(pool, raw[:, :, 0:SSM_CONV - 1], 0.0),
                 memset(pool, XP, 0.0), memset(pool, ST, 0.0)]

        t_gate, t_val = [None] * KC, [None] * KC
        t_conv = [None] * KC
        conv_sums = Sums(True)

        def gate_and_value():
            for m0 in range(0, KC, 2):
                def evac_gate(m, b, t, m0=m0):
                    gi, g, gf = gate_ring.take()
                    tg = fn(g, b, ACT.Tanh, t, gf, scale=0.5)
                    t_gate[m0 + m] = gi, g, ts(pool, g, g, 0.5, ALU.mult, tg, s2=0.5, op1=ALU.add)
                    return tg

                def evac_value(m, b, t, m0=m0):
                    gi, g, tg = t_gate[m0 + m]
                    t = tt(dve, val[:, m0 + m, CONV_W - 1:], b, g, ALU.mult, t, tg, t_pad[0])
                    t_val[m0 + m] = gate_ring.free[gi] = t
                    return t

                c = m0 * P
                yield from linear([(w_even[:, EV_GATE + c:EV_GATE + c + 2 * P], X)], 2 * P, evac_gate, lead=m0 == 0)
                yield from linear([(w_even[:, EV_VAL + c:EV_VAL + c + 2 * P], X)], 2 * P, evac_value)

        def conv_taps():
            for m in range(KC):
                while t_val[m] is None:
                    yield
                o = conv[:, m, :]
                t = ts(dve, o, val[:, m, 0:S], conv_tap(0, m), ALU.mult, t_val[m], s2=column("even_conv_b_2", m), op1=ALU.add)
                for tap in range(1, CONV_W):
                    yield
                    t = stt(o, val[:, m, tap:tap + S], conv_tap(tap, m), o, ALU.mult, ALU.add, t)
                t_conv[m] = t
                conv_sums.add(conv[:, m, :], t)
                yield

        taps = conv_taps()
        gv_fill = gate_and_value()

        raw_ring = Ring([raw[:, j, :] for j in range(3)])
        sil = Ring([tmp4[:, j, :] for j in range(2)])
        t_xbc = [None] * XBC_C

        def evac_xbc(m, b, t):
            i, r, f = raw_ring.take()
            te = copy(act, r[:, SSM_CONV - 1:], b, t, f, t_pad[1])
            wcol = lambda j: column("even_ssm_conv_w_2", j * XBC_C + m)
            o = xbc[:, m, :]
            tc = ts(dve, o, r[:, 0:S], wcol(0), ALU.mult, te)
            for j in range(1, SSM_CONV):
                tc = stt(o, r[:, j:j + S], wcol(j), o, ALU.mult, ALU.add, tc)
            raw_ring.free[i] = tc
            si, s, sf = sil.take()
            t1 = fn(s, o, ACT.Tanh, tc, sf, t_hb, bias=hb12[:, m:m + 1], scale=0.5)
            t2 = ts(dve, o, o, 0.5, ALU.mult, t1, t_hb, s2=hb12[:, m:m + 1], op1=ALU.add)
            t_xbc[m] = sil.free[si] = stt(o, s, 1.0, o, ALU.add, ALU.mult, t1, t2)
            return te

        t_z = [None] * KC

        def evac_z(m, b, t):
            while t_conv[m] is None:
                step(taps)
            si, s, sf = sil.take()
            sil.free[si], t2 = silu_of(zT[:, m, :], b, s, t, sf, t_conv[m])
            t_z[m] = sil.free[si]
            return t2


        step(gv_fill)
        bi, b, free = lin.take()
        for c in range(NT):
            t = mm_group(b[:, c * 16:(c + 1) * 16],
                         [(h(k)[:, c * P:(c + 1) * P], wsmall[:, k, :]) for k in range(KC)], t_wdt, free, *t_hs)
        b4 = b[:, 0:64].rearrange("p (c h) -> p c h", c=NT)
        v4 = lambda a: a.rearrange("p (c h) -> p c h", c=NT)
        t = lin.free[bi] = tt(dve, v4(dt_), b4, prm[:, 0, :].unsqueeze(1).to_broadcast([P, NT, 16]), ALU.add, t, *t_p)

        def log1p_exp_minus(x, e, uu, ln, o, t):
            t1 = ts(dve, e, x, -1.0, ALU.mult, t)
            t1 = tt(dve, e, e, x, ALU.min, t1)
            t1 = fn(e, e, ACT.Exp, t1)
            t2 = ts(dve, uu, e, 1.0, ALU.add, t1)
            t3 = fn(ln, uu, ACT.Ln, t2)
            t1 = stt(e, uu, -1.0, e, ALU.add, ALU.subtract, t1, t2)
            t2 = recip(uu, uu, t2, t3, t1)
            t1 = tt(dve, e, e, uu, ALU.mult, t1, t2)
            return tt(dve, o, ln, e, ALU.subtract, t3, t1)

        t = log1p_exp_minus(dt_, sc1, sc2, sc3, sc4, t)
        t_dt = stt(dt_, dt_, 0.0, sc4, ALU.max, ALU.add, t)
        a_b = prm[:, 1, :].unsqueeze(1).to_broadcast([P, NT, 16])
        t = tt(dve, v4(adt), v4(dt_), a_b, ALU.mult, t_dt, t_a)
        t_adt = ts(dve, adt, adt, -1.0, ALU.mult, t)
        i, b, free = att.take()
        t = mm_group(b[:, 0:64], [(upper, adt)], t_adt, free)
        t = mm_group(b[:, 64:128], [(ones[:, :], adt)])
        t_n = ts(dve, nacs, b[:, 0:64], -1.0, ALU.mult, t)
        t = att.free[i] = tt(dve, dte, b[:, 64:128], nacs, ALU.add, t_n)
        t_dte = fn(dte, dte, ACT.Exp, t)

        for _ in gv_fill:
            step(taps, 8)
        run_all(linear([(w_even[:, EV_XBC:EV_XBC + XBC], X)], XBC, evac_xbc))

        pair = lambda a: a.rearrange("p (g two) d -> p g two d", two=2)
        t_y, t_st = None, None
        set_free = [[None] * 3 for _ in sets]
        started = {}

        def scan_begin(c, q4):
            cs = slice(c * P, (c + 1) * P)
            n, g = q4 % 2, q4 // 2
            E1, DEC, CE = (sets[n][:, j, :, :] for j in range(3))
            e1_free, dec_free, ce_free = set_free[n]
            i, b, free = att.take()
            for j in range(4):
                hd = c * 16 + q4 * 4 + j
                t = mm(b[:, j * P:(j + 1) * P], adt[:, hd:hd + 1].to_broadcast([P, P]), upper, True, True,
                       free, t_adt, signal=j == 3)
            bb = b[:, :].rearrange("p (a b) -> p a b", a=4)
            t_e = fn(E1, bb, ACT.Exp, t, e1_free)
            t_seg = att.free[i] = tt(dve, DEC, bb, seg_mask.unsqueeze(1).to_broadcast([P, 4, P]), ALU.add, t, dec_free, t_e)
            t_de = copy(dve, DE[:, q4 * 4:q4 * 4 + 4], E1[:, :, P - 1], t_e, t_st)
            for j in range(4):
                hd = c * 16 + q4 * 4 + j
                t = fn(DEC[:, j, :], DEC[:, j, :], ACT.Exp, t_seg, t_n, bias=nacs[:, hd:hd + 1])
            t_g = tt(dve, DEC, DEC, CB[:, g, :].unsqueeze(1).to_broadcast([P, 4, P]), ALU.mult, t, t_cb)
            t_ce = tt(pool, CE, E1, xbc[:, 10 + g, cs].unsqueeze(1).to_broadcast([P, 4, P]), ALU.mult, t_e, ce_free)
            started[q4] = t_g, t_ce, t_de

        def scan_end(c, q4):
            cs = slice(c * P, (c + 1) * P)
            n = q4 % 2
            E1, DEC, CE = (sets[n][:, j, :, :] for j in range(3))
            t_g, t_ce, t_de = started[q4]
            i, b, free = att.take()
            for pr_ in range(2):
                heads = [q4 * 4 + pr_ * 2 + par for par in range(2)]
                t = mm_group(b[:, pr_ * P:(pr_ + 1) * P],
                             [(XP[:, hh, :], DEC[:, hh % 4, :]) for hh in heads] +
                             [(ST[:, hh, :], CE[:, hh % 4, :]) for hh in heads],
                             free, t_g, t_ce, t_st, *t_xp, t_pad[3])
            set_free[n] = [[t_ce, t_de], t, t]
            for pr_ in range(2):
                m = q4 * 2 + pr_
                t_y = stt(xbc[:, m, cs], xbc[:, m, cs], dsk[:, m:m + 1], b[:, pr_ * P:(pr_ + 1) * P],
                          ALU.mult, ALU.add, t, t_dsk)
            att.free[i] = t_y
            return t_y

        z_fill = linear([(w_even[:, EV_Z:EV_Z + D], X)], D, evac_z)
        for c in range(NT):
            cs = slice(c * P, (c + 1) * P)
            dtc = dt_[:, c * 16:(c + 1) * 16].rearrange("p (g two) -> p g two", two=2)
            t_xp = []
            for half in range(2):
                i, b, free = att.take()
                for j in range(4):
                    t = turn(b[:, j * P:(j + 1) * P], xbc[:, half * 4 + j, cs], free, *t_xbc, signal=j == 3)
                bb = b[:, :].rearrange("p (g two d) -> p g two d", two=2, d=DH)
                for par in range(2):
                    t2 = tt(dve, pair(XP)[:, half * 4:half * 4 + 4, par, par * DH:(par + 1) * DH], bb[:, :, par, :],
                            dtc[:, half * 4:half * 4 + 4, par].unsqueeze(2).to_broadcast([P, 4, DH]), ALU.mult,
                            t, t_dt, t_pad[2], t_y)
                    t_xp.append(t2)
                att.free[i] = t2
            t_xw = None
            dtec = dte[:, c * 16:(c + 1) * 16].rearrange("p (g two) -> p g two", two=2)
            for par in range(2):
                t_xw = tt(pool, pair(XW)[:, :, par, :], pair(XP)[:, :, par, par * DH:(par + 1) * DH],
                          dtec[:, :, par].unsqueeze(2).to_broadcast([P, 8, DH]), ALU.mult, *t_xp, t_dte, t_st)
            i, b, free = att.take()
            for g in range(2):
                t = turn(b[:, g * P:(g + 1) * P], xbc[:, 8 + g, cs], free, signal=False)
            for g in range(2):
                t = mm(b[:, 256 + g * P:256 + (g + 1) * P], xbc[:, 8 + g, cs], xbc[:, 10 + g, cs], True, True,
                       signal=g == 1)
            t_bm = copy(act, BM, b[:, 0:256].rearrange("p (a b) -> p a b", a=2), t, t_st)
            t_cb = att.free[i] = copy(act, CB, b[:, 256:512].rearrange("p (a b) -> p a b", a=2), t, dve.now)
            for q4 in range(5):
                if q4 < 4:
                    scan_begin(c, q4)
                if q4:
                    t_y = scan_end(c, q4 - 1)
                if q4 == 1:
                    step(z_fill)
                step(taps, 7)
            t_de = started[3][2]
            for g in range(2):
                i, b, free = att.take()
                t = mm_group(b[:, :], [(BM[:, g, :], XW[:, g * 8:(g + 1) * 8, :].rearrange("p a b -> p (a b)"))],
                             t_bm, t_xw, free)
                bb = b[:, :].rearrange("p (g two d) -> p g two d", two=2, d=DH)
                de = DE.rearrange("p (g two) -> p g two", two=2)
                for par in range(2):
                    s_ = pair(ST)[:, g * 4:(g + 1) * 4, par, par * DH:(par + 1) * DH]
                    t2 = tt(dve, s_, s_, de[:, g * 4:(g + 1) * 4, par].unsqueeze(2).to_broadcast([P, 4, DH]),
                            ALU.mult, t_de, t, t_y)
                    t_st = tt(dve, s_, s_, bb[:, :, par, :], ALU.add, t2)
                att.free[i] = t_st
        run_all(taps)

        sil2 = Ring([XP[:, 4 * j:4 * j + 4, :].rearrange("p a b -> p (a b)") for j in range(2)])
        sil2.free = [[t_y, t_xw, t_st]] * 2
        t_u = [None] * KC

        def ln_silu(k, s, t):
            bcol = column("even_conv_ln_b_2", k)
            i, w, f = sil2.take()
            t = fn(s, s, ACT.Identity, t, bias=bcol)
            t1 = fn(w, s, ACT.Tanh, t, f, scale=0.5)
            t2 = stt(s, w, 1.0, s, ALU.add, ALU.mult, t1)
            sil2.free[i] = t2
            t_u[k] = t2

        for n, _ in enumerate(layer_norm(lambda k: conv[:, k, :], conv_sums, lambda k: column("even_conv_ln_g_2", k), ln_silu)):
            if n % 2 == 0:
                step(z_fill)
        run_all(z_fill)
        for k in range(KC):
            t_h = act.do(lambda e, k=k: e.activation(XH[:, k, :], conv[:, k, :], ACT.Copy, scale=0.5), t_u[k], pe.now)
            t_l = dve.do(lambda e, k=k: e.scalar_tensor_tensor(out=XL[:, k, :], in0=conv[:, k, :], scalar=0.5,
                                                               in1=XH[:, k, :].bitcast(F32), op0=ALU.mult,
                                                               op1=ALU.subtract), t_h, t_u[k])
            t_X[k] = [t_h, t_l]

        def gated_norm():
            for g in range(2):
                ms = range(g * 4, g * 4 + 4)
                ty = {m: tt(dve, xbc[:, m, :], xbc[:, m, :], zT[:, m, :], ALU.mult, t_y, t_z[m]) for m in ms}
                r = rms_stats(lambda k: xbc[:, k, :], ms, 4 * P, 1, stat[:, 2, :], ty)
                for m in ms:
                    t = stt(xbc[:, m, :], xbc[:, m, :], column("even_ssm_norm_g_2", m), stat[:, 2, :],
                            ALU.mult, ALU.mult, r)
                    t_y2[m] = split_of(xbc[:, m, :], y_high[:, m, :], y_low[:, m, :], t)
                    stat_free[:] = [t]
                yield
            low_engine[0] = dve

        t_y2 = [None] * KC
        w_out = A["even_w_out_2"][0]

        qT, o = area(0, KC, S)
        ws2, o = area(o, 4, MEM)
        PT2, o = area(o, 2, 2, S)
        assert o <= O_XBC
        kT, o = area(-(-(O_XBC + KC * S) // 16) * 16, KC, MEM)
        vv, o = area(o, 2, D)
        O_MEM = o
        mem_high, o = area(o, KC, MEM, r=True)
        mem_low, o = area(o, KC, MEM, r=True)
        mem, o = area(o, 2, D)

        out_high = area(0, KC, S, r=True)[0]
        out_low = area(O_MEM, KC, S, r=True)[0]

        def memory_kv(li):
            t_m = small_dma(pool, mem, A["mem_2"][0].rearrange("(t p) n -> p t n", p=P), *so_far())
            t_mt = [None] * KC

            def to_vv(m, b, t):
                return copy(act, vv[:, :, m * P:(m + 1) * P], b[:, 0:MEM].rearrange("p (t c) -> p t c", t=2), t)

            def steps():
                for k in range(0, KC, 2):
                    i, b, free = att.take()
                    for kk in range(2):
                        for t_ in range(2):
                            t = turn(b[:, kk * MEM + t_ * P:kk * MEM + (t_ + 1) * P],
                                     mem[:, t_, (k + kk) * P:(k + kk + 1) * P], t_m, free, signal=kk + t_ == 2)
                    att.free[i] = t_mt[k] = t_mt[k + 1] = split_of(
                        b[:, :].rearrange("p (a b) -> p a b", a=2), mem_high[:, k:k + 2, :], mem_low[:, k:k + 2, :], t)
                    yield
                M = lambda k: (mem_high[:, k, :], mem_low[:, k, :], t_mt[k])
                yield from linear([(A["xa_w_v_2"][li], M)], D, by_tokens(to_vv, MEM), MEM)
                yield from linear([(A["xa_w_k_2"][li], M)], D, to(kT), MEM)
            return steps()

        def mixer_out(parts, li, lead=False, early=iter(())):
            kv_fill = memory_kv(li)
            evac, sums = to_deepnorm()
            for n, _ in enumerate(linear(parts, D, evac, lead=lead)):
                if n in (0, 1, 3):
                    step(early)
                if n >= (4 if lead else 8):
                    step(kv_fill)
            block_norm(li, 0, sums, fill=kv_fill)
            return kv_fill

        def cross_attention(li, kv_fill):
            run_all(kv_fill)
            flush()
            t_q = [None] * KC
            t_o = [None] * KC

            def evac_qx(m, b, t):
                t_q[m] = copy(act, qT[:, m, :], b, t)
                return t_q[m]

            q_fill = linear([(A["xa_w_q_2"][li], X)], D, evac_qx)
            step(q_fill, 2)
            ring = Ring([ws2[:, j, :] for j in range(4)])
            ptr = Ring([PT2[:, j, :, :] for j in range(2)])
            tiles = [(hd, qt) for hd in range(XA_HEADS) for qt in range(NT)]
            state = {}

            def first_half(hd, qt):
                i, b, free = att.take()
                t = mm_group(b[:, 0:MEM], [(qT[:, 2 * hd + j, qt * P:(qt + 1) * P], kT[:, 2 * hd + j, :]) for j in range(2)],
                             t_q[2 * hd + 1], free)
                wi, w, wf = ring.take()
                si, st, sf = st_ring.take()
                t = dve.do(lambda e: e.tensor_reduce(st[:, 0:1], b[:, 0:MEM], AX.X, ALU.max, negate=True), t, sf)
                t = ts(dve, st[:, 1:2], st[:, 0:1], 256 ** -0.5, ALU.mult, t)
                t = att.free[i] = fn(w, b[:, 0:MEM], ACT.Exp, t, wf, bias=st[:, 1:2], scale=256 ** -0.5, accum=st[:, 2:3])
                t = recip(st[:, 3:4], st[:, 2:3], t)
                t = st_ring.free[si] = ts(dve, w, w, st[:, 3:4], ALU.mult, t)
                state[hd, qt] = (wi, w, t)

            def second_half(hd, qt):
                wi, w, tw = state.pop((hd, qt))
                if qt == 0:
                    state["pt"] = ptr.take()
                pi, pt, pf = state["pt"]
                i, b, free = att.take()
                for kt in range(2):
                    t = turn(b[:, kt * P:(kt + 1) * P], w[:, kt * P:(kt + 1) * P], tw, free, signal=kt == 1)
                ring.free[wi] = t
                t = att.free[i] = copy(act, pt[:, :, qt * P:(qt + 1) * P],
                                       b[:, 0:MEM].rearrange("p (a b) -> p a b", a=2), t, pf)
                if qt == NT - 1:
                    for e_ in range(2):
                        bi, b, free = lin.take()
                        m = 2 * hd + e_
                        t2 = mm_group(b[:, :], [(vv[:, kt, m * P:(m + 1) * P], pt[:, kt, :]) for kt in range(2)], t, free)
                        t_o[m] = lin.free[bi] = split_of(b[:, :], out_high[:, m, :], out_low[:, m, :], t2)
                    ptr.free[pi] = t2

            for n, _ in enumerate(pipelined(tiles, lambda t: first_half(*t), lambda t: second_half(*t))):
                if n % 2 == 0 or n >= 12:
                    step(q_fill)
            evac, sums = to_deepnorm()
            run_all(linear([(A["xa_w_o_2"][li], lambda k: (out_high[:, k, :], out_low[:, k, :], t_o[k]))], D, evac,
                           lead=True))
            return sums

        t_wl = small_dma(pool, wsmall[:, :, :],
                         A["odd_w_in_2"][0][:, OD_LOW:OD_LOW + GLA_RANK].rearrange("(k p) n -> p k n", p=P), t_dt)

        def block_mlp(li):
            evac, sums = to_deepnorm()
            mlp(A["mlp_w1_2"][li], A["mlp_w2_2"][li], evac)
            return sums

        kv_fill = mixer_out([(w_out[0:D, :], X),
                             (w_out[D:2 * D, :], lambda k: (y_high[:, k, :], y_low[:, k, :], t_y2[k]))], 0,
                            early=gated_norm())
        block_norm(0, 1, cross_attention(0, kv_fill))
        block_norm(0, 2, block_mlp(0))

        w_odd = A["odd_w_in_2"][0]
        o = 0
        q_, o = area(o, 4, S)
        k_, o = area(o, 4, S)
        gv, o = area(o, NT, D)
        go, o = area(o, KC, S)
        kend, o = area(o, 4, S)
        kt_ = k_
        lg, o = area(o, S)
        bcs, o = area(o, 4, S)
        sca, o = area(o, 3, S)
        SG, o = area(o, 2, GLA_HEADS, 256)
        low, o = area(o, S)
        wg2, o = area(o, 512)
        KE = bcs
        gT, o = area(o, KC, S)
        dec, o = area(o, 4, 8)
        ATT = kend
        ev = so_far()
        t_wg = small_dma(pool, wg2[0:GLA_RANK, :], A["odd_w_gate2_2"][0], *ev)
        t_qk = {}

        def evac_q(m, b, t):
            t_qk["q", m] = copy(act, q_[:, m, :], b, t)
            return t_qk["q", m]

        def evac_k(m, b, t):
            t_qk["k", m] = copy(act, k_[:, m, :], b, t)
            return t_qk["k", m]

        odd_fill = chain(linear([(w_odd[:, OD_Q:OD_Q + 512], X)], 512, evac_q, lead=True),
                         linear([(w_odd[:, OD_K:OD_K + 512], X)], 512, evac_k))
        step(odd_fill)
        bi, b, free = lin.take()
        t = mm_group(b[0:GLA_RANK, :], [(wsmall[:, k, :], h(k)) for k in range(KC)], t_wl, free, *t_hs)
        t_low = lin.free[bi] = copy(act, low[0:GLA_RANK, :], b[0:GLA_RANK, :], t)

        t_b4 = [None] * 4
        for hd in range(4):
            i, b, free = att.take()
            t = mm_group(b[:, :], [(wg2[0:GLA_RANK, hd * P:(hd + 1) * P], low[0:GLA_RANK, :])], t_wg, t_low, free)
            x_ = lg[:, :]
            t = att.free[i] = ts(dve, x_, b[:, :], column("odd_b_gate_2", hd), ALU.add, t, t_b4[hd - 1] if hd else None)
            t = log1p_exp_minus(x_, sca[:, 0, :], sca[:, 1, :], sca[:, 2, :], sca[:, 2, :], t)
            t = stt(x_, x_, 0.0, sca[:, 2, :], ALU.min, ALU.subtract, t)
            t = ts(dve, x_, x_, 1.0 / 16.0, ALU.mult, t)
            t_b4[hd] = dve.do(lambda e, hd=hd: e.tensor_tensor_scan(bcs[:, hd, :], again, lg[:, :], 0.0, ALU.mult, ALU.add), t)
            step(odd_fill, 2)
        run_all(odd_fill)
        t_dec = copy(dve, dec, bcs.rearrange("p h (n c) -> p h n c", c=GLA_C)[:, :, :, GLA_C - 1], *t_b4)
        t_qt = [None] * 4
        t_kt = [None] * 4
        t_ke = [None] * 4
        def to_gv(m, b, t):
            return copy(act, gv[:, :, m * P:(m + 1) * P], b[:, :].rearrange("p (t c) -> p t c", t=NT), t)

        vfill = linear([(w_odd[:, OD_V:OD_V + D], X)], D, by_tokens(to_gv))
        for hd in range(4):
            s0, s1, s2 = (sca[:, j, :] for j in range(3))
            bh = bcs[:, hd, :]
            t0 = fn(s0, bh, ACT.Exp, *t_b4, dve.now)
            t_qt[hd] = stt(q_[:, hd, :], q_[:, hd, :], P ** -0.5, s0, ALU.mult, ALU.mult, t0, t_qk["q", hd])
            t_e = fn(s1, bh, ACT.Exp, scale=-1.0)
            t0 = tt(dve, s2.rearrange("p (n c) -> p n c", c=GLA_C), dec[:, hd, :].unsqueeze(2).to_broadcast([P, 8, GLA_C]),
                    bh.rearrange("p (n c) -> p n c", c=GLA_C), ALU.subtract, t_dec, act.now)
            t0 = fn(s2, s2, ACT.Exp, t0)
            t_ke[hd] = tt(dve, kend[:, hd, :], k_[:, hd, :], s2, ALU.mult, t0, t_qk["k", hd])
            t_kt[hd] = tt(dve, kt_[:, hd, :], k_[:, hd, :], s1, ALU.mult, t_e, t_ke[hd])
            step(vfill, 2)
        t_dec = fn(dec, dec, ACT.Exp, t_dec, *t_ke)
        run_all(vfill)
        flush()
        t_v = act.now
        t_g = {}

        def evac_go(m, b, t):
            t_g[m], t2 = silu_of(go[:, m, :], b, sca[:, m % 2, :], t, dve.now)
            return t2

        gfill = linear([(w_odd[:, OD_G:OD_G + D], X)], D, evac_go)
        for tt_ in range(NT):
            i, b, free = att.take()
            for hd in range(4):
                t = turn(b[:, hd * P:(hd + 1) * P], kend[:, hd, tt_ * P:(tt_ + 1) * P], free, t_ke[hd], signal=hd == 3)
            t_KE = att.free[i] = copy(act, KE[:, tt_, :], b[:, :], t, dve.now)
        t_at = [None] * NT
        for tt_ in range(NT):
            ts_ = slice(tt_ * P, (tt_ + 1) * P)
            i, b, free = att.take()
            for hd in range(4):
                t = mm(b[:, hd * P:(hd + 1) * P], kt_[:, hd, ts_], q_[:, hd, ts_], True, True,
                       t_kt[hd], t_qt[hd], free, signal=hd == 3)
            a4 = ATT[:, tt_, :].rearrange("p (a b) -> p a b", a=4)
            t = att.free[i] = copy(act, ATT[:, tt_, :], b[:, :], t, t_KE)
            t = pool.do(lambda e, a4=a4: e.affine_select(out=a4, in_=a4, compare_op=ALU.is_ge, fill=0.0, base=0,
                                                         pattern=[[0, 4], [1, P]], channel_multiplier=-1), t)
            a5 = a4[:, :, GLA_C:P]
            t_at[tt_] = pool.do(lambda e, a5=a5: e.affine_select(out=a5, in_=a5, compare_op=ALU.is_ge, fill=0.0, base=-GLA_C,
                                                                 pattern=[[0, 4], [0, GLA_C]], channel_multiplier=1), t)
            step(gfill)
        t_s = memset(dve, SG[:, 0, :, :], 0.0)
        t_og = [None] * NT
        rd = None
        t_cur = [t_s] * 4
        for tt_ in range(NT):
            ts_ = slice(tt_ * P, (tt_ + 1) * P)
            outs = [att.take(), att.take()]
            for half in range(2):
                n = 2 * tt_ + half
                hs = slice(half * GLA_C, (half + 1) * GLA_C)
                for e_ in range(8):
                    hd, vh = e_ // 2, e_ % 2
                    i, b, free = outs[e_ // 4]
                    dst = b[:, (e_ % 4) * P + half * GLA_C:(e_ % 4) * P + (half + 1) * GLA_C]
                    t = mm_group(dst, [
                        (gv[:, tt_, hd * 256 + vh * P:hd * 256 + (vh + 1) * P], ATT[:, tt_, hd * P + half * GLA_C:hd * P + (half + 1) * GLA_C]),
                        (SG[:, n % 2, hd, vh * P:(vh + 1) * P], q_[:, hd, tt_ * P + half * GLA_C:tt_ * P + (half + 1) * GLA_C]),
                    ], t_v, t_at[tt_], free, t_cur[hd])
                rd = t
                if n < 7:
                    for pr_ in range(2):
                        bi, b, free = lin.take()
                        for j in range(2):
                            hd = pr_ * 2 + j
                            t = mm(b[:, j * 256:(j + 1) * 256], KE[hs, tt_, hd * P:(hd + 1) * P],
                                   gv[hs, tt_, hd * 256:(hd + 1) * 256], True, True, free, t_KE, signal=j == 1)
                        for j in range(2):
                            hd = pr_ * 2 + j
                            t_cur[hd] = stt(SG[:, (n + 1) % 2, hd, :], SG[:, n % 2, hd, :], dec[:, hd, n:n + 1],
                                            b[:, j * 256:(j + 1) * 256], ALU.mult, ALU.add, t, t_dec, rd, t_cur[hd])
                        lin.free[bi] = t_cur[hd]
                step(gfill)
            for z in range(2):
                i, b, free = outs[z]
                t_og[tt_] = att.free[i] = copy(dve, gT[:, 4 * z:4 * z + 4, ts_], b[:, :].rearrange("p (a b) -> p a b", a=4), rd)
        run_all(gfill)
        t_r = []
        for hd in range(GLA_HEADS):
            squares = [q_[:, hd, :], k_[:, hd, :]]
            tq = [fn(squares[j], gT[:, 2 * hd + j, :], ACT.Square, t_og[-1], rd) for j in range(2)]
            i, b, free = att.take()
            t = mm_group(b[:, :], [(ones[:, :], squares[j]) for j in range(2)], *tq, free)
            t_r.append((i, b, t))
        for hd, (i, b, t) in enumerate(t_r):
            att.free[i] = fn(KE[:, hd, :], b[:, :], ACT.Ln, t, rd, bias=eps_t[:, 1:2], scale=1.0 / 256)
        t_r = [fn(KE[:, hd, :], KE[:, hd, :], ACT.Exp, att.free[i], scale=-0.5) for hd, (i, b, t) in enumerate(t_r)]

        def scaled_head(m):
            t = stt(gT[:, m, :], gT[:, m, :], column("odd_head_norm_g_2", m % 2), KE[:, m // 2, :],
                    ALU.mult, ALU.mult, t_r[m // 2])
            return tt(pool, gT[:, m, :], gT[:, m, :], go[:, m, :], ALU.mult, t, t_g[m])

        ts_g = [scaled_head(m) for m in range(2)]
        for m in range(KC):
            if m + 2 < KC:
                ts_g.append(scaled_head(m + 2))
            t_X[m] = split_of(gT[:, m, :], XH[:, m, :], XL[:, m, :], ts_g[m])
        kv_fill = mixer_out([(A["odd_w_out_2"][0], X)], 1, lead=True)
        block_norm(1, 1, cross_attention(1, kv_fill))
        block_norm(1, 2, block_mlp(1), last=True)

        ot, _ = area(0, NT, D)
        outs = []
        for t_ in range(NT):
            for half in range(2):
                i, b, free = att.take()
                for j in range(4):
                    t = turn(b[:, j * P:(j + 1) * P], hT[:, half * 4 + j, t_ * P:(t_ + 1) * P], *t_hs, free, signal=j == 3)
                t_o = att.free[i] = copy(act if half else dve, ot[:, t_, half * 512:(half + 1) * 512], b[:, :], t)
                outs.append(small_dma(sp, out[0, t_ * P:(t_ + 1) * P, half * 512:(half + 1) * 512],
                                      ot[:, t_, half * 512:(half + 1) * 512], t_o))
        sp.wait(*outs, t_sd)

        if schedule is None:
            return noted

        with nc.Block() as block:
            @block.sync
            def _(e):
                sp.run(e)

            @block.scalar
            def _(e):
                act.run(e)

            @block.vector
            def _(e):
                dve.run(e)

            @block.gpsimd
            def _(e):
                pool.run(e)

            @block.tensor
            def _(e):
                pe.run(e)


_INS = ['x', 'c', 'rel_bias', 'ada_w', 'ada_b', 'norm_mix', 'w_in', 'gate_b', 'diff_lambda', 'diff_subln',
        'dsa_kv_norm', 'dsa_w_uv', 'w_br_a', 'w_br_b', 'w_br_c', 'w_o', 'norm_mlp', 'w_ff1', 'w_ff2', 'norm_final',
        'mem_2', 'even_w_in_2', 'even_conv_w_2', 'even_conv_b_2', 'even_conv_ln_g_2', 'even_conv_ln_b_2',
        'even_ssm_conv_w_2', 'even_ssm_conv_b_2', 'even_dt_bias_2', 'even_a_log_2', 'even_d_skip_2',
        'even_ssm_norm_g_2', 'even_w_out_2', 'odd_w_in_2', 'odd_w_gate2_2', 'odd_b_gate_2', 'odd_head_norm_g_2',
        'odd_w_out_2', 'xa_w_q_2', 'xa_w_k_2', 'xa_w_v_2', 'xa_w_o_2', 'mlp_w1_2', 'mlp_w2_2', 'ln_g_2', 'ln_b_2']


def kernel(**inputs):
    import concourse.bacc as bacc
    from concourse.bass_utils import run_bass_kernel_spmd

    square, onehot = shape_constants()
    arrays = {f"in_{name}": np.ascontiguousarray(inputs[name]) for name in _INS}
    arrays["in_c_square"], arrays["in_c_onehot"] = square, onehot

    def described(schedule):
        nc = bacc.Bacc("TRN2", target_bir_lowering=False, num_devices=1)
        A = {key[3:]: nc.dram_tensor(key, a.shape, mybir.dt.from_np(a.dtype), kind="ExternalInput").ap()
             for key, a in arrays.items()}
        A["strip"] = nc.dram_tensor("strip", (12, 640), F32, kind="Internal").ap()
        out = nc.dram_tensor("out", (1, S, D), F32, kind="ExternalOutput").ap()
        return nc, program(nc, A, out, schedule)

    nc, _ = described(described(None)[1])
    r = run_bass_kernel_spmd(nc, [arrays], core_ids=[0])
    return r.results[0]["out"]
```
